# Optimizing a Trainium2 kernel written in Bass

```python
import math
import jax, jax.numpy as jnp
from jax import lax
import numpy as np

D_MODEL = 1024
BATCH = 1
SEQ = 256
DEPTH = 2

GRID_W = 64
CTX_LEN = 256
EPS = 1e-6
N_MOD = 6

HEAD_DIM = 64
N_Q_HEADS = 8
N_KV_HEADS = 2
Q_PER_KV = N_Q_HEADS // N_KV_HEADS
WINDOW = 128
ATTN_BLOCK = 128
BAND = 3 * ATTN_BLOCK
ROPE_BASE = 10000.0

FNET_GROUPS = 4
FNET_GROUP_DIM = 128
FNET_WIDTH = FNET_GROUPS * FNET_GROUP_DIM

HYENA_WIDTH = 512
HYENA_ORDER = 2
SHORT_CONV = 3
FILTER_EMB = 33
FILTER_BANDS = (FILTER_EMB - 1) // 2
FILTER_HIDDEN = 64
DECAY_TARGET = 1e-2
FAST_DECAY_PCT = 0.3
SLOW_DECAY_PCT = 1.5

ATTN_WIDTH = N_Q_HEADS * HEAD_DIM
KV_WIDTH = N_KV_HEADS * HEAD_DIM
N_BRANCHES = 3
Q_OFF = 0
K_OFF = Q_OFF + ATTN_WIDTH
V_OFF = K_OFF + KV_WIDTH
F_OFF = V_OFF + KV_WIDTH
H_OFF = F_OFF + FNET_WIDTH
G_OFF = H_OFF + (HYENA_ORDER + 1) * HYENA_WIDTH
IN_WIDTH = G_OFF + N_BRANCHES * D_MODEL

N_EXPERTS = 16
N_GROUPS = 4
EXPERTS_PER_GROUP = N_EXPERTS // N_GROUPS
TOP_K = 2
EXPERT_FF = 1024
EXPERT_BLOCK = 128

kernel_name = 'hybrid_gated_attn_fnet_hyena_moe_dit'

def rms_norm(x, g):
    xf = x.astype(jnp.float32)
    y = xf * lax.rsqrt(jnp.mean(xf * xf, axis=-1, keepdims=True) + EPS)
    return (y * g.astype(jnp.float32)).astype(x.dtype)

def modulate(h, shift, scale):
    return h * (1 + scale) + shift

def axial_rope(x, rows, cols):
    n_freq = HEAD_DIM // 4
    freqs = ROPE_BASE ** (-jnp.arange(n_freq, dtype=jnp.float32) / n_freq)

    def rotate(xa, pos):
        ang = pos.astype(jnp.float32)[:, None] * freqs
        cos = jnp.cos(ang)[None, :, None, :]
        sin = jnp.sin(ang)[None, :, None, :]
        x1, x2 = xa[..., :n_freq], xa[..., n_freq:]
        return jnp.concatenate([x1 * cos - x2 * sin, x1 * sin + x2 * cos], axis=-1)

    half = HEAD_DIM // 2
    out = jnp.concatenate([rotate(x[..., :half], rows), rotate(x[..., half:], cols)], axis=-1)
    return out.astype(x.dtype)

def banded_attention(q, k, v, kc, vc, sink):
    bsz, n = q.shape[:2]
    nb = n // ATTN_BLOCK
    scale = HEAD_DIM ** -0.5
    qb = q.reshape(bsz, nb, ATTN_BLOCK, N_KV_HEADS, Q_PER_KV, HEAD_DIM)
    pad = ((0, 0), (ATTN_BLOCK, ATTN_BLOCK), (0, 0), (0, 0))

    def band(t):
        tb = jnp.pad(t, pad).reshape(bsz, nb + 2, ATTN_BLOCK, N_KV_HEADS, HEAD_DIM)
        return jnp.concatenate([tb[:, :-2], tb[:, 1:-1], tb[:, 2:]], axis=2)

    kb, vb = band(k), band(v)
    s_band = jnp.einsum('bnqhgd,bnkhd->bnhgqk', qb, kb).astype(jnp.float32) * scale
    qpos = jnp.arange(n, dtype=jnp.int32).reshape(nb, ATTN_BLOCK)
    kpos = (jnp.arange(nb, dtype=jnp.int32)[:, None] - 1) * ATTN_BLOCK + jnp.arange(BAND, dtype=jnp.int32)[None, :]
    kp = kpos[:, None, :]
    valid = (kp >= 0) & (kp < n) & (jnp.abs(kp - qpos[:, :, None]) <= WINDOW)
    s_band = jnp.where(valid[None, :, None, None], s_band, jnp.finfo(jnp.float32).min)
    s_ctx = jnp.einsum('bnqhgd,bchd->bnhgqc', qb, kc).astype(jnp.float32) * scale
    s_sink = jnp.broadcast_to(sink.astype(jnp.float32).reshape(1, 1, N_KV_HEADS, Q_PER_KV, 1, 1),
                              s_band.shape[:-1] + (1,))
    p = jax.nn.softmax(jnp.concatenate([s_band, s_ctx, s_sink], axis=-1), axis=-1)
    n_ctx = kc.shape[1]
    p_band = p[..., :BAND].astype(v.dtype)
    p_ctx = p[..., BAND:BAND + n_ctx].astype(v.dtype)
    o = jnp.einsum('bnhgqk,bnkhd->bnqhgd', p_band, vb) + jnp.einsum('bnhgqc,bchd->bnqhgd', p_ctx, vc)
    return o.reshape(bsz, n, ATTN_WIDTH)

def context_attention(q, kc, vc, sink):
    bsz, n = q.shape[:2]
    scale = HEAD_DIM ** -0.5
    qg = q.reshape(bsz, n, N_KV_HEADS, Q_PER_KV, HEAD_DIM)
    s = jnp.einsum('bqhgd,bkhd->bhgqk', qg, kc).astype(jnp.float32) * scale
    s_sink = jnp.broadcast_to(sink.astype(jnp.float32).reshape(1, N_KV_HEADS, Q_PER_KV, 1, 1), s.shape[:-1] + (1,))
    p = jax.nn.softmax(jnp.concatenate([s, s_sink], axis=-1), axis=-1)[..., :-1]
    o = jnp.einsum('bhgqk,bkhd->bqhgd', p.astype(vc.dtype), vc)
    return o.reshape(bsz, n, ATTN_WIDTH)

def fourier_mix(u):
    bsz, n, _ = u.shape
    ug = u.astype(jnp.float32).reshape(bsz, n, FNET_GROUPS, FNET_GROUP_DIM)
    y = jnp.fft.fft2(ug, axes=(1, 3), norm='ortho').real
    return y.reshape(bsz, n, FNET_WIDTH).astype(u.dtype)

def short_conv(u, w, b):
    up = jnp.pad(u, ((0, 0), (1, 1), (0, 0)))
    return up[:, :-2] * w[0] + up[:, 1:-1] * w[1] + up[:, 2:] * w[2] + b

def hyena_filters(n, w1, b1, freq, w2, b2, w3):
    pos = jnp.arange(n, dtype=jnp.float32)
    t = pos / max(n - 1, 1)
    omega = 2.0 * math.pi * pos / n
    bands = jnp.linspace(1e-4, FILTER_BANDS - 1, FILTER_BANDS, dtype=jnp.float32)
    feats = jnp.concatenate([t[:, None], jnp.cos(omega[:, None] * bands), -jnp.sin(omega[:, None] * bands)], axis=-1)
    h = jnp.sin(freq * (feats @ w1 + b1))
    h = jnp.sin(freq * (h @ w2 + b2))
    h = (h @ w3).reshape(n, HYENA_ORDER, 2, HYENA_WIDTH)
    deltas = jnp.abs(jnp.linspace(math.log(DECAY_TARGET) / SLOW_DECAY_PCT, math.log(DECAY_TARGET) / FAST_DECAY_PCT,
                                  HYENA_WIDTH, dtype=jnp.float32))
    h = h * jnp.exp(-t[:, None] * deltas)[:, None, None, :]
    fwd, bwd = h[:, :, 0], h[:, :, 1]
    k = jnp.concatenate([fwd, jnp.zeros_like(fwd[:1]), bwd[:0:-1]], axis=0)
    return k / jnp.sum(jnp.abs(k), axis=0, keepdims=True)

def fft_long_conv(u, k):
    n = u.shape[1]
    uf = jnp.fft.rfft(u, n=2 * n, axis=1)
    kf = jnp.fft.rfft(k, n=2 * n, axis=0)
    return jnp.fft.irfft(uf * kf[None], n=2 * n, axis=1)[:, :n]

def hyena_mix(u, conv_w, conv_b, filt, hyena_bias):
    n = u.shape[1]
    z = short_conv(u, conv_w, conv_b).astype(jnp.float32)
    v, x1, x2 = jnp.split(z, HYENA_ORDER + 1, axis=-1)
    k = hyena_filters(n, *filt)
    bias = hyena_bias.astype(jnp.float32)
    y = v
    for o, gate in enumerate((x1, x2)):
        y = gate * (fft_long_conv(y, k[:, o]) + y * bias[o])
    return y.astype(u.dtype)

def mix_tokens(p, kc, vc, pos, sink, conv_w, conv_b, filt, hyena_bias, w_ba, w_bf, w_bh, w_out):
    bsz, n, _ = p.shape
    q = p[..., Q_OFF:K_OFF].reshape(bsz, n, N_Q_HEADS, HEAD_DIM)
    if pos is None:
        ya = context_attention(q, kc, vc, sink)
    else:
        rows, cols = pos
        k = p[..., K_OFF:V_OFF].reshape(bsz, n, N_KV_HEADS, HEAD_DIM)
        v = p[..., V_OFF:F_OFF].reshape(bsz, n, N_KV_HEADS, HEAD_DIM)
        ya = banded_attention(axial_rope(q, rows, cols), axial_rope(k, rows, cols), v, kc, vc, sink)
    yf = fourier_mix(p[..., F_OFF:H_OFF])
    yh = hyena_mix(p[..., H_OFF:G_OFF], conv_w, conv_b, filt, hyena_bias)
    ga, gf, gh = jnp.split(jax.nn.sigmoid(p[..., G_OFF:]), N_BRANCHES, axis=-1)
    merged = ga * (ya @ w_ba) + gf * (yf @ w_bf) + gh * (yh @ w_bh)
    return merged @ w_out

def moe_ffn(h, w_router, b_router, w_gate, w_up, w_down):
    shape = h.shape
    tok = h.reshape(-1, D_MODEL)
    n_tok = tok.shape[0]
    aff = jax.nn.sigmoid((tok @ w_router).astype(jnp.float32))
    biased = (aff + b_router.astype(jnp.float32)).reshape(n_tok, N_GROUPS, EXPERTS_PER_GROUP)
    group_score = lax.top_k(biased, TOP_K)[0].sum(axis=-1)
    g_sel = jnp.argmax(group_score, axis=-1).astype(jnp.int32)
    in_group = jnp.take_along_axis(biased, g_sel[:, None, None], axis=1)[:, 0]
    e_idx = g_sel[:, None] * EXPERTS_PER_GROUP + lax.top_k(in_group, TOP_K)[1]
    w_sel = jnp.take_along_axis(aff, e_idx, axis=1)
    w_sel = w_sel / jnp.sum(w_sel, axis=-1, keepdims=True)
    n_asg = n_tok * TOP_K
    flat_e = e_idx.reshape(-1)
    flat_tok = jnp.repeat(jnp.arange(n_tok, dtype=jnp.int32), TOP_K)
    order = jnp.argsort(flat_e)
    se = flat_e[order]
    counts = jnp.bincount(flat_e, length=N_EXPERTS)
    padded = (counts + EXPERT_BLOCK - 1) // EXPERT_BLOCK * EXPERT_BLOCK
    pad_end = jnp.cumsum(padded)
    pad_start = pad_end - padded
    start = jnp.cumsum(counts) - counts
    dest = pad_start[se] + jnp.arange(n_asg, dtype=jnp.int32) - start[se]
    n_rows = -(-n_asg // EXPERT_BLOCK) * EXPERT_BLOCK + N_EXPERTS * EXPERT_BLOCK
    n_blk = n_rows // EXPERT_BLOCK
    row_tok = jnp.full((n_rows,), n_tok, jnp.int32).at[dest].set(flat_tok[order])
    row_w = jnp.zeros((n_rows,), jnp.float32).at[dest].set(w_sel.reshape(-1)[order])
    blk_expert = jnp.minimum(
        jnp.searchsorted(pad_end, jnp.arange(n_blk, dtype=pad_end.dtype) * EXPERT_BLOCK, side='right'),
        N_EXPERTS - 1)
    tok_pad = jnp.concatenate([tok, jnp.zeros((1, D_MODEL), tok.dtype)], axis=0)
    xs = tok_pad[row_tok].reshape(n_blk, EXPERT_BLOCK, D_MODEL)

    def expert_block(args):
        xb, e = args
        hb = jax.nn.silu(xb @ w_gate[e]) * (xb @ w_up[e])
        return hb @ w_down[e]

    ys = lax.map(expert_block, (xs, blk_expert)).reshape(n_rows, D_MODEL)
    out = jnp.zeros((n_tok + 1, D_MODEL), ys.dtype).at[row_tok].add(ys * row_w[:, None].astype(ys.dtype))
    return out[:n_tok].reshape(shape)

def setup_inputs(seed: int = 0) -> dict:
    key = jax.random.key(seed)
    ks = jax.random.split(key, 32)
    D = D_MODEL
    L = DEPTH

    def nrm(k, shape, scale):
        return scale * jax.random.normal(k, shape, jnp.float32)

    return {
        'x': nrm(ks[0], (BATCH, SEQ, D), 1.0),
        'c': nrm(ks[1], (BATCH, D), 1.0),
        'ctx': nrm(ks[2], (BATCH, CTX_LEN, D), 1.0),
        'c_ctx': nrm(ks[3], (D,), 1.0),
        'w_mod': nrm(ks[4], (L, D, N_MOD * D), 0.5 * D ** -0.5),
        'b_mod': nrm(ks[5], (L, N_MOD * D), 0.02),
        'norm_mix': 1.0 + nrm(ks[6], (L, D), 0.02),
        'norm_ffn': 1.0 + nrm(ks[7], (L, D), 0.02),
        'w_in': nrm(ks[8], (L, D, IN_WIDTH), D ** -0.5),
        'attn_sink': nrm(ks[9], (L, N_Q_HEADS), 0.5),
        'conv_w': nrm(ks[10], (L, SHORT_CONV, (HYENA_ORDER + 1) * HYENA_WIDTH), SHORT_CONV ** -0.5),
        'conv_b': nrm(ks[11], (L, (HYENA_ORDER + 1) * HYENA_WIDTH), 0.02),
        'filt_w1': nrm(ks[12], (L, FILTER_EMB, FILTER_HIDDEN), FILTER_EMB ** -0.5),
        'filt_b1': nrm(ks[13], (L, FILTER_HIDDEN), 0.02),
        'filt_freq': 1.0 + nrm(ks[14], (L, FILTER_HIDDEN), 0.02),
        'filt_w2': nrm(ks[15], (L, FILTER_HIDDEN, FILTER_HIDDEN), FILTER_HIDDEN ** -0.5),
        'filt_b2': nrm(ks[16], (L, FILTER_HIDDEN), 0.02),
        'filt_w3': nrm(ks[17], (L, FILTER_HIDDEN, HYENA_ORDER * 2 * HYENA_WIDTH), FILTER_HIDDEN ** -0.5),
        'hyena_bias': nrm(ks[18], (L, HYENA_ORDER, HYENA_WIDTH), 0.5),
        'w_branch_attn': nrm(ks[19], (L, ATTN_WIDTH, D), ATTN_WIDTH ** -0.5),
        'w_branch_fnet': nrm(ks[20], (L, FNET_WIDTH, D), FNET_WIDTH ** -0.5),
        'w_branch_hyena': nrm(ks[21], (L, HYENA_WIDTH, D), HYENA_WIDTH ** -0.5),
        'w_out': nrm(ks[22], (L, D, D), D ** -0.5),
        'w_router': nrm(ks[23], (D, N_EXPERTS), D ** -0.5),
        'b_router': nrm(ks[24], (N_EXPERTS,), 0.01),
        'w_exp_gate': nrm(ks[25], (L, N_EXPERTS, D, EXPERT_FF), D ** -0.5),
        'w_exp_up': nrm(ks[26], (L, N_EXPERTS, D, EXPERT_FF), D ** -0.5),
        'w_exp_down': nrm(ks[27], (L, N_EXPERTS, EXPERT_FF, D), EXPERT_FF ** -0.5),
        'norm_final': 1.0 + nrm(ks[28], (D,), 0.02),
    }

def reference(x, c, ctx, c_ctx, w_mod, b_mod, norm_mix, norm_ffn, w_in, attn_sink, conv_w, conv_b,
              filt_w1, filt_b1, filt_freq, filt_w2, filt_b2, filt_w3, hyena_bias,
              w_branch_attn, w_branch_fnet, w_branch_hyena, w_out,
              w_router, b_router, w_exp_gate, w_exp_up, w_exp_down, norm_final):
    bsz, n_lat, _ = x.shape
    n_ctx = ctx.shape[1]
    ROWS = n_lat // GRID_W
    rows = jnp.repeat(jnp.arange(ROWS, dtype=jnp.int32), GRID_W)
    cols = jnp.tile(jnp.arange(GRID_W, dtype=jnp.int32), ROWS)
    xl, xc = x, ctx
    silu_c = jax.nn.silu(c)
    silu_cc = jax.nn.silu(c_ctx)
    for l in range(DEPTH):
        last = l == DEPTH - 1
        mod_l = jnp.split(silu_c @ w_mod[l] + b_mod[l], N_MOD, axis=-1)
        mod_c = jnp.split(silu_cc @ w_mod[l] + b_mod[l], N_MOD, axis=-1)
        sh1, sc1, g1, sh2, sc2, g2 = [m[:, None, :] for m in mod_l]
        csh1, csc1, cg1, csh2, csc2, cg2 = mod_c
        filt = (filt_w1[l], filt_b1[l], filt_freq[l], filt_w2[l], filt_b2[l], filt_w3[l])
        mixer_weights = (attn_sink[l], conv_w[l], conv_b[l], filt, hyena_bias[l],
                         w_branch_attn[l], w_branch_fnet[l], w_branch_hyena[l], w_out[l])
        hl = modulate(rms_norm(xl, norm_mix[l]), sh1, sc1)
        hc = modulate(rms_norm(xc, norm_mix[l]), csh1, csc1)
        if last:
            kv_c = hc @ w_in[l][:, K_OFF:F_OFF]
        else:
            pc = hc @ w_in[l]
            kv_c = pc[..., K_OFF:F_OFF]
        kc = kv_c[..., :KV_WIDTH].reshape(bsz, n_ctx, N_KV_HEADS, HEAD_DIM)
        vc = kv_c[..., KV_WIDTH:].reshape(bsz, n_ctx, N_KV_HEADS, HEAD_DIM)
        pl = hl @ w_in[l]
        xl = xl + g1 * mix_tokens(pl, kc, vc, (rows, cols), *mixer_weights)
        if not last:
            xc = xc + cg1 * mix_tokens(pc, kc, vc, None, *mixer_weights)
        experts = (w_exp_gate[l], w_exp_up[l], w_exp_down[l])
        h2l = modulate(rms_norm(xl, norm_ffn[l]), sh2, sc2)
        xl = xl + g2 * moe_ffn(h2l, w_router, b_router, *experts)
        if not last:
            h2c = modulate(rms_norm(xc, norm_ffn[l]), csh2, csc2)
            xc = xc + cg2 * moe_ffn(h2c, w_router, b_router, *experts)
    return rms_norm(xl, norm_final)


_drawn_inputs = setup_inputs


def setup_inputs(seed=0):
    import zlib

    import numpy as np

    out = dict(_drawn_inputs(seed))
    spreads = {}
    factors = {'norm_mix': 2.902,
     'attn_sink': 64.0,
     'conv_b': 8.0,
     'filt_b1': 8.0,
     'filt_freq': 8.0,
     'filt_b2': 5.009,
     'norm_final': 7.356}
    for name, (base, spread) in spreads.items():
        noise = np.random.default_rng([zlib.crc32(name.encode()), seed]).standard_normal(out[name].shape)
        drawn = base * np.exp(spread * noise) if base else spread * noise
        out[name] = __import__('jax').numpy.asarray(drawn.astype(out[name].dtype))
    for name, factor in factors.items():
        out[name] = (out[name] * factor).astype(out[name].dtype)
    return out
```

```python
from contextlib import ExitStack

import concourse.bass as bass
from concourse import mybir

F32 = mybir.dt.float32
I32 = mybir.dt.int32
ALU = mybir.AluOpType
ACT = mybir.ActivationFunctionType
AX = mybir.AxisListType

P = 128
D = 1024
KB = D // P
SEQ = 256
DEPTH = 2
HD = 64
NH = 8
NKV = 2
NE = 16
EPS = 1e-6
HY = 512
CH = 512
SLOT = KB * CH
W_OFF = {"q": 0, "kv": 512, "f": 768, "v": 1280, "x1": 1792, "x2": 2304, "ga": 2816, "gf": 3840, "gh": 4864}
ROWS_PER_PART = 64
OVER_BLOCKS = [3, 1]
MAGIC = 12582912.0
TWO_PI = (6.28125, 0.0019350051879882812, 3.019915981956753e-07)
INV_2PI = 0.15915494309189535
PI = 3.1415925

C_ID, C_TRI, C_ONE = 0, 128, 256
C_DFT = 384
C_INV = C_DFT + 2 * 6 * P
C_ROPE = C_INV + 4 * SEQ
C_MASK = C_ROPE + 2 * 4 * HD
C_EXP = C_MASK + 2 * 512
C_END = C_EXP + 64
FR0, FR1, FI0, FI1, FIZ, FRN = range(6)


def tokens_of(l):
    return [0, 1, 2, 3] if l < DEPTH - 1 else [0, 1]


def plan_jobs(l):
    T = tokens_of(l)
    S = list(range(len(T) // 2))
    out = []

    def job(who, *name):
        out.append((name, who))

    for tb in range(4):
        for half in range(2):
            job("act", "hT", l, 0, tb, half)
    for tb in range(4):
        job("dve", "in", l, "kv", tb)
    for tb in T:
        job("dve", "in", l, "q", tb)
    for tb in range(4):
        job("act", "kT", l, tb)
    for tb in T:
        job("act", "in", l, "f", tb)
    for tb in T:
        job("act", "qT", l, tb)
    for c in ("v", "x1", "x2"):
        for tb in T:
            job("act", "in", l, c, tb)
    job("dve", "fl", l, 1)
    job("dve", "fl", l, 2)
    for o in range(2):
        for d in range(2):
            for tt in range(2):
                job("dve", "f3", l, o, d, tt)
        job("dve", "fn", l, o)
        for b in range(5):
            job("dve", "fk", l, o, b)
    for s in S:
        for g in range(5):
            if g < 4:
                job("act", "fp", l, s, g)
            if g > 0:
                job("act", "fy", l, s, g - 1)
    heads = [(tb, h) for tb in T for h in range(NH)]
    for i in range(len(heads) + 3):
        if i < len(heads):
            job("dve", "sc", l, *heads[i])
        if 2 <= i < len(heads) + 2:
            job("act", "pt", l, *heads[i - 2])
        if i >= 3:
            job("dve", "pv", l, *heads[i - 3])
            if heads[i - 3][1] == NH - 1 and heads[i - 3][0] > 0:
                job("act", "yaT", l, heads[i - 3][0] - 1)
    job("act", "yaT", l, T[-1])
    for o in range(2):
        for s in S:
            for b in (FR0, FI0, FR1, FI1):
                job("dve", "u", l, o, s, b)
            for tt in range(2):
                job("dve", "c", l, o, s, tt)
    for tb in T:
        job("act", "yhT", l, tb)
    for br in range(3):
        for n in range(2):
            for tb in T:
                job("act", "g", l, br, n, tb)
                job("dve", "b", l, br, n, tb)
    for tb in T:
        for half in range(2):
            job("act", "mT", l, tb, half)
    for n in range(2):
        for tb in T:
            job("dve", "o", l, n, tb)
    for tb in T:
        for half in range(2):
            job("act", "hT", l, 1, tb, half)
    for tb in T:
        job("act", "r", l, tb)
    job("dve", "cnt", l)
    return out


def hybrid_kernel(nc, A, out):
    jobs = [(("mod", l, c), "dve") for l in range(DEPTH) for c in range(12)]
    for l in range(DEPTH):
        jobs += plan_jobs(l)
    order = [n for n, _ in jobs]
    taker = dict(jobs)
    DONE = {n: i + 1 for i, n in enumerate(order)}
    TAKEN, seen = {}, {"act": 0, "dve": 0}
    for n in order:
        seen[taker[n]] += 1
        TAKEN[n] = seen[taker[n]]

    def w_in(l, name, n, cols):
        o = W_OFF[name] + n * CH
        return A["w_in"][l, :, o:o + cols].rearrange("(k p) n -> p k n", p=P)

    mix = []
    for l in range(DEPTH):
        for c in range(12):
            mix.append((("mod", l, c), A["w_mod"][l, :, c * CH:(c + 1) * CH].rearrange("(k p) n -> p k n", p=P),
                        ("mod", l, c)))
    layer_start = []
    for l in range(DEPTH):
        layer_start.append(len(mix))
        last = tokens_of(l)[-1]
        mix.append((("in", l, "kv"), w_in(l, "kv", 0, 256), ("in", l, "kv", 3)))
        for c in ("q", "f", "v", "x1", "x2"):
            mix.append((("in", l, c), w_in(l, c, 0, CH), ("in", l, c, last)))
        for br, (g, wb) in enumerate((("ga", "w_branch_attn"), ("gf", "w_branch_fnet"), ("gh", "w_branch_hyena"))):
            mix.append((("g", l, br, 0), w_in(l, g, 0, CH), ("g", l, br, 0, last)))
            mix.append((("b", l, br), A[wb][l].rearrange("(k p) n -> p k n", p=P), ("b", l, br, 1, last)))
            mix.append((("g", l, br, 1), w_in(l, g, 1, CH), ("g", l, br, 1, last)))
        for n in range(2):
            mix.append((("o", l, n), A["w_out"][l, :, n * CH:(n + 1) * CH].rearrange("(k p) n -> p k n", p=P),
                        ("o", l, n, last)))
    slot_at, loads, base_loads, n_mix = {}, [0] * 6, [], 0
    for l in range(DEPTH):
        until = layer_start[l + 1] if l + 1 < DEPTH else len(mix)
        for key, _, _ in mix[n_mix:until]:
            s = n_mix % 3
            loads[s] += 1
            slot_at[key] = (s, 16 * loads[s])
            n_mix += 1
        base_loads.append(list(loads))
        loads = [x + NE for x in loads]

    ctx = ExitStack()
    with ctx:
        def sb(name, shape, dt=F32):
            return ctx.enter_context(nc.sbuf_tensor(name, shape, dt))

        def sem(name):
            return ctx.enter_context(nc.semaphore(name))

        bank = [ctx.enter_context(nc.psum_tensor(f"bank{i}", [P, 512], F32)) for i in range(8)]

        ring = sb("ring", [P, 6 * SLOT])
        x = sb("x", [P, 4, D])
        hT = sb("hT", [P, KB, 512])
        work = sb("work", [P, 8192])
        mixed = sb("mixed", [P, 7168])
        const = sb("const", [P, C_END])
        ident = const[:, C_ID:C_ID + P]
        tri = const[:, C_TRI:C_TRI + P]
        ones = const[:, C_ONE:C_ONE + P]
        dft = const[:, C_DFT:C_INV].rearrange("p (t b m) -> p t b m", t=2, b=6)
        inv = const[:, C_INV:C_ROPE].rearrange("p (b m) -> p b m", b=4)
        rope = const[:, C_ROPE:C_MASK].rearrange("p (t j d) -> p t j d", t=2, j=4)
        mask = const[:, C_MASK:C_EXP].rearrange("p (t k) -> p t k", t=2)
        expert_id = const[:, C_EXP:C_END].rearrange("p (t e) -> p t e", t=4)

        M = 3 * SLOT

        def lent(a, n):
            return ring[:, M + a:M + a + n]

        z = lent(0, 6144).rearrange("p (t c n) -> p t c n", t=4, c=3)
        filt = lent(0, 2048).rearrange("p (d t n) -> p d t n", d=2, t=2)
        filt_pm = lent(2048, 2048).rearrange("p (d t n) -> p d t n", d=2, t=2)
        filt_abs = lent(4096, 2048).rearrange("p (d t n) -> p d t n", d=2, t=2)
        merged = lent(0, 4096).rearrange("p (t n) -> p t n", t=4)
        spectra = lent(6144, 5120).rearrange("p (o b n) -> p o b n", o=2, b=5)
        hstage = lent(6144, 1024).rearrange("p (i n) -> p i n", i=2)
        gate_buf = lent(6144, 1024).rearrange("p (i n) -> p i n", i=2)
        merge_tmp = lent(7168, 512)
        out_tmp = lent(7680, 512)
        hid = lent(11264, 1024).rearrange("p (i n) -> p i n", i=4)
        pq = lent(11264, 1024).rearrange("p (i n) -> p i n", i=2)
        hy_bias = lent(11264, 1024).rearrange("p (o n) -> p o n", o=2)
        mod_rows = lent(0, 2 * 6 * D).rearrange("p (l n) -> p l n", l=2)
        norm_rows = hT[0:2, :, :].rearrange("p k n -> p (k n)").rearrange("p (l i n) -> p l i n", l=2, i=2)

        A_bc = work[:, 0:2048].rearrange("p (s n) -> p s n", s=2)
        B_bc = work[:, 2048:4096].rearrange("p (s n) -> p s n", s=2)
        G_bc = work[:, 4096:6144].rearrange("p (s n) -> p s n", s=2)
        hrow = work[:, 6144:8192].rearrange("p (i n) -> p i n", i=2)
        w3 = work[0:64, 0:2048]
        w1 = work[0:33, 2048:2112]
        w2 = work[0:64, 2112:2176]
        feats = work[0:33, 2304:2560]
        decay = work[:, 2560:4096].rearrange("p (i n) -> p i n", i=3)
        four = work[:, 0:1280]
        S_buf = work[:, 0:1024].rearrange("p (i n) -> p i n", i=2)
        P_buf = work[:, 1024:2048].rearrange("p (i n) -> p i n", i=2)
        PT = work[:, 2048:3072].rearrange("p (i k n) -> p i k n", i=2, k=4)
        ya = work[:, 3072:4096].rearrange("p (i n) -> p i n", i=2)
        stage = work[:, 0:3072].rearrange("p (i j n) -> p i j n", i=2, j=3)
        Yspec = work[:, 0:2048].rearrange("p (b n) -> p b n", b=4)
        hy_tmp = work[:, 2048:3072].rearrange("p (i n) -> p i n", i=2)
        rope_tmp = work[:, 4096:5120].rearrange("p (i n) -> p i n", i=2)
        rnorm = work[:, 4096:4608]
        krow = work[:, 5120:5632].rearrange("p (t n) -> p t n", t=4)
        conv_w = work[:, 4096:6144].rearrange("p (j n) -> p j n", j=4)
        qrow = work[:, 6144:8192].rearrange("p (t n) -> p t n", t=4)
        got_a = work[:, 0:2048].rearrange("p (i n) -> p i n", i=2)
        got_b = work[:, 2048:4096].rearrange("p (i n) -> p i n", i=2)

        qT = mixed[:, 0:2048].rearrange("p (j n) -> p j n", j=4)
        yhT = mixed[:, 0:2048].rearrange("p (j n) -> p j n", j=4)
        kT = mixed[:, 2048:2560]
        vrow = mixed[:, 2560:3072].rearrange("p (t n) -> p t n", t=4)
        yaT = mixed[:, 3072:5120].rearrange("p (j n) -> p j n", j=4)
        frow = mixed[:, 3072:5120].rearrange("p (t n) -> p t n", t=4)
        yfT = mixed[:, 5120:7168].rearrange("p (j n) -> p j n", j=4)
        branch_T = [yaT, yfT, yhT]
        xs = mixed[:, 0:2048].rearrange("p (i n) -> p i n", i=2)
        xsT = mixed[:, 2048:4096].rearrange("p (i k n) -> p i k n", i=2, k=KB)
        silu = mixed[:, 4096:5120].rearrange("p (i n) -> p i n", i=2)
        hexp = mixed[:, 5120:6144].rearrange("p (i n) -> p i n", i=2)
        hT_flat = hT[:, :, :].rearrange("p k n -> p (k n)")
        hexpT = hT_flat[:, 0:2048].rearrange("p (i k n) -> p i k n", i=2, k=KB)
        ys = hT_flat[:, 2048:4096].rearrange("p (i n) -> p i n", i=2)
        final_w = mixed[:, 2048:3072]
        final_rows = mixed[:, 0:2048].rearrange("p (i n) -> p i n", i=2)

        c_raw = sb("c_raw", [P, KB, 2])
        c_act = sb("c_act", [P, KB, 2])
        wr = sb("wr", [P, KB, NE])
        br_bc = sb("br_bc", [P, NE])
        sink = sb("sink", [P, DEPTH, NH])
        fcol = sb("fcol", [64, DEPTH, 3])
        stat = sb("stat", [P, 5, 4])
        att = sb("att", [P, 2, 6, NH])
        rt = mixed[:, 6144:7168].rearrange("p (i n) -> p i n", i=16)
        rt4 = sb("rt4", [P, 8, 16])
        rt1 = sb("rt1", [P, 8, 4])
        w_tok = sb("w_tok", [P, 2, 4])
        idx_tok = sb("idx_tok", [P, 2, 4], I32)
        tok_id = sb("tok_id", [P, 4], I32)
        idx_exp = sb("idx_exp", [P, NE], I32)
        idx_over = sb("idx_over", [P, 1], I32)
        zero_i = work[:, 3584:3584 + ROWS_PER_PART].bitcast(I32)
        most = sb("most", [P, 1], I32)
        pace = c_raw[:, 0, :]
        idx_beyond = c_act[:, 0:4, :].rearrange("p k s -> p (k s)").rearrange("p (i t) -> p i t", i=2).bitcast(I32)
        mod_dram = nc.dram_tensor("mod_dram", (DEPTH, 2, 6, D), F32, kind="Internal").ap()
        hp_dram = nc.dram_tensor("hp_dram", (DEPTH * 2, SEQ + 2, 3 * HY), F32, kind="Internal").ap()
        ys_dram = nc.dram_tensor("ys_dram", (P * NE, D), F32, kind="Internal").ap()
        ys_over = [nc.dram_tensor(f"ys_over{l}", (P * NE * OVER_BLOCKS[l], D), F32, kind="Internal").ap()
                   for l in range(DEPTH)]
        h2_of = [nc.dram_tensor(f"h2_dram{l}", (P * len(tokens_of(l)), D), F32, kind="Internal").ap() for l in range(DEPTH)]
        row_tok_of = [nc.dram_tensor(f"row_tok{l}", (P * ROWS_PER_PART, 1), I32, kind="Internal").ap()
                      for l in range(DEPTH)]

        slot_loaded = [sem(f"slot_loaded{i}") for i in range(6)]
        const_loaded = sem("const_loaded")
        small_loaded = sem("small_loaded")
        c_ready = sem("c_ready")
        mm_done = sem("mm_done")
        act_took = sem("act_took")
        dve_took = sem("dve_took")
        dve_step = sem("dve_step")
        act_step = sem("act_step")
        mod_stored = sem("mod_stored")
        zero_ready = sem("zero_ready")
        zero_stored = sem("zero_stored")
        ab_loaded = sem("ab_loaded")
        g_loaded = sem("g_loaded")
        var_ready = sem("var_ready")
        root_ready = sem("root_ready")
        rows_ready = sem("rows_ready")
        filt_loaded = sem("filt_loaded")
        four_loaded = sem("four_loaded")
        bias_loaded = sem("bias_loaded")
        sin_in = sem("sin_in")
        sin_out = sem("sin_out")
        abs_ready = sem("abs_ready")
        pm_ready = sem("pm_ready")
        hp_stored = [sem(f"hp_stored{i}") for i in range(2)]
        max_ready = sem("max_ready")
        exp_done = sem("exp_done")
        sink_in = sem("sink_in")
        sink_exp = sem("sink_exp")
        ya_ready = sem("ya_ready")
        convw_loaded = sem("convw_loaded")
        stage_loaded = [sem(f"stage_loaded{i}") for i in range(2)]
        conv_done = sem("conv_done")
        spec_ready = sem("spec_ready")
        y_ready = sem("y_ready")
        merged_ready = sem("merged_ready")
        h2_stored = [sem(f"h2_stored{i}") for i in range(2)]
        sel_ready = sem("sel_ready")
        idx_ready = sem("idx_ready")
        scattered = sem("scattered")
        idx_loaded = sem("idx_loaded")
        xs_loaded = [sem(f"xs_loaded{i}") for i in range(2)]
        xt_mm = sem("xt_mm")
        xt_took = sem("xt_took")
        gu_mm = sem("gu_mm")
        silu_done = sem("silu_done")
        h_done = sem("h_done")
        ht_mm = sem("ht_mm")
        ht_took = sem("ht_took")
        d_mm = sem("d_mm")
        ys_took = sem("ys_took")
        ys_stored = [sem(f"ys_stored{i}") for i in range(2)]
        got_loaded = sem("got_loaded")
        got_ready = sem("got_ready")
        combined = sem("combined")
        final_loaded = sem("final_loaded")
        final_ready = sem("final_ready")
        out_stored = sem("out_stored")
        over = [{n: sem(f"over{l}_{n}") for n in ("w", "idx", "xs", "xt", "xe", "gu", "s", "h", "ht", "he", "d", "ys",
                                                  "st", "got", "pace")} for l in range(DEPTH)]

        ctx.enter_context(nc.allow_non_contiguous_dma(reason="small vectors laid along the partitions"))
        block = ctx.enter_context(nc.Block())

        T_BEFORE = [0, 4]
        ROWS_AT = {(0, 0): 0, (0, 1): 4, (1, 0): 8, (1, 1): 12}
        N_SMALL = 16 * 11

        def expert_w(l, name, e, n):
            w = A[name]
            if isinstance(e, int):
                return w[l, e, :, n * CH:(n + 1) * CH].rearrange("(k p) n -> p k n", p=P)
            return w[l, bass.ds(e, 1), :, n * CH:(n + 1) * CH].rearrange("o (k p) n -> p (o k) n", p=P)

        def slot(s, cols=CH):
            return ring[:, s * SLOT:s * SLOT + KB * cols].rearrange("p (k n) -> p k n", k=KB)

        EXPERT_CHUNKS = (("w_exp_gate", 0), ("w_exp_up", 0), ("w_exp_gate", 1), ("w_exp_up", 1),
                         ("w_exp_down", 0), ("w_exp_down", 1))

        @block.sync
        def _(sp):
            sp.dma_start(const[:, :], A["k_const"]).then_inc(const_loaded, 16)
            sp.dma_start(x[:, 0:2, :], A["x"][0].rearrange("(t p) n -> p t n", p=P)).then_inc(const_loaded, 16)
            sp.dma_start(x[:, 2:4, :], A["ctx"][0].rearrange("(t p) n -> p t n", p=P)).then_inc(const_loaded, 16)
            owner = [None] * 6

            def wait_slot(s):
                if owner[s] is not None:
                    sp.wait_ge(owner[s][0], owner[s][1])

            n = 0
            for l in range(DEPTH):
                until = layer_start[l + 1] if l + 1 < DEPTH else len(mix)
                while n < until:
                    key, src, last = mix[n]
                    s = n % 3
                    wait_slot(s)
                    if key[0] == "b":
                        dst = ring[:, s * SLOT:(s + 1) * SLOT].rearrange("p (k n) -> p k n", k=4)
                    else:
                        dst = slot(s, src.shape[-1])
                    sp.dma_start(dst, src).then_inc(slot_loaded[s], 16)
                    owner[s] = (mm_done, DONE[last])
                    n += 1
                Lb = NE * l

                def load(e, c, first=False):
                    name, half = EXPERT_CHUNKS[c]
                    if first and c >= 3:
                        sp.wait_ge(dve_took, TAKEN[("o", l, 1, tokens_of(l)[-1])])
                    if first:
                        wait_slot(c)
                    elif c < 4:
                        sp.wait_ge(gu_mm, e * 4 + (4 * (Lb - 1) + c + 1))
                    else:
                        sp.wait_ge(d_mm, e * 2 + (2 * (Lb - 1) + c - 3))
                    sp.dma_start(slot(c), expert_w(l, name, e, half)).then_inc(slot_loaded[c], 16)

                for c in range(4):
                    load(0, c, first=True)
                for c in range(4):
                    load(1, c)
                for c in (4, 5):
                    load(0, c, first=True)
                with sp.Fori(2, NE) as e:
                    for c in range(4):
                        load(e, c)
                    for c in (4, 5):
                        load(e - 1, c)
                for c in (4, 5):
                    load(NE - 1, c)
                for c in range(4):
                    owner[c] = (gu_mm, 4 * (Lb + NE - 1) + c + 1)
                for c in (4, 5):
                    owner[c] = (d_mm, 2 * (Lb + NE - 1) + c - 3)
                o = over[l]
                sp.wait_ge(idx_ready, 2 * l + 2)
                busiest = sp.value_load(most[0:1, 0:1], min_val=0, max_val=512)
                with sp.If(busiest > P):
                    sp.wait_ge(d_mm, 2 * (Lb + NE))

                    def load_all(e, done):
                        if done is not None:
                            sp.wait_ge(o["d"], done)
                        for c, (name, half) in enumerate(EXPERT_CHUNKS):
                            sp.dma_start(slot(c), expert_w(l, name, e, half)).then_inc(o["w"], 16)

                    load_all(0, None)
                    with sp.Fori(1, NE) as e:
                        load_all(e, e)
                    if OVER_BLOCKS[l] > 1:
                        with sp.Fori(1, OVER_BLOCKS[l]) as b:
                            with sp.Fori(0, NE) as e:
                                load_all(e, b * NE + e)
                    sp.wait_ge(o["d"], NE * OVER_BLOCKS[l])
            sp.wait_ge(final_ready, 1)
            sp.dma_start(out[0, 0:P, :], final_rows[:, 0, :]).then_inc(out_stored, 16)
            sp.wait_ge(final_ready, 2)
            sp.dma_start(out[0, P:2 * P, :], final_rows[:, 1, :]).then_inc(out_stored, 16)
            sp.wait_ge(out_stored, 32)

        @block.gpsimd
        def _(pool):
            small = [
                (c_raw[:, :, 0], A["c"].rearrange("o (k p) -> p (o k)", p=P)),
                (c_raw[:, :, 1], A["c_ctx"].rearrange("(k p) -> p k", p=P)),
                (mod_rows[0:2, 0, :], A["b_mod"][0].partition_broadcast(2)),
                (mod_rows[0:2, 1, :], A["b_mod"][1].partition_broadcast(2)),
                (norm_rows[:, :, 0, :], A["norm_mix"].partition_broadcast(2)),
                (norm_rows[:, :, 1, :], A["norm_ffn"].partition_broadcast(2)),
                (wr[:, :, :], A["w_router"].rearrange("(k p) e -> p k e", p=P)),
                (br_bc[:, :], A["b_router"].partition_broadcast(P)),
                (sink[:, :, :], A["attn_sink"].partition_broadcast(P)),
                (tok_id[:, :], A["k_tok"]),
                (fcol[:, :, 0], A["filt_b1"].rearrange("l h -> h l")),
            ]
            for dst, src in small:
                pool.dma_start(dst, src).then_inc(small_loaded, 16)
            pool.dma_start(fcol[:, :, 1], A["filt_freq"].rearrange("l h -> h l")).then_inc(filt_loaded, 16)
            pool.dma_start(fcol[:, :, 2], A["filt_b2"].rearrange("l h -> h l")).then_inc(filt_loaded, 16)
            pool.memset(work[0:4, 0:2 * 3 * HY], 0.0).then_inc(zero_ready, 1)
            pool.memset(zero_i, 0).then_inc(zero_ready, 1)
            pool.wait_ge(zero_ready, 2)
            pool.dma_start(hp_dram[:, 0:SEQ + 2:SEQ + 1, :],
                           work[0:4, 0:2 * 3 * HY].rearrange("p (r n) -> p r n", r=2)).then_inc(zero_stored, 16)
            for l in range(DEPTH):
                pool.dma_start(row_tok_of[l].rearrange("(p m) o -> p (m o)", p=P), zero_i).then_inc(zero_stored, 16)
            pool.wait_ge(zero_stored, 16 * 3)
            for l in range(DEPTH):
                pool.wait_ge(dve_took, TAKEN[("mod", l, 11)])
                pool.dma_start(mod_dram[l].rearrange("s j n -> s (j n)"), mod_rows[0:2, l, :]).then_inc(mod_stored, 16)
            pool.wait_ge(mod_stored, 16 * DEPTH)

            def rows_of(l, j):
                return mod_dram[l, :, j, :].partition_broadcast(P)

            for l in range(DEPTH):
                T = tokens_of(l)
                Lb = NE * l
                if l > 0:
                    pool.wait_ge(combined, 4)
                pool.dma_start(B_bc, rows_of(l, 0)).then_inc(ab_loaded, 16)
                pool.dma_start(A_bc, rows_of(l, 1)).then_inc(ab_loaded, 16)
                pool.wait_ge(rows_ready, ROWS_AT[l, 0] + 4)
                for dst, src in ((w1, A["filt_w1"][l]), (w2, A["filt_w2"][l]), (w3, A["filt_w3"][l]),
                                 (feats, A["k_feats"]), (decay, A["k_decay"].rearrange("p (i n) -> p i n", i=3))):
                    pool.dma_start(dst, src).then_inc(filt_loaded, 16)
                pool.wait_ge(mm_done, DONE[("f3", l, 1, 1, 1)])
                pool.dma_start(four, A["k_four"]).then_inc(four_loaded, 16)
                pool.wait_ge(mm_done, DONE[("fy", l, len(T) // 2 - 1, 3)])
                pool.dma_start(hy_bias, A["hyena_bias"][l].partition_broadcast(P)).then_inc(bias_loaded, 16)
                pool.wait_ge(ya_ready, T_BEFORE[l] + len(T))
                pool.wait_ge(mm_done, DONE[("yaT", l, T[-1])])
                for b in range(2):
                    pool.wait_ge(hp_stored[b], 16 * (3 * (T_BEFORE[l] + len(T)) // 2))
                i = 3 * T_BEFORE[l]
                for c in range(3):
                    if c > 0:
                        pool.wait_ge(conv_done, i)
                    pool.dma_start(conv_w[:, 0:3, :], A["conv_w"][l, :, c * HY:(c + 1) * HY].partition_broadcast(P))\
                        .then_inc(convw_loaded, 16)
                    pool.dma_start(conv_w[:, 3, :], A["conv_b"][l, c * HY:(c + 1) * HY].partition_broadcast(P))\
                        .then_inc(convw_loaded, 16)
                    for tb in T:
                        if i >= 3 * T_BEFORE[l] + 2:
                            pool.wait_ge(conv_done, i - 1)
                        for j in range(3):
                            r = (tb % 2) * P + j
                            pool.dma_start(stage[:, i % 2, j, :], hp_dram[2 * l + tb // 2, r:r + P, c * HY:(c + 1) * HY])\
                                .then_inc(stage_loaded[i % 2], 16)
                        i += 1
                pool.wait_ge(conv_done, i)
                pool.dma_start(G_bc, rows_of(l, 2)).then_inc(g_loaded, 16)
                pool.wait_ge(y_ready, 2 * (T_BEFORE[l] + len(T)))
                pool.wait_ge(mm_done, DONE[("c", l, 1, len(T) // 2 - 1, 1)])
                pool.dma_start(B_bc, rows_of(l, 3)).then_inc(ab_loaded, 16)
                pool.dma_start(A_bc, rows_of(l, 4)).then_inc(ab_loaded, 16)
                pool.wait_ge(dve_took, TAKEN[("o", l, 1, T[-1])])
                pool.dma_start(G_bc, rows_of(l, 5)).then_inc(g_loaded, 16)
                for k, tb in enumerate(T):
                    pool.wait_ge(rows_ready, ROWS_AT[l, 1] + k + 1)
                    pool.dma_start(h2_of[l][tb * P:(tb + 1) * P, :], hrow[:, k % 2, :]).then_inc(h2_stored[k % 2], 16)
                pool.wait_ge(idx_ready, 2 * l + 2)
                for tb in T:
                    for i2 in range(2):
                        pool.indirect_dma_start(row_tok_of[l][:, :], bass.IndirectOffsetOnAxis(ap=idx_tok[:, i2, tb:tb + 1], axis=0),
                                                tok_id[:, tb:tb + 1], None).then_inc(scattered, 16)
                pool.wait_ge(scattered, 16 * 2 * (T_BEFORE[l] + len(T)))
                m_over = NE * OVER_BLOCKS[l]
                first_rows = row_tok_of[l][0:P * NE, :].rearrange("(p m) o -> p (m o)", p=P)
                over_rows = row_tok_of[l][P * NE:P * (NE + m_over), :].rearrange("(p m) o -> p (m o)", p=P)
                pool.dma_start(idx_exp[:, :], first_rows).then_inc(idx_loaded, 16)
                pool.wait_ge(idx_loaded, 16 * (l + 1))
                for b in range(2):
                    pool.wait_ge(h2_stored[b], 16 * (T_BEFORE[l] + len(T)) // 2)
                ys_rows = ys_dram.rearrange("(p m) n -> p m n", p=P)
                ys_beyond = ys_over[l].rearrange("(p m) n -> p m n", p=P)
                for e in range(NE + 2):
                    if e < NE:
                        if e >= 2:
                            pool.wait_ge(xt_mm, 2 * (Lb + e - 1))
                        pool.indirect_dma_start(xs[:, e % 2, :], None, h2_of[l][:, :],
                                                bass.IndirectOffsetOnAxis(ap=idx_exp[:, e:e + 1], axis=0))\
                            .then_inc(xs_loaded[e % 2], 16)
                    if e >= 2:
                        pool.wait_ge(ys_took, 2 * (Lb + e - 1))
                        pool.dma_start(ys_rows[:, e - 2, :], ys[:, e % 2, :]).then_inc(ys_stored[e % 2], 16)
                for b in range(2):
                    pool.wait_ge(ys_stored[b], 8 * (Lb + NE))
                o = over[l]
                busiest = pool.value_load(most[0:1, 0:1], min_val=0, max_val=512)
                with pool.If(busiest > P):
                    nc.gpsimd.tensor_tensor(pace, pace, pace, ALU.subtract).then_inc(o["pace"], 1)
                    with pool.Fori(0, OVER_BLOCKS[l]) as b:
                        with pool.Fori(0, NE) as e:
                            k = pool.snap(b * NE + e)
                            pool.dma_start(idx_over[:, :], over_rows[:, bass.ds(k, 1)]).then_inc(o["idx"], 16)
                            pool.wait_ge(o["idx"], k * 16 + 16)
                            pool.wait_ge(o["pace"], k * 2 + 1)
                            nc.gpsimd.tensor_tensor(pace, pace, pace, ALU.subtract).then_inc(o["pace"], 1)
                            pool.indirect_dma_start(xs[:, 0, :], None, h2_of[l][:, :],
                                                    bass.IndirectOffsetOnAxis(ap=idx_over[:, 0:1], axis=0))\
                                .then_inc(o["xs"], 16)
                            pool.wait_ge(o["ys"], k + 1)
                            pool.wait_ge(o["pace"], k * 2 + 2)
                            nc.gpsimd.tensor_tensor(pace, pace, pace, ALU.subtract).then_inc(o["pace"], 1)
                            pool.dma_start(ys_beyond[:, bass.ds(k, 1), :].rearrange("p o n -> p (o n)"), ys[:, 0, :])\
                                .then_inc(o["st"], 16)
                            pool.wait_ge(o["st"], k * 16 + 16)
                    pool.wait_ge(o["pace"], 2 * m_over + 1)
                for k, tb in enumerate(T):
                    if k >= 2:
                        pool.wait_ge(combined, T_BEFORE[l] + k - 1)
                    for i2, got in ((0, got_a), (1, got_b)):
                        pool.indirect_dma_start(got[:, k % 2, :], None, ys_dram[:, :],
                                                bass.IndirectOffsetOnAxis(ap=idx_tok[:, i2, tb:tb + 1], axis=0),
                                                bounds_check=P * NE - 1, oob_is_err=False).then_inc(got_loaded, 16)
                    pool.wait_ge(got_loaded, 32 * (T_BEFORE[l] + k + 1))
                    with pool.If(busiest > P):
                        for i2, got in ((0, got_a), (1, got_b)):
                            pool.indirect_dma_start(got[:, k % 2, :], None, ys_over[l][:, :],
                                                    bass.IndirectOffsetOnAxis(ap=idx_beyond[:, i2, tb:tb + 1], axis=0),
                                                    bounds_check=P * m_over - 1, oob_is_err=False).then_inc(o["got"], 16)
                        pool.wait_ge(o["got"], 32 * (k + 1))
                    nc.gpsimd.tensor_tensor(pace, pace, pace, ALU.subtract).then_inc(got_ready, 1)
                    pool.wait_ge(got_ready, T_BEFORE[l] + k + 1)
            pool.dma_start(final_w, A["norm_final"].partition_broadcast(P)).then_inc(final_loaded, 16)
            pool.wait_ge(final_loaded, 16)

        @block.scalar
        def _(act):
            took = [0]

            def take(name):
                assert taker[name] == "act" and TAKEN[name] == took[0] + 1, name
                took[0] += 1
                act.wait_ge(mm_done, DONE[name])
                return bank[(DONE[name] - 1) % 8]

            act.wait_ge(small_loaded, N_SMALL)
            nc.scalar.activation(c_act[:, :, :], c_raw[:, :, :], ACT.Silu).then_inc(c_ready, 1)

            def root(ph, nt):
                act.wait_ge(var_ready, ph + 1)
                nc.scalar.activation(stat[:, 2, 0:nt], stat[:, 1, 0:nt], ACT.Sqrt).then_inc(root_ready, 1)

            def transposed(l, ph, tbs):
                for tb in tbs:
                    for half in range(2):
                        b = take(("hT", l, ph, tb, half))
                        nc.scalar.activation(hT[:, 4 * half:4 * half + 4, tb * P:(tb + 1) * P],
                                             b[:, :].rearrange("p (k n) -> p k n", k=4), ACT.Copy)\
                            .then_inc(act_took, 1)

            for l in range(DEPTH):
                T = tokens_of(l)
                Lb = NE * l
                root(2 * l, 4)
                transposed(l, 0, range(4))
                for tb in range(4):
                    b = take(("kT", l, tb))
                    nc.scalar.activation(kT[:, tb * P:(tb + 1) * P], b[:, 0:P], ACT.Copy).then_inc(act_took, 1)
                for tb in T:
                    b = take(("in", l, "f", tb))
                    nc.scalar.activation(frow[:, tb, :], b[:, :], ACT.Copy).then_inc(act_took, 1)
                for tb in T:
                    b = take(("qT", l, tb))
                    nc.scalar.activation(qT[:, :, tb * P:(tb + 1) * P], b[:, :].rearrange("p (j n) -> p j n", j=4),
                                         ACT.Copy).then_inc(act_took, 1)
                i = 3 * T_BEFORE[l]
                for c, name in enumerate(("v", "x1", "x2")):
                    for tb in T:
                        b = take(("in", l, name, tb))
                        if i >= 2:
                            act.wait_ge(hp_stored[i % 2], 16 * (i // 2))
                        nc.scalar.activation(hstage[:, i % 2, :], b[:, :], ACT.Copy).then_inc(act_took, 1)
                        act.wait_ge(act_took, took[0])
                        r = 1 + (tb % 2) * P
                        act.dma_start(hp_dram[2 * l + tb // 2, r:r + P, c * HY:(c + 1) * HY], hstage[:, i % 2, :])\
                            .then_inc(hp_stored[i % 2], 16)
                        i += 1
                for n in range(2):
                    act.wait_ge(sin_in, 2 * l + n + 1)
                    nc.scalar.activation(hid[0:64, 2 + n, :], hid[0:64, 0, :], ACT.Sin).then_inc(sin_out, 1)
                for o in range(2):
                    if o:
                        act.wait_ge(mm_done, DONE[("fn", l, 0)])
                    for d in range(2):
                        for tt in range(2):
                            act.wait_ge(dve_took, TAKEN[("f3", l, o, d, tt)])
                            nc.scalar.activation(filt_abs[:, d, tt, :], filt[:, d, tt, :], ACT.Abs).then_inc(abs_ready, 1)
                for s in range(len(T) // 2):
                    for g in range(5):
                        if g < 4:
                            b = take(("fp", l, s, g))
                            nc.scalar.activation(pq[:, g % 2, :], b[:, :], ACT.Copy).then_inc(act_took, 1)
                        if g > 0:
                            b = take(("fy", l, s, g - 1))
                            nc.scalar.activation(yfT[:, g - 1, s * SEQ:(s + 1) * SEQ], b[:, 0:SEQ], ACT.Copy)\
                                .then_inc(act_took, 1)
                heads = [(tb, h) for tb in T for h in range(NH)]
                hb = 8 * T_BEFORE[l]
                for i in range(len(heads) + 3):
                    if i < len(heads):
                        tb, h = heads[i]
                        nk = 512 if tb < 2 else 256
                        act.wait_ge(max_ready, hb + i + 1)
                        if i >= 2:
                            act.wait_ge(mm_done, DONE[("pt", l, *heads[i - 2])])
                        k = i // NH
                        if h == 0 and k >= 2:
                            act.wait_ge(ya_ready, T_BEFORE[l] + k - 1)
                        nc.scalar.activation(P_buf[:, i % 2, 0:nk], S_buf[:, i % 2, 0:nk], ACT.Exp,
                                             bias=att[:, k % 2, 1, h:h + 1], accum_out=att[:, k % 2, 2, h:h + 1]).then_inc(exp_done, 1)
                        if h == NH - 1:
                            act.wait_ge(sink_in, T_BEFORE[l] + i // NH + 1)
                            nc.scalar.activation(att[:, k % 2, 4, :], att[:, k % 2, 3, :], ACT.Exp).then_inc(sink_exp, 1)
                    if 2 <= i < len(heads) + 2:
                        tb, h = heads[i - 2]
                        nk = 4 if tb < 2 else 2
                        b = take(("pt", l, tb, h))
                        nc.scalar.activation(PT[:, i % 2, 0:nk, :], b[:, 0:nk * P].rearrange("p (k n) -> p k n", k=nk),
                                             ACT.Copy).then_inc(act_took, 1)
                    if i >= 3 and heads[i - 3][1] == NH - 1 and heads[i - 3][0] > 0:
                        tb = heads[i - 3][0] - 1
                        b = take(("yaT", l, tb))
                        nc.scalar.activation(yaT[:, :, tb * P:(tb + 1) * P], b[:, :].rearrange("p (j n) -> p j n", j=4),
                                             ACT.Copy).then_inc(act_took, 1)
                b = take(("yaT", l, T[-1]))
                nc.scalar.activation(yaT[:, :, T[-1] * P:(T[-1] + 1) * P], b[:, :].rearrange("p (j n) -> p j n", j=4),
                                     ACT.Copy).then_inc(act_took, 1)
                for tb in T:
                    b = take(("yhT", l, tb))
                    nc.scalar.activation(yhT[:, :, tb * P:(tb + 1) * P], b[:, :].rearrange("p (j n) -> p j n", j=4),
                                         ACT.Copy).then_inc(act_took, 1)
                seq = [(br, n, tb) for br in range(3) for n in range(2) for tb in T]
                for i, key in enumerate(seq):
                    b = take(("g", l, *key))
                    if i >= 2:
                        act.wait_ge(dve_took, TAKEN[("b", l, *seq[i - 2])])
                    nc.scalar.activation(gate_buf[:, i % 2, :], b[:, :], ACT.Sigmoid).then_inc(act_took, 1)
                for tb in T:
                    for half in range(2):
                        b = take(("mT", l, tb, half))
                        nc.scalar.activation(hT[:, 4 * half:4 * half + 4, tb * P:(tb + 1) * P],
                                             b[:, :].rearrange("p (k n) -> p k n", k=4), ACT.Copy)\
                            .then_inc(act_took, 1)
                root(2 * l + 1, len(T))
                transposed(l, 1, T)
                for tb in T:
                    b = take(("r", l, tb))
                    nc.scalar.activation(rt[:, 0, tb * NE:(tb + 1) * NE], b[:, 0:NE], ACT.Sigmoid).then_inc(act_took, 1)

                def take_xs(e, par):
                    for half in range(2):
                        act.wait_ge(xt_mm, e * 2 + (2 * Lb + half + 1))
                        nc.scalar.activation(xsT[:, par, 4 * half:4 * half + 4, :],
                                             bank[2 + half][:, :].rearrange("p (k n) -> p k n", k=4), ACT.Copy)\
                            .then_inc(xt_took, 1)

                def expert(e, par, last=False):
                    for n in range(2):
                        act.wait_ge(gu_mm, e * 4 + (4 * Lb + 2 * n + 1))
                        if not (isinstance(e, int) and e + Lb == 0):
                            act.wait_ge(h_done, e * 2 + (2 * Lb - 2 + n + 1))
                        nc.scalar.activation(silu[:, n, :], bank[2 + 2 * n][:, :], ACT.Silu).then_inc(silu_done, 1)
                    for half in range(2):
                        act.wait_ge(ht_mm, e * 2 + (2 * Lb + half + 1))
                        nc.scalar.activation(hexpT[:, par, 4 * half:4 * half + 4, :],
                                             bank[6 + half][:, :].rearrange("p (k n) -> p k n", k=4), ACT.Copy)\
                            .then_inc(ht_took, 1)
                    if not last:
                        take_xs(e + 1, 1 - par)

                take_xs(0, 0)
                expert(0, 0)
                with act.Fori(0, NE // 2 - 1) as i:
                    expert(i * 2 + 1, 1)
                    expert(i * 2 + 2, 0)
                expert(NE - 1, 1, last=True)
                o = over[l]
                act.wait_ge(idx_ready, 2 * l + 2)
                busiest = act.value_load(most[0:1, 0:1], min_val=0, max_val=512)
                with act.If(busiest > P):
                    with act.Fori(0, OVER_BLOCKS[l] * NE) as k:
                        act.wait_ge(o["xt"], k + 1)
                        for half in range(2):
                            t = nc.scalar.activation(xsT[:, 0, 4 * half:4 * half + 4, :],
                                                     bank[2 + half][:, :].rearrange("p (k n) -> p k n", k=4), ACT.Copy)
                        t.then_inc(o["xe"], 1)
                        act.wait_ge(o["gu"], k + 1)
                        for n in range(2):
                            t = nc.scalar.activation(silu[:, n, :], bank[2 + 2 * n][:, :], ACT.Silu)
                        t.then_inc(o["s"], 1)
                        act.wait_ge(o["ht"], k + 1)
                        for half in range(2):
                            t = nc.scalar.activation(hexpT[:, 0, 4 * half:4 * half + 4, :],
                                                     bank[6 + half][:, :].rearrange("p (k n) -> p k n", k=4), ACT.Copy)
                        t.then_inc(o["he"], 1)
            root(4, 2)

        @block.vector
        def _(dve):
            steps = [0]
            took = [0]

            def link(ins):
                steps[0] += 1
                ins.then_inc(dve_step, 1)
                dve.wait_ge(dve_step, steps[0])

            def take(name):
                assert taker[name] == "dve" and TAKEN[name] == took[0] + 1, name
                took[0] += 1
                dve.wait_ge(mm_done, DONE[name])
                return bank[(DONE[name] - 1) % 8]

            def TT(o, a, b, op):
                return nc.vector.tensor_tensor(o, a, b, op)

            dve.wait_ge(small_loaded, N_SMALL)
            for l in range(DEPTH):
                for c in range(12):
                    b = take(("mod", l, c))
                    row = mod_rows[0:2, l, c * CH:(c + 1) * CH]
                    ins = TT(row, b[0:2, :], row, ALU.add).then_inc(dve_took, 1)
                    dve.wait_ge(dve_took, took[0])
                    if c in (2, 3, 8, 9):
                        dve.wait_ge(dve_took, took[0])
                        link(nc.vector.scalar_tensor_tensor(out=row, in0=row, scalar=1.0,
                                                            in1=norm_rows[:, l, c // 6, (c % 2) * CH:(c % 2 + 1) * CH],
                                                            op0=ALU.add, op1=ALU.mult))

            def inverse_rms(ph, tbs):
                nt = len(tbs)
                for k, tb in enumerate(tbs):
                    link(nc.vector.tensor_tensor_reduce(hrow[:, k % 2, :], x[:, tb, :], x[:, tb, :], 1.0, 0.0,
                                                        ALU.mult, ALU.add, stat[:, 0, k:k + 1]))
                nc.vector.tensor_scalar(stat[:, 1, 0:nt], stat[:, 0, 0:nt], 1.0 / D, EPS, ALU.mult, ALU.add)\
                    .then_inc(var_ready, 1)
                dve.wait_ge(root_ready, ph + 1)
                link(nc.vector.reciprocal(stat[:, 3, 0:nt], stat[:, 2, 0:nt]))
                link(TT(stat[:, 4, 0:nt], stat[:, 3, 0:nt], stat[:, 3, 0:nt], ALU.mult))
                link(TT(stat[:, 4, 0:nt], stat[:, 4, 0:nt], stat[:, 1, 0:nt], ALU.mult))
                link(nc.vector.tensor_scalar(stat[:, 4, 0:nt], stat[:, 4, 0:nt], -0.5, 1.5, ALU.mult, ALU.add))
                link(TT(stat[:, 3, 0:nt], stat[:, 3, 0:nt], stat[:, 4, 0:nt], ALU.mult))

            def norm(l, p, tbs):
                ph = 2 * l + p
                inverse_rms(ph, tbs)
                dve.wait_ge(ab_loaded, 32 * (ph + 1))
                for k, tb in enumerate(tbs):
                    if k >= 2:
                        dve.wait_ge(mm_done, DONE[("hT", l, p, tbs[k - 2], 1)])
                        if p == 1:
                            dve.wait_ge(h2_stored[k % 2], 16 * (T_BEFORE[l] // 2 + k // 2))
                    link(nc.vector.scalar_tensor_tensor(out=hrow[:, k % 2, :], in0=x[:, tb, :], scalar=stat[:, 3, k:k + 1],
                                                        in1=A_bc[:, tb // 2, :], op0=ALU.mult, op1=ALU.mult))
                    TT(hrow[:, k % 2, :], hrow[:, k % 2, :], B_bc[:, tb // 2, :], ALU.add).then_inc(rows_ready, 1)

            def rotate(src, tb, nh, j, dst):
                w = nh * HD
                cos = rope[:, tb, 2 * j, :].unsqueeze(1).broadcast_to([P, nh, HD])
                sin = rope[:, tb, 2 * j + 1, :].rearrange("p (a b i) -> p a b i", a=2, b=2)
                t0 = rope_tmp[:, 0, 0:w].rearrange("p (h d) -> p h d", h=nh)
                t1 = rope_tmp[:, 1, 0:w].rearrange("p (h a b i) -> p h a b i", h=nh, a=2, b=2)
                s5 = src.rearrange("p (h a b i) -> p h a b i", h=nh, a=2, b=2)
                TT(t0, src.rearrange("p (h d) -> p h d", h=nh), cos, ALU.mult).then_inc(dve_step, 1)
                for b in range(2):
                    TT(t1[:, :, :, b, :], s5[:, :, :, 1 - b, :],
                       sin[:, :, b, :].unsqueeze(1).broadcast_to([P, nh, 2, 16]), ALU.mult).then_inc(dve_step, 1)
                steps[0] += 3
                dve.wait_ge(dve_step, steps[0])
                if nh == NH:
                    a = rope_tmp[:, 0, :].rearrange("p (g j d) -> p g j d", g=2, j=4)
                    b2 = rope_tmp[:, 1, :].rearrange("p (g j d) -> p g j d", g=2, j=4)
                    return TT(dst.rearrange("p (j g d) -> p g j d", g=2, j=4), a, b2, ALU.add)
                return TT(dst, rope_tmp[:, 0, 0:w], rope_tmp[:, 1, 0:w], ALU.add)

            dve.wait_ge(const_loaded, 48)
            for l in range(DEPTH):
                T = tokens_of(l)
                nt = len(T)
                Lb = NE * l
                norm(l, 0, range(4))
                for tb in range(4):
                    b = take(("in", l, "kv", tb))
                    link(nc.vector.tensor_copy(vrow[:, tb, :], b[:, P:2 * P]))
                    kdst = krow[:, tb, :]
                    if tb < 2:
                        rotate(b[:, 0:P], tb, NKV, 1, kdst).then_inc(dve_took, 1)
                        dve.wait_ge(dve_took, took[0])
                    else:
                        nc.vector.tensor_copy(kdst, b[:, 0:P]).then_inc(dve_took, 1)
                        dve.wait_ge(dve_took, took[0])
                for k, tb in enumerate(T):
                    b = take(("in", l, "q", tb))
                    if k == 0:
                        dve.wait_ge(mm_done, DONE[("hT", l, 0, 3, 1)])
                    if tb < 2:
                        rotate(b[:, :], tb, NH, 0, qrow[:, tb, :]).then_inc(dve_took, 1)
                        dve.wait_ge(dve_took, took[0])
                    else:
                        nc.vector.tensor_scalar(qrow[:, tb, :].rearrange("p (j g d) -> p g j d", g=2, j=4),
                                                b[:, :].rearrange("p (g j d) -> p g j d", g=2, j=4),
                                                HD ** -0.5, None, ALU.mult).then_inc(dve_took, 1)
                        dve.wait_ge(dve_took, took[0])
                if l == 0:
                    dve.wait_ge(filt_loaded, 16 * 7)
                else:
                    dve.wait_ge(filt_loaded, 16 * 12)
                for n in range(2):
                    b = take(("fl", l, n + 1))
                    h0, h1 = hid[0:64, 0, :], hid[0:64, 1, :]
                    nc.vector.tensor_scalar(h0, b[0:64, 0:SEQ], fcol[:, l, 2 * n:2 * n + 1], fcol[:, l, 1:2],
                                            ALU.add, ALU.mult).then_inc(dve_took, 1)
                    dve.wait_ge(dve_took, took[0])
                    link(nc.vector.tensor_scalar(h1, h0, INV_2PI, MAGIC, ALU.mult, ALU.add))
                    link(nc.vector.tensor_scalar(h1, h1, -MAGIC, None, ALU.add))
                    for part in TWO_PI:
                        link(nc.vector.scalar_tensor_tensor(out=h0, in0=h1, scalar=-part, in1=h0, op0=ALU.mult,
                                                            op1=ALU.add))
                    nc.vector.tensor_scalar(h0, h0, PI, -PI, ALU.min, ALU.max).then_inc(sin_in, 1)
                    dve.wait_ge(sin_out, 2 * l + n + 1)
                for o in range(2):
                    for d in range(2):
                        for tt in range(2):
                            b = take(("f3", l, o, d, tt))
                            if o:
                                dve.wait_ge(abs_ready, 8 * l + 4)
                            TT(filt[:, d, tt, :], b[:, :], decay[:, 2 if (d == 1 and tt == 0) else tt, :], ALU.mult)\
                                .then_inc(dve_took, 1)
                            dve.wait_ge(dve_took, took[0])
                    if o:
                        dve.wait_ge(mm_done, DONE[("fk", l, 0, 4)])
                    for tt in range(2):
                        link(TT(filt_pm[:, 0, tt, :], filt[:, 0, tt, :], filt[:, 1, tt, :], ALU.add))
                        ins = TT(filt_pm[:, 1, tt, :], filt[:, 0, tt, :], filt[:, 1, tt, :], ALU.subtract)
                        link(ins) if tt == 0 else ins.then_inc(pm_ready, 1)
                    b = take(("fn", l, o))
                    nc.vector.reciprocal(rnorm, b[:, :]).then_inc(dve_took, 1)
                    dve.wait_ge(dve_took, took[0])
                    if o == 0:
                        for i in range(2):
                            dve.wait_ge(hp_stored[i], 16 * (3 * (T_BEFORE[l] + nt) // 2))
                    for k in range(5):
                        b = take(("fk", l, o, k))
                        TT(spectra[:, o, k, :], b[:, :], rnorm, ALU.mult).then_inc(dve_took, 1)
                        dve.wait_ge(dve_took, took[0])
                heads = [(tb, h) for tb in T for h in range(NH)]
                hb = NH * T_BEFORE[l]
                dve.wait_ge(mm_done, DONE[("fy", l, nt // 2 - 1, 3)])

                def finish_block(tb, i):
                    n = T_BEFORE[l] + i
                    dve.wait_ge(sink_exp, n + 1)
                    dve.wait_ge(exp_done, NH * (n + 1))
                    link(TT(att[:, i % 2, 5, :], att[:, i % 2, 2, :], att[:, i % 2, 4, :], ALU.add))
                    link(nc.vector.reciprocal(att[:, i % 2, 5, :], att[:, i % 2, 5, :]))
                    dve.wait_ge(dve_took, took[0])
                    y3 = ya[:, i % 2, :].rearrange("p (h d) -> p h d", h=NH)
                    TT(y3, y3, att[:, i % 2, 5, :].unsqueeze(2).broadcast_to([P, NH, HD]), ALU.mult).then_inc(ya_ready, 1)

                for i in range(len(heads) + 3):
                    if i < len(heads):
                        tb, h = heads[i]
                        nk = 512 if tb < 2 else 256
                        b = take(("sc", l, tb, h))
                        if i >= 2:
                            dve.wait_ge(exp_done, hb + i - 1)
                        m = mask[:, tb, :] if tb < 2 else mask[:, 0, 256:512]
                        nc.vector.tensor_tensor_reduce(S_buf[:, i % 2, 0:nk], b[:, 0:nk], m, 1.0, -3.0e38, ALU.add,
                                                       ALU.max, att[:, i // NH % 2, 0, h:h + 1]).then_inc(dve_took, 1)
                        dve.wait_ge(dve_took, took[0])
                        nc.vector.tensor_scalar(att[:, i // NH % 2, 1, h:h + 1], att[:, i // NH % 2, 0, h:h + 1], sink[:, l, h:h + 1], -1.0,
                                                ALU.max, ALU.mult).then_inc(max_ready, 1)
                        if h == NH - 1:
                            dve.wait_ge(max_ready, hb + i + 1)
                            TT(att[:, i // NH % 2, 3, :], att[:, i // NH % 2, 1, :], sink[:, l, :], ALU.add).then_inc(sink_in, 1)
                    if i >= 3:
                        tb, h = heads[i - 3]
                        k = (i - 3) // NH
                        if h == 0 and k >= 2:
                            dve.wait_ge(mm_done, DONE[("yaT", l, T[k - 2])])
                        b = take(("pv", l, tb, h))
                        nc.vector.tensor_copy(ya[:, k % 2, h * HD:(h + 1) * HD], b[:, 0:HD]).then_inc(dve_took, 1)
                        dve.wait_ge(dve_took, took[0])
                        if h == NH - 1:
                            finish_block(tb, k)
                i = 3 * T_BEFORE[l]
                for c in range(3):
                    dve.wait_ge(convw_loaded, 32 * (3 * l + c + 1))
                    for tb in T:
                        dve.wait_ge(stage_loaded[i % 2], 48 * (i // 2 + 1))
                        st = stage[:, i % 2, :, :]
                        link(TT(st, st, conv_w[:, 0:3, :], ALU.mult))
                        zt = z[:, tb, c, :]
                        link(TT(zt, st[:, 0, :], st[:, 1, :], ALU.add))
                        link(TT(zt, zt, st[:, 2, :], ALU.add))
                        TT(zt, zt, conv_w[:, 3, :], ALU.add).then_inc(conv_done, 1)
                        i += 1
                dve.wait_ge(conv_done, i)
                dve.wait_ge(bias_loaded, 16 * (l + 1))
                for o in range(2):
                    for s in range(nt // 2):
                        for half in range(2):
                            re, im = spectra[:, o, half, :], spectra[:, o, 2 + half, :]
                            re2 = spectra[:, o, 4 if half == 0 else 1, :]
                            ur = take(("u", l, o, s, (FR0, FR1)[half]))
                            if half == 0 and (o or s):
                                prev = ("c", l, o, s - 1, 1) if s else ("c", l, o - 1, nt // 2 - 1, 1)
                                dve.wait_ge(mm_done, DONE[prev])
                            yr, yi = Yspec[:, half, :], Yspec[:, 2 + half, :]
                            link(TT(yr, ur[:, :], re, ALU.mult))
                            TT(yi, ur[:, :], im, ALU.mult).then_inc(dve_took, 1)
                            dve.wait_ge(dve_took, took[0])
                            ui = take(("u", l, o, s, (FI0, FI1)[half]))
                            link(TT(hy_tmp[:, 0, :], ui[:, :], im, ALU.mult))
                            TT(hy_tmp[:, 1, :], ui[:, :], re2, ALU.mult).then_inc(dve_took, 1)
                            dve.wait_ge(dve_took, took[0])
                            link(TT(yr, yr, hy_tmp[:, 0, :], ALU.subtract))
                            TT(yi, yi, hy_tmp[:, 1, :], ALU.add).then_inc(spec_ready, 1)
                            dve.wait_ge(spec_ready, 2 * (o * (nt // 2) + s) + half + 1 + 2 * T_BEFORE[l])
                        for tt in range(2):
                            tb = 2 * s + tt
                            y = z[:, tb, 0, :]
                            link(TT(hy_tmp[:, tt, :], y, hy_bias[:, o, :], ALU.mult))
                            b = take(("c", l, o, s, tt))
                            TT(hy_tmp[:, tt, :], b[:, :], hy_tmp[:, tt, :], ALU.add).then_inc(dve_took, 1)
                            dve.wait_ge(dve_took, took[0])
                            TT(y, hy_tmp[:, tt, :], z[:, tb, 1 + o, :], ALU.mult).then_inc(y_ready, 1)
                        dve.wait_ge(y_ready, 2 * T_BEFORE[l] + o * nt + 2 * (s + 1))
                for br in range(3):
                    for n in range(2):
                        for tb in T:
                            b = take(("b", l, br, n, tb))
                            g = ("g", l, br, n, tb)
                            dve.wait_ge(act_took, TAKEN[g])
                            gb = gate_buf[:, (br * 2 * nt + n * nt + T.index(tb)) % 2, :]
                            m = merged[:, tb, n * CH:(n + 1) * CH]
                            if br == 0:
                                TT(m, b[:, :], gb, ALU.mult).then_inc(dve_took, 1)
                                dve.wait_ge(dve_took, took[0])
                                continue
                            TT(merge_tmp, b[:, :], gb, ALU.mult).then_inc(dve_took, 1)
                            dve.wait_ge(dve_took, took[0])
                            ins = TT(m, m, merge_tmp, ALU.add)
                            if br == 1:
                                link(ins)
                            else:
                                ins.then_inc(merged_ready, 1)
                                dve.wait_ge(merged_ready, 2 * T_BEFORE[l] + n * nt + T.index(tb) + 1)
                dve.wait_ge(g_loaded, 16 * (2 * l + 1))
                for n in range(2):
                    for tb in T:
                        b = take(("o", l, n, tb))
                        link(TT(out_tmp, b[:, :], G_bc[:, tb // 2, n * CH:(n + 1) * CH], ALU.mult))
                        xt = x[:, tb, n * CH:(n + 1) * CH]
                        TT(xt, xt, out_tmp, ALU.add).then_inc(dve_took, 1)
                        dve.wait_ge(dve_took, took[0])
                norm(l, 1, T)
                w16 = nt * NE
                dve.wait_ge(act_took, TAKEN[("r", l, T[-1])])

                def r(i):
                    return rt[:, i, 0:w16]

                def r4(i):
                    return r(i).rearrange("p (q i) -> p q i", i=4)

                def r16(i):
                    return r(i).rearrange("p (t e) -> p t e", e=NE)

                def beats(val, res, k):
                    for j in range(4):
                        if j < 3:
                            link(TT(res[j][:, :, j + 1:4], val[:, :, j:j + 1].broadcast_to([P, k, 3 - j]),
                                    val[:, :, j + 1:4], ALU.is_ge))
                        if j > 0:
                            link(TT(res[j][:, :, 0:j], val[:, :, j:j + 1].broadcast_to([P, k, j]), val[:, :, 0:j],
                                    ALU.is_gt))

                link(nc.vector.memset(rt[:, 2:6, :], 0.0))
                link(nc.vector.memset(rt4[:, 1:5, :], 0.0))
                link(TT(r16(1), r16(0), br_bc[:, :].unsqueeze(1).broadcast_to([P, nt, NE]), ALU.add))
                beats(r4(1), [r4(2 + j) for j in range(4)], nt * 4)
                link(TT(r(6), r(2), r(3), ALU.add))
                link(TT(r(6), r(6), r(4), ALU.add))
                link(TT(r(6), r(6), r(5), ALU.add))
                link(nc.vector.tensor_scalar(r(7), r(6), 2.0, None, ALU.is_lt))
                link(TT(r(8), r(1), r(7), ALU.mult))
                gs = rt4[:, 0, 0:nt * 4]
                link(nc.vector.tensor_reduce(gs, r4(8), AX.X, ALU.add))

                def q4(i):
                    return rt4[:, i, 0:nt * 4].rearrange("p (t g) -> p t g", g=4)

                beats(q4(0), [q4(1 + j) for j in range(4)], nt)
                link(TT(rt4[:, 5, 0:nt * 4], rt4[:, 1, 0:nt * 4], rt4[:, 2, 0:nt * 4], ALU.add))
                link(TT(rt4[:, 5, 0:nt * 4], rt4[:, 5, 0:nt * 4], rt4[:, 3, 0:nt * 4], ALU.add))
                link(TT(rt4[:, 5, 0:nt * 4], rt4[:, 5, 0:nt * 4], rt4[:, 4, 0:nt * 4], ALU.add))
                link(nc.vector.tensor_scalar(rt4[:, 6, 0:nt * 4], rt4[:, 5, 0:nt * 4], 1.0, None, ALU.is_lt))
                TT(r4(9), r4(7), rt4[:, 6, 0:nt * 4].unsqueeze(2).broadcast_to([P, nt * 4, 4]), ALU.mult)\
                    .then_inc(sel_ready, 1)
                dve.wait_ge(sel_ready, l + 1)
                link(TT(r(10), r(0), r(9), ALU.mult))
                link(nc.vector.tensor_reduce(rt1[:, 0, 0:nt], r16(10), AX.X, ALU.add))
                link(nc.vector.reciprocal(rt1[:, 1, 0:nt], rt1[:, 0, 0:nt]))
                link(TT(r16(10), r16(10), rt1[:, 1, 0:nt].unsqueeze(2).broadcast_to([P, nt, NE]), ALU.mult))
                b = take(("cnt", l))
                link(nc.vector.tensor_copy(r(11), b[:, 0:w16]))
                nc.vector.tensor_reduce(most[:, :], b[:, 64:80], AX.X, ALU.max).then_inc(dve_took, 1)
                dve.wait_ge(dve_took, took[0])
                m_over = NE * OVER_BLOCKS[l]
                link(nc.vector.scalar_tensor_tensor(out=r(12), in0=r(11), scalar=float(NE),
                                                    in1=const[:, C_EXP:C_EXP + w16], op0=ALU.mult, op1=ALU.add))
                if OVER_BLOCKS[l] > 1:
                    link(nc.vector.tensor_scalar(r(13), r(11), float(-P), 0.0, ALU.add, ALU.max))
                    link(nc.vector.scalar_tensor_tensor(out=r(12), in0=r(13), scalar=float(m_over - NE), in1=r(12),
                                                        op0=ALU.mult, op1=ALU.add))
                for blk in range(2, OVER_BLOCKS[l] + 1):
                    link(nc.vector.tensor_scalar(r(13), r(11), float(blk * P), float(NE - P * m_over), ALU.is_ge,
                                                 ALU.mult))
                    link(TT(r(12), r(12), r(13), ALU.add))
                link(nc.vector.scalar_tensor_tensor(out=r(12), in0=r(12), scalar=1.0, in1=r(9), op0=ALU.add,
                                                    op1=ALU.mult))
                link(nc.vector.tensor_reduce(rt1[:, 2, 0:nt], r16(12), AX.X, ALU.max))
                link(nc.vector.tensor_reduce(rt1[:, 3, 0:nt], r16(12), AX.X, ALU.add))
                link(TT(rt1[:, 3, 0:nt], rt1[:, 3, 0:nt], rt1[:, 2, 0:nt], ALU.subtract))
                link(TT(r16(13), r16(12), rt1[:, 2, 0:nt].unsqueeze(2).broadcast_to([P, nt, NE]), ALU.is_equal))
                link(TT(r(14), r(9), r(13), ALU.subtract))
                link(TT(r(13), r(13), r(10), ALU.mult))
                link(TT(r(14), r(14), r(10), ALU.mult))
                link(nc.vector.tensor_reduce(w_tok[:, 0, 0:nt], r16(13), AX.X, ALU.add))
                link(nc.vector.tensor_reduce(w_tok[:, 1, 0:nt], r16(14), AX.X, ALU.add))
                far = float(1 << 20)
                for i2 in range(2):
                    link(nc.vector.tensor_scalar(rt1[:, 4, 0:nt], rt1[:, 2 + i2, 0:nt], P * NE + 0.5, far, ALU.is_lt,
                                                 ALU.mult))
                    link(nc.vector.scalar_tensor_tensor(out=idx_beyond[:, i2, 0:nt], in0=rt1[:, 2 + i2, 0:nt],
                                                        scalar=float(-P * NE - 1), in1=rt1[:, 4, 0:nt], op0=ALU.add,
                                                        op1=ALU.add))
                for i2 in range(2):
                    nc.vector.tensor_scalar(idx_tok[:, i2, 0:nt], rt1[:, 2 + i2, 0:nt], -1.0, None, ALU.add)\
                        .then_inc(idx_ready, 1)

                def take_ys(e, par):
                    for n in range(2):
                        dve.wait_ge(d_mm, e * 2 + (2 * Lb + n + 1))
                        if n == 0 and not (isinstance(e, int) and e < 2):
                            dve.wait_ge(ys_stored[par], (e - par) * 8 + 8 * Lb)
                        nc.vector.tensor_copy(ys[:, par, n * CH:(n + 1) * CH], bank[n][:, :]).then_inc(ys_took, 1)

                def expert(e, par):
                    for n in range(2):
                        dve.wait_ge(silu_done, e * 2 + (2 * Lb + n + 1))
                        dve.wait_ge(gu_mm, e * 4 + (4 * Lb + 2 * n + 2))
                        if not (isinstance(e, int) and e + Lb == 0):
                            dve.wait_ge(ht_mm, e * 2 + (2 * Lb - 2 + n + 1))
                        TT(hexp[:, n, :], bank[3 + 2 * n][:, :], silu[:, n, :], ALU.mult).then_inc(h_done, 1)

                expert(0, 0)
                expert(1, 1)
                take_ys(0, 0)
                expert(2, 0)
                take_ys(1, 1)
                expert(3, 1)
                take_ys(2, 0)
                with dve.Fori(1, NE // 2 - 1) as i:
                    expert(i * 2 + 2, 0)
                    take_ys(i * 2 + 1, 1)
                    expert(i * 2 + 3, 1)
                    take_ys(i * 2 + 2, 0)
                take_ys(NE - 1, 1)
                o = over[l]
                dve.wait_ge(idx_ready, 2 * l + 2)
                busiest = dve.value_load(most[0:1, 0:1], min_val=0, max_val=512)
                with dve.If(busiest > P):
                    dve.wait_ge(ys_stored[0], 8 * (Lb + NE))
                    with dve.Fori(0, OVER_BLOCKS[l] * NE) as k:
                        dve.wait_ge(o["s"], k + 1)
                        for n in range(2):
                            t = TT(hexp[:, n, :], bank[3 + 2 * n][:, :], silu[:, n, :], ALU.mult)
                        t.then_inc(o["h"], 1)
                        dve.wait_ge(o["d"], k + 1)
                        for n in range(2):
                            t = nc.vector.tensor_copy(ys[:, 0, n * CH:(n + 1) * CH], bank[n][:, :])
                        t.then_inc(o["ys"], 1)
                dve.wait_ge(g_loaded, 16 * (2 * l + 2))
                for k, tb in enumerate(T):
                    dve.wait_ge(got_ready, T_BEFORE[l] + k + 1)
                    ga, gb = got_a[:, k % 2, :], got_b[:, k % 2, :]
                    link(nc.vector.tensor_scalar(ga, ga, w_tok[:, 0, k:k + 1], None, ALU.mult))
                    link(nc.vector.scalar_tensor_tensor(out=gb, in0=gb, scalar=w_tok[:, 1, k:k + 1], in1=ga,
                                                        op0=ALU.mult, op1=ALU.add))
                    link(TT(gb, gb, G_bc[:, tb // 2, :], ALU.mult))
                    TT(x[:, tb, :], x[:, tb, :], gb, ALU.add).then_inc(combined, 1)
                    dve.wait_ge(combined, T_BEFORE[l] + k + 1)
            inverse_rms(4, [0, 1])
            dve.wait_ge(final_loaded, 16)
            for tb in range(2):
                nc.vector.scalar_tensor_tensor(out=final_rows[:, tb, :], in0=x[:, tb, :], scalar=stat[:, 3, tb:tb + 1],
                                               in1=final_w, op0=ALU.mult, op1=ALU.mult).then_inc(final_ready, 1)

        @block.tensor
        def _(pe):
            at = [0]

            def begin(*name):
                i = at[0]
                assert order[i] == name, (order[i], name)
                if i >= 8:
                    old = order[i - 8]
                    pe.wait_ge(act_took if taker[old] == "act" else dve_took, TAKEN[old])
                at[0] += 1
                return bank[i % 8]

            def mm(o, a, b, first, last):
                return nc.tensor.matmul(o, a, b, start=first, stop=last)

            def wait_chunk(key):
                s, v = slot_at[key]
                pe.wait_ge(slot_loaded[s], v)
                return s

            def turn(dst, src, n):
                for j in range(n):
                    ins = nc.tensor.transpose(dst[:, j * P:(j + 1) * P], src[:, j * P:(j + 1) * P], ident)
                return ins

            pe.wait_ge(const_loaded, 48)
            pe.wait_ge(c_ready, 1)
            for l in range(DEPTH):
                for c in range(12):
                    s = wait_chunk(("mod", l, c))
                    w = slot(s)
                    b = begin("mod", l, c)
                    for k in range(KB):
                        ins = mm(b[0:2, :], c_act[:, k, :], w[:, k, :], k == 0, k == KB - 1)
                    ins.then_inc(mm_done, 1)

            for l in range(DEPTH):
                T = tokens_of(l)
                nt = len(T)
                Lb = NE * l

                def turn_rows(p, tbs):
                    for k, tb in enumerate(tbs):
                        pe.wait_ge(rows_ready, ROWS_AT[l, p] + k + 1)
                        for half in range(2):
                            b = begin("hT", l, p, tb, half)
                            turn(b, hrow[:, k % 2, half * 512:(half + 1) * 512], 4).then_inc(mm_done, 1)

                def project(key, tb, name, cols=CH):
                    s, _ = slot_at[key]
                    w = slot(s, cols)
                    b = begin(*name)
                    for k in range(KB):
                        ins = mm(b[:, 0:cols], hT[:, k, tb * P:(tb + 1) * P], w[:, k, :], k == 0, k == KB - 1)
                    ins.then_inc(mm_done, 1)

                turn_rows(0, range(4))
                wait_chunk(("in", l, "kv"))
                for tb in range(4):
                    pe.wait_ge(act_took, TAKEN[("hT", l, 0, tb, 1)])
                    project(("in", l, "kv"), tb, ("in", l, "kv", tb), 256)
                wait_chunk(("in", l, "q"))
                for tb in T:
                    project(("in", l, "q"), tb, ("in", l, "q", tb))
                for tb in range(4):
                    pe.wait_ge(dve_took, TAKEN[("in", l, "kv", tb)])
                    b = begin("kT", l, tb)
                    turn(b, krow[:, tb, :], 1).then_inc(mm_done, 1)
                wait_chunk(("in", l, "f"))
                for tb in T:
                    project(("in", l, "f"), tb, ("in", l, "f", tb))
                for tb in T:
                    pe.wait_ge(dve_took, TAKEN[("in", l, "q", tb)])
                    b = begin("qT", l, tb)
                    turn(b, qrow[:, tb, :], 4).then_inc(mm_done, 1)
                for c in ("v", "x1", "x2"):
                    wait_chunk(("in", l, c))
                    for tb in T:
                        project(("in", l, c), tb, ("in", l, c, tb))
                pe.wait_ge(filt_loaded, 16 * (7 + 5 * l))
                b = begin("fl", l, 1)
                mm(b[0:64, 0:SEQ], w1, feats, True, True).then_inc(mm_done, 1)
                pe.wait_ge(sin_out, 2 * l + 1)
                b = begin("fl", l, 2)
                mm(b[0:64, 0:SEQ], w2, hid[0:64, 2, :], True, True).then_inc(mm_done, 1)
                pe.wait_ge(sin_out, 2 * l + 2)
                for o in range(2):
                    for d in range(2):
                        for tt in range(2):
                            b = begin("f3", l, o, d, tt)
                            mm(b[:, :], hid[0:64, 3, tt * P:(tt + 1) * P],
                               w3[:, (2 * o + d) * HY:(2 * o + d + 1) * HY], True, True).then_inc(mm_done, 1)
                    pe.wait_ge(abs_ready, 8 * l + 4 * o + 4)
                    b = begin("fn", l, o)
                    for i in range(4):
                        ins = mm(b[:, :], ones, filt_abs[:, i // 2, i % 2, :], i == 0, i == 3)
                    ins.then_inc(mm_done, 1)
                    pe.wait_ge(pm_ready, 2 * l + o + 1)
                    for k, (blk, sign) in enumerate(((FR0, 0), (FR1, 0), (FIZ, 1), (FI1, 1), (FRN, 0))):
                        b = begin("fk", l, o, k)
                        for tt in range(2):
                            ins = mm(b[:, :], dft[:, tt, blk, :], filt_pm[:, sign, tt, :], tt == 0, tt == 1)
                        ins.then_inc(mm_done, 1)
                pe.wait_ge(four_loaded, 16 * (l + 1))
                pe.wait_ge(act_took, TAKEN[("in", l, "f", T[-1])])
                for s in range(nt // 2):
                    for g in range(5):
                        if g < 4:
                            b = begin("fp", l, s, g)
                            for tt in range(2):
                                ins = mm(b[:, :], frow[:, 2 * s + tt, g * P:(g + 1) * P],
                                         four[:, tt * 512:(tt + 1) * 512], tt == 0, tt == 1)
                            ins.then_inc(mm_done, 1)
                        if g > 0:
                            pe.wait_ge(act_took, TAKEN[("fp", l, s, g - 1)])
                            b = begin("fy", l, s, g - 1)
                            for j in range(2):
                                ins = mm(b[:, 0:SEQ], four[:, 1024 + j * P:1024 + (j + 1) * P],
                                         pq[:, (g - 1) % 2, j * SEQ:(j + 1) * SEQ], j == 0, j == 1)
                            ins.then_inc(mm_done, 1)
                heads = [(tb, h) for tb in T for h in range(NH)]
                hb = NH * T_BEFORE[l]
                pe.wait_ge(act_took, TAKEN[("qT", l, T[-1])])

                def turn_ya(k):
                    pe.wait_ge(ya_ready, T_BEFORE[l] + k + 1)
                    b = begin("yaT", l, T[k])
                    turn(b, ya[:, k % 2, :], 4).then_inc(mm_done, 1)

                for i in range(len(heads) + 3):
                    if i < len(heads):
                        tb, h = heads[i]
                        g, j = h // 4, h % 4
                        keys = slice(0, 512) if tb < 2 else slice(256, 512)
                        b = begin("sc", l, tb, h)
                        mm(b[:, 0:keys.stop - keys.start], qT[g * HD:(g + 1) * HD, j, tb * P:(tb + 1) * P],
                           kT[g * HD:(g + 1) * HD, keys], True, True).then_inc(mm_done, 1)
                    if 2 <= i < len(heads) + 2:
                        tb, h = heads[i - 2]
                        pe.wait_ge(exp_done, hb + i - 1)
                        b = begin("pt", l, tb, h)
                        turn(b, P_buf[:, i % 2, :], 4 if tb < 2 else 2).then_inc(mm_done, 1)
                    if i >= 3:
                        tb, h = heads[i - 3]
                        g = h // 4
                        kb = range(4) if tb < 2 else range(2, 4)
                        pe.wait_ge(act_took, TAKEN[("pt", l, tb, h)])
                        b = begin("pv", l, tb, h)
                        for n, k in enumerate(kb):
                            ins = mm(b[:, 0:HD], PT[:, (i - 3) % 2, n, :], vrow[:, k, g * HD:(g + 1) * HD], n == 0,
                                     n == len(kb) - 1)
                        ins.then_inc(mm_done, 1)
                        if h == NH - 1 and tb > 0:
                            turn_ya((i - 3) // NH - 1)
                turn_ya(nt - 1)
                pe.wait_ge(conv_done, 3 * (T_BEFORE[l] + nt))
                for o in range(2):
                    for s in range(nt // 2):
                        if o:
                            pe.wait_ge(y_ready, 2 * T_BEFORE[l] + 2 * (s + 1))
                        for blk in (FR0, FI0, FR1, FI1):
                            b = begin("u", l, o, s, blk)
                            for tt in range(2):
                                ins = mm(b[:, :], dft[:, tt, blk, :], z[:, 2 * s + tt, 0, :], tt == 0, tt == 1)
                            ins.then_inc(mm_done, 1)
                        pe.wait_ge(spec_ready, 2 * T_BEFORE[l] + 2 * (o * (nt // 2) + s + 1))
                        for tt in range(2):
                            b = begin("c", l, o, s, tt)
                            for k in range(4):
                                ins = mm(b[:, :], inv[:, k, tt * P:(tt + 1) * P], Yspec[:, k, :], k == 0, k == 3)
                            ins.then_inc(mm_done, 1)
                for k, tb in enumerate(T):
                    pe.wait_ge(y_ready, 2 * T_BEFORE[l] + nt + k + 1)
                    b = begin("yhT", l, tb)
                    turn(b, z[:, tb, 0, :], 4).then_inc(mm_done, 1)
                pe.wait_ge(act_took, TAKEN[("yhT", l, T[-1])])
                for br in range(3):
                    wait_chunk(("g", l, br, 0))
                    sb_ = wait_chunk(("b", l, br))
                    wb = ring[:, sb_ * SLOT:(sb_ + 1) * SLOT].rearrange("p (k n) -> p k n", k=4)
                    for n in range(2):
                        wait_chunk(("g", l, br, n))
                        for tb in T:
                            project(("g", l, br, n), tb, ("g", l, br, n, tb))
                            b = begin("b", l, br, n, tb)
                            for k in range(4):
                                ins = mm(b[:, :], branch_T[br][:, k, tb * P:(tb + 1) * P], wb[:, k, n * CH:(n + 1) * CH],
                                         k == 0, k == 3)
                            ins.then_inc(mm_done, 1)
                for k, tb in enumerate(T):
                    pe.wait_ge(merged_ready, 2 * T_BEFORE[l] + nt + k + 1)
                    for half in range(2):
                        b = begin("mT", l, tb, half)
                        turn(b, merged[:, tb, half * 512:(half + 1) * 512], 4).then_inc(mm_done, 1)
                for n in range(2):
                    wait_chunk(("o", l, n))
                    for tb in T:
                        pe.wait_ge(act_took, TAKEN[("mT", l, tb, 1)])
                        project(("o", l, n), tb, ("o", l, n, tb))
                turn_rows(1, T)
                for tb in T:
                    pe.wait_ge(act_took, TAKEN[("hT", l, 1, tb, 1)])
                    b = begin("r", l, tb)
                    for k in range(KB):
                        ins = mm(b[:, 0:NE], hT[:, k, tb * P:(tb + 1) * P], wr[:, k, :], k == 0, k == KB - 1)
                    ins.then_inc(mm_done, 1)
                pe.wait_ge(sel_ready, l + 1)
                b = begin("cnt", l)
                sel = rt[:, 9, :].rearrange("p (t e) -> p t e", e=NE)
                for k in range(nt):
                    for k2 in range(k + 1):
                        mm(b[:, k * NE:(k + 1) * NE], tri if k2 == k else ones, sel[:, k2, :], k2 == 0, k2 == k)
                for k in range(nt):
                    ins = mm(b[:, 64:64 + NE], ones, sel[:, k, :], k == 0, k == nt - 1)
                ins.then_inc(mm_done, 1)

                pe.wait_ge(act_took, TAKEN[("r", l, T[-1])])
                pe.wait_ge(dve_took, TAKEN[("cnt", l)])
                loaded = base_loads[l]

                def turn_xs(e, par):
                    if isinstance(e, int):
                        pe.wait_ge(xs_loaded[par], 8 * Lb + 16 * (e // 2 + 1))
                    else:
                        pe.wait_ge(xs_loaded[par], (e - par) * 8 + (8 * Lb + 16))
                    if not (isinstance(e, int) and e == 0):
                        pe.wait_ge(h_done, e * 2 + (2 * Lb - 1))
                    for half in range(2):
                        turn(bank[2 + half], xs[:, par, half * 512:(half + 1) * 512], 4).then_inc(xt_mm, 1)

                def gate_up(e, par):
                    pe.wait_ge(xt_took, e * 2 + (2 * Lb + 2))
                    for c in range(4):
                        pe.wait_ge(slot_loaded[c], e * 16 + 16 * (loaded[c] + 1))
                        if c >= 2 and not (isinstance(e, int) and e == 0):
                            pe.wait_ge(h_done, e * 2 + 2 * Lb)
                        for k in range(KB):
                            ins = mm(bank[2 + c][:, :], xsT[:, par, k, :], slot(c)[:, k, :], k == 0, k == KB - 1)
                        ins.then_inc(gu_mm, 1)

                def down(e, par, n):
                    pe.wait_ge(slot_loaded[4 + n], e * 16 + 16 * (loaded[4 + n] + 1))
                    pe.wait_ge(ht_took, e * 2 + (2 * Lb + 2))
                    if not (isinstance(e, int) and e == 0):
                        pe.wait_ge(ys_took, e * 2 + (2 * Lb - 2 + n + 1))
                    for k in range(KB):
                        ins = mm(bank[n][:, :], hexpT[:, par, k, :], slot(4 + n)[:, k, :], k == 0, k == KB - 1)
                    ins.then_inc(d_mm, 1)

                def turn_h(e):
                    for half in range(2):
                        pe.wait_ge(h_done, e * 2 + (2 * Lb + half + 1))
                        if not (isinstance(e, int) and e == 0):
                            pe.wait_ge(ht_took, e * 2 + (2 * Lb - 2 + half + 1))
                        turn(bank[6 + half], hexp[:, half, :], 4).then_inc(ht_mm, 1)

                turn_xs(0, 0)
                gate_up(0, 0)
                turn_h(0)
                turn_xs(1, 1)

                def expert(e, par, last=False):
                    gate_up(e, par)
                    down(e - 1, 1 - par, 0)
                    turn_h(e)
                    down(e - 1, 1 - par, 1)
                    if not last:
                        turn_xs(e + 1, 1 - par)

                expert(1, 1)
                with pe.Fori(0, NE // 2 - 2) as i:
                    expert(i * 2 + 2, 0)
                    expert(i * 2 + 3, 1)
                expert(NE - 2, 0)
                expert(NE - 1, 1, last=True)
                down(NE - 1, 1, 0)
                down(NE - 1, 1, 1)
                pe.wait_ge(ys_took, 2 * (Lb + NE))
                o = over[l]
                pe.wait_ge(idx_ready, 2 * l + 2)
                busiest = pe.value_load(most[0:1, 0:1], min_val=0, max_val=512)
                with pe.If(busiest > P):
                    with pe.Fori(0, OVER_BLOCKS[l] * NE) as k:
                        pe.wait_ge(o["xs"], k * 16 + 16)
                        for half in range(2):
                            t = turn(bank[2 + half], xs[:, 0, half * 512:(half + 1) * 512], 4)
                        t.then_inc(o["xt"], 1)
                        pe.wait_ge(o["xe"], k + 1)
                        pe.wait_ge(o["w"], k * 96 + 96)
                        for c in range(4):
                            for kk in range(KB):
                                t = mm(bank[2 + c][:, :], xsT[:, 0, kk, :], slot(c)[:, kk, :], kk == 0, kk == KB - 1)
                        t.then_inc(o["gu"], 1)
                        pe.wait_ge(o["h"], k + 1)
                        for half in range(2):
                            t = turn(bank[6 + half], hexp[:, half, :], 4)
                        t.then_inc(o["ht"], 1)
                        pe.wait_ge(o["he"], k + 1)
                        for n in range(2):
                            for kk in range(KB):
                                t = mm(bank[n][:, :], hexpT[:, 0, kk, :], slot(4 + n)[:, kk, :], kk == 0, kk == KB - 1)
                        t.then_inc(o["d"], 1)
                    pe.wait_ge(o["ys"], OVER_BLOCKS[l] * NE)


_INS = ['x', 'c', 'ctx', 'c_ctx', 'w_mod', 'b_mod', 'norm_mix', 'norm_ffn', 'w_in', 'attn_sink', 'conv_w', 'conv_b',
        'filt_w1', 'filt_b1', 'filt_freq', 'filt_w2', 'filt_b2', 'filt_w3', 'hyena_bias', 'w_branch_attn',
        'w_branch_fnet', 'w_branch_hyena', 'w_out', 'w_router', 'b_router', 'w_exp_gate', 'w_exp_up', 'w_exp_down',
        'norm_final']


def _constants():
    import math
    import numpy as np

    f32 = np.float32
    p = np.arange(128)
    const = np.zeros((128, C_END), f32)
    const[:, C_ID:C_ID + 128] = np.eye(128)
    const[:, C_TRI:C_TRI + 128] = p[:, None] < p[None, :]
    const[:, C_ONE:C_ONE + 128] = 1.0
    t = np.arange(256)
    f = np.arange(256)
    ang = 2 * np.pi * (np.outer(t, f) % 512) / 512
    cos, msin, alt = np.cos(ang), -np.sin(ang), (-1.0) ** t
    dft = np.zeros((256, 6, 128))
    dft[:, 0], dft[:, 1] = cos[:, :128], cos[:, 128:]
    dft[:, 2], dft[:, 3] = msin[:, :128], msin[:, 128:]
    dft[:, 4] = dft[:, 2]
    dft[:, 4, 0] = 0.0
    dft[:, 2, 0] = alt
    dft[:, 5] = dft[:, 0]
    dft[:, 5, 0] = alt
    const[:, C_DFT:C_INV] = dft.reshape(2, 128, 6 * 128).transpose(1, 0, 2).reshape(128, -1)
    inv = np.zeros((4, 128, 256))
    ci, si = 2 * cos.T / 512, 2 * msin.T / 512
    ci[0] /= 2
    si[0] = alt / 512
    inv[0], inv[1], inv[2], inv[3] = ci[:128], ci[128:], si[:128], si[128:]
    const[:, C_INV:C_ROPE] = inv.transpose(1, 0, 2).reshape(128, -1)
    freqs = (f32(10000.0) ** (-np.arange(16, dtype=f32) / f32(16))).astype(f32)
    rope = np.zeros((256, 4, 64))
    for half, pos in ((0, t // 64), (1, t % 64)):
        a = (pos.astype(f32)[:, None] * freqs).astype(f32).astype(np.float64)
        c = slice(32 * half, 32 * half + 32)
        rope[:, 2, c] = np.concatenate([np.cos(a), np.cos(a)], 1)
        rope[:, 3, c] = np.concatenate([-np.sin(a), np.sin(a)], 1)
    rope[:, 0:2] = rope[:, 2:4].astype(f32) * 0.125
    const[:, C_ROPE:C_MASK] = rope.reshape(2, 128, 256).transpose(1, 0, 2).reshape(128, -1)
    mask = np.zeros((256, 512))
    mask[:, :256] = np.where(np.abs(t[:, None] - t[None, :]) <= 128, 0.0, -1.0e30)
    const[:, C_MASK:C_EXP] = mask.reshape(2, 128, 512).transpose(1, 0, 2).reshape(128, -1)
    const[:, C_EXP:C_END] = np.tile(np.arange(16), 4)[None]
    an = 2 * np.pi * (np.outer(t, t) % 256) / 256
    ad = 2 * np.pi * (np.outer(p, p) % 128) / 128
    scale = 1.0 / math.sqrt(256 * 128)
    four = np.zeros((128, 1280))
    cs = np.concatenate([np.cos(an), np.sin(an)], 1)
    four[:, 0:512], four[:, 512:1024] = cs[:128], cs[128:]
    four[:, 1024:1152], four[:, 1152:1280] = np.cos(ad) * scale, -np.sin(ad) * scale
    pos = np.arange(256, dtype=f32)
    tt = pos / f32(255)
    omega = (f32(2.0 * math.pi) * pos / f32(256)).astype(f32)
    bands = np.linspace(1e-4, 15, 16, dtype=f32)
    arg = (omega[:, None] * bands).astype(f32)
    feats = np.concatenate([tt[:, None], np.cos(arg), -np.sin(arg)], -1).T
    deltas = np.abs(np.linspace(math.log(1e-2) / 1.5, math.log(1e-2) / 0.3, 512, dtype=f32))
    dec = np.exp(-tt[:, None] * deltas)
    decay = np.zeros((128, 3, 512), f32)
    decay[:, 0], decay[:, 1], decay[:, 2] = dec[:128], dec[128:], dec[:128]
    decay[0, 2] = 0.0
    tok = (np.arange(4)[None, :] * 128 + p[:, None]).astype(np.int32)
    return {"k_const": const, "k_four": four.astype(f32), "k_feats": np.ascontiguousarray(feats, f32),
            "k_decay": decay.reshape(128, -1), "k_tok": tok}


def kernel(**inputs):
    import numpy as _np
    import concourse.bacc as _bacc
    from concourse import mybir as _mybir
    from concourse.bass_utils import run_bass_kernel_spmd as _run

    nc = _bacc.Bacc("TRN2", target_bir_lowering=False, num_devices=1)
    arrays, aps = {}, {}
    for name in _INS:
        a = _np.ascontiguousarray(inputs[name])
        arrays[f"in_{name}_dram"] = a
        aps[name] = nc.dram_tensor(f"in_{name}_dram", a.shape, _mybir.dt.from_np(a.dtype), kind="ExternalInput").ap()
    for name, a in _constants().items():
        arrays[f"in_{name}_dram"] = a
        aps[name] = nc.dram_tensor(f"in_{name}_dram", a.shape, _mybir.dt.from_np(a.dtype), kind="ExternalInput").ap()
    out = nc.dram_tensor("out_0_dram", (1, SEQ, D), _mybir.dt.float32, kind="ExternalOutput").ap()
    hybrid_kernel(nc, aps, out)
    r = _run(nc, [arrays], core_ids=[0])
    return r.results[0]["out_0_dram"]
```

```python
from contextlib import ExitStack

import concourse.bass as bass
from concourse import mybir

F32 = mybir.dt.float32
F32R = mybir.dt.float32r
I32 = mybir.dt.int32
ALU = mybir.AluOpType
ACT = mybir.ActivationFunctionType
AX = mybir.AxisListType

P = 128
D = 1024
KB = D // P
SEQ = 256
DEPTH = 2
HD = 64
NH = 8
NKV = 2
NE = 16
EPS = 1e-6
HY = 512
CH = 512
SLOT = KB * CH
HALF = SLOT // 2
N_RAW, N_SPLIT = 6, 3
PER_EXPERT = 12
PER_LAYER = PER_EXPERT * NE
W_OFF = {"q": 0, "kv": 512, "f": 768, "v": 1280, "x1": 1792, "x2": 2304, "ga": 2816, "gf": 3840, "gh": 4864}
ROWS_PER_PART = 64
OVER_BLOCKS = [3, 1]
MAGIC = 12582912.0
TWO_PI = (6.28125, 0.0019350051879882812, 3.019915981956753e-07)
INV_2PI = 0.15915494309189535
PI = 3.1415925

C_ID, C_TRI, C_ONE = 0, 128, 256
C_DFT = 384
C_INV = C_DFT + 2 * 6 * P
C_ROPE = C_INV + 4 * SEQ
C_MASK = C_ROPE + 2 * 4 * HD
C_EXP = C_MASK + 2 * 512
C_END = C_EXP + 64
FR0, FR1, FI0, FI1, FIZ, FRN = range(6)


def tokens_of(l):
    return [0, 1, 2, 3] if l < DEPTH - 1 else [0, 1]


def plan_jobs(l):
    T = tokens_of(l)
    S = list(range(len(T) // 2))
    out = []

    def job(who, *name):
        out.append((name, who))

    for tb in range(4):
        for half in range(2):
            job("act", "hT", l, 0, tb, half)
    for c in ("v", "x1", "x2"):
        for tb in T:
            job("act", "in", l, c, tb)
    for tb in range(4):
        job("dve", "in", l, "kv", tb)
    for tb in T:
        job("dve", "in", l, "q", tb)
    for tb in range(4):
        job("act", "kT", l, tb)
    for tb in T:
        job("act", "in", l, "f", tb)
    for tb in T:
        job("act", "qT", l, tb)
    for s in S:
        for g in range(5):
            if g < 4:
                job("act", "fp", l, s, g)
            if g > 0:
                job("act", "fy", l, s, g - 1)
    heads = [(tb, h) for tb in T for h in range(NH)]
    for i in range(len(heads) + 3):
        if i < len(heads):
            job("dve", "sc", l, *heads[i])
        if 2 <= i < len(heads) + 2:
            job("act", "pt", l, *heads[i - 2])
        if i >= 3:
            job("dve", "pv", l, *heads[i - 3])
            if heads[i - 3][1] == NH - 1 and heads[i - 3][0] > 0:
                job("act", "yaT", l, heads[i - 3][0] - 1)
    job("act", "yaT", l, T[-1])
    for o in range(2):
        for s in S:
            for b in (FR0, FI0, FR1, FI1):
                job("dve", "u", l, o, s, b)
        for s in S:
            for tt in range(2):
                job("dve", "c", l, o, s, tt)
    for tb in T:
        job("act", "yhT", l, tb)
    for br in range(3):
        for n in range(2):
            for tb in T:
                job("act", "g", l, br, n, tb)
                job("dve", "b", l, br, n, tb)
    for tb in T:
        for half in range(2):
            job("act", "mT", l, tb, half)
    for n in range(2):
        for tb in T:
            job("dve", "o", l, n, tb)
    for tb in T:
        for half in range(2):
            job("act", "hT", l, 1, tb, half)
    for tb in T:
        job("act", "r", l, tb)
    job("dve", "cnt", l)
    return out


def filter_jobs(l, g):
    taps = [[("f3", l, o, d, tt) for d in range(2) for tt in range(2)] for o in range(2)]
    spec = [[("fk", l, o, b) for b in range(5)] for o in range(2)]
    return [[("fl", l, 1)], [("fl", l, 2)], taps[0], [("fn", l, 0)], spec[0] + taps[1], [("fn", l, 1)], spec[1]][g]


OPENING = []
for _l in range(DEPTH):
    for _c in range(12):
        OPENING.append(("mod", _l, _c))
        if 1 <= _c <= 7:
            OPENING.append(("filter", _l, _c - 1))


def hybrid_kernel(nc, A, out):
    jobs = []
    for kind, l, i in OPENING:
        jobs += [(n, "dve") for n in ([(kind, l, i)] if kind == "mod" else filter_jobs(l, i))]
    for l in range(DEPTH):
        jobs += plan_jobs(l)
    order = [n for n, _ in jobs]
    taker = dict(jobs)
    DONE = {n: i + 1 for i, n in enumerate(order)}
    TAKEN, seen = {}, {"act": 0, "dve": 0}
    for n in order:
        seen[taker[n]] += 1
        TAKEN[n] = seen[taker[n]]

    def w_in(l, name, n, cols):
        o = W_OFF[name] + n * CH
        return A["w_in"][l, :, o:o + cols].rearrange("(k p) n -> p k n", p=P)

    mix = []
    for l in range(DEPTH):
        for c in range(12):
            mix.append((("mod", l, c), A["w_mod"][l, :, c * CH:(c + 1) * CH].rearrange("(k p) n -> p k n", p=P),
                        ("mod", l, c)))
    layer_start = []
    for l in range(DEPTH):
        layer_start.append(len(mix))
        last = tokens_of(l)[-1]
        for c in ("v", "x1", "x2", "kv", "q", "f"):
            mix.append((("in", l, c), w_in(l, c, 0, 256 if c == "kv" else CH), ("in", l, c, 3 if c == "kv" else last)))
        for br, (g, wb) in enumerate((("ga", "w_branch_attn"), ("gf", "w_branch_fnet"), ("gh", "w_branch_hyena"))):
            mix.append((("g", l, br, 0), w_in(l, g, 0, CH), ("g", l, br, 0, last)))
            mix.append((("b", l, br), A[wb][l].rearrange("(k p) n -> p k n", p=P), ("b", l, br, 1, last)))
            mix.append((("g", l, br, 1), w_in(l, g, 1, CH), ("g", l, br, 1, last)))
        for n in range(2):
            mix.append((("o", l, n), A["w_out"][l, :, n * CH:(n + 1) * CH].rearrange("(k p) n -> p k n", p=P),
                        ("o", l, n, last)))
    slot_at, loads, base_loads, n_mix = {}, [0] * N_RAW, [], 0
    for l in range(DEPTH):
        until = layer_start[l + 1] if l + 1 < DEPTH else len(mix)
        for key, _, _ in mix[n_mix:until]:
            s = n_mix % 3
            loads[2 * s] += 1
            slot_at[key] = (s, 16 * loads[2 * s])
            n_mix += 1
        base_loads.append(list(loads))
        loads = [x + PER_LAYER // N_RAW for x in loads]

    ctx = ExitStack()
    with ctx:
        def sb(name, shape, dt=F32):
            return ctx.enter_context(nc.sbuf_tensor(name, shape, dt))

        def sem(name):
            return ctx.enter_context(nc.semaphore(name))

        bank = [ctx.enter_context(nc.psum_tensor(f"bank{i}", [P, 512], F32)) for i in range(8)]

        ring_at = -(-nc.sbuf_base // 32) * 32
        ring = sb("ring", [P, 6 * SLOT])
        x = sb("x", [P, 4, D])
        hT_at = -(-nc.sbuf_base // 32) * 32
        hT = sb("hT", [P, KB, 512])
        work_at = -(-nc.sbuf_base // 32) * 32
        work = sb("work", [P, 8192])
        mixed_at = -(-nc.sbuf_base // 32) * 32
        mixed = sb("mixed", [P, 7168])
        const = sb("const", [P, C_END])
        ident = const[:, C_ID:C_ID + P]
        tri = const[:, C_TRI:C_TRI + P]
        ones = const[:, C_ONE:C_ONE + P]
        dft = const[:, C_DFT:C_INV].rearrange("p (t b m) -> p t b m", t=2, b=6)
        inv = const[:, C_INV:C_ROPE].rearrange("p (b m) -> p b m", b=4)
        rope = const[:, C_ROPE:C_MASK].rearrange("p (t j d) -> p t j d", t=2, j=4)
        mask = const[:, C_MASK:C_EXP].rearrange("p (t k) -> p t k", t=2)
        expert_id = const[:, C_EXP:C_END].rearrange("p (t e) -> p t e", t=4)

        M = 3 * SLOT

        def lent(a, n):
            return ring[:, M + a:M + a + n]

        z = lent(0, 6144).rearrange("p (t c n) -> p t c n", t=4, c=3)
        filt = lent(0, 2048).rearrange("p (d t n) -> p d t n", d=2, t=2)
        filt_pm = lent(2048, 2048).rearrange("p (d t n) -> p d t n", d=2, t=2)
        filt_abs = lent(4096, 2048).rearrange("p (d t n) -> p d t n", d=2, t=2)
        merged = lent(0, 4096).rearrange("p (t n) -> p t n", t=4)
        spectra = lent(6144, 5120).rearrange("p (o b n) -> p o b n", o=2, b=5)
        hstage = lent(6144, 1024).rearrange("p (i n) -> p i n", i=2)
        gate_buf = lent(6144, 1024).rearrange("p (i n) -> p i n", i=2)
        merge_tmp = lent(7168, 512)
        out_tmp = lent(7680, 512)
        hid = lent(11264, 1024).rearrange("p (i n) -> p i n", i=4)
        pq = lent(11264, 1024).rearrange("p (i n) -> p i n", i=2)
        hy_bias = lent(11264, 1024).rearrange("p (o n) -> p o n", o=2)
        x_flat = x[:, :, :].rearrange("p t n -> p (t n)")
        w3 = x_flat[0:64, 0:2048]
        w1 = x_flat[0:33, 2048:2112]
        w2 = x_flat[0:64, 2112:2176]
        feats = x_flat[0:33, 2304:2560]
        decay = x_flat[:, 2560:4096].rearrange("p (i n) -> p i n", i=3)
        mod_rows = [work[0:2, 0:6 * D], mixed[0:2, 0:6 * D]]
        zeros = work[0:4, 6144:6144 + 3 * HY]
        rnorm = mixed[:, 6144:6656]
        norm_rows = hT[0:2, :, :].rearrange("p k n -> p (k n)").rearrange("p (l i n) -> p l i n", l=2, i=2)

        A_bc = work[:, 0:2048].rearrange("p (s n) -> p s n", s=2)
        B_bc = work[:, 2048:4096].rearrange("p (s n) -> p s n", s=2)
        G_bc = work[:, 4096:6144].rearrange("p (s n) -> p s n", s=2)
        hrow = work[:, 6144:8192].rearrange("p (i n) -> p i n", i=2)
        four = work[:, 0:1280]
        S_buf = work[:, 0:1024].rearrange("p (i n) -> p i n", i=2)
        P_buf = work[:, 1024:2048].rearrange("p (i n) -> p i n", i=2)
        PT = work[:, 2048:3072].rearrange("p (i k n) -> p i k n", i=2, k=4)
        ya = work[:, 3072:4096].rearrange("p (i n) -> p i n", i=2)
        stage = work[:, 0:3072].rearrange("p (i j n) -> p i j n", i=2, j=3)
        Yspec = work[:, 0:4096].rearrange("p (s b n) -> p s b n", s=2, b=4)
        hy_tmp = work[:, 4096:5120].rearrange("p (i n) -> p i n", i=2)
        rope_tmp = work[:, 4096:5120].rearrange("p (i n) -> p i n", i=2)
        krow = work[:, 5120:5632].rearrange("p (t n) -> p t n", t=4)
        conv_w = mixed[:, 5120:7168].rearrange("p (j n) -> p j n", j=4)
        qrow = work[:, 6144:8192].rearrange("p (t n) -> p t n", t=4)
        got_a = lent(0, 4096).rearrange("p (i n) -> p i n", i=4)
        got_b = lent(4096, 4096).rearrange("p (i n) -> p i n", i=4)

        qT = mixed[:, 0:2048].rearrange("p (j n) -> p j n", j=4)
        yhT = mixed[:, 0:2048].rearrange("p (j n) -> p j n", j=4)
        kT = mixed[:, 2048:2560]
        vrow = mixed[:, 2560:3072].rearrange("p (t n) -> p t n", t=4)
        yaT = mixed[:, 3072:5120].rearrange("p (j n) -> p j n", j=4)
        frow = mixed[:, 3072:5120].rearrange("p (t n) -> p t n", t=4)
        yfT = mixed[:, 5120:7168].rearrange("p (j n) -> p j n", j=4)
        branch_T = [yaT, yfT, yhT]
        xs = mixed[:, 0:2048].rearrange("p (i n) -> p i n", i=2)
        silu = mixed[:, 4096:5120].rearrange("p (i n) -> p i n", i=2)
        hexp = mixed[:, 5120:6144].rearrange("p (i n) -> p i n", i=2)
        hT_flat = hT[:, :, :].rearrange("p k n -> p (k n)")
        ys = work[:, 2048:4096].rearrange("p (i n) -> p i n", i=2)
        over_xT = work[:, 0:1024].rearrange("p (k n) -> p k n", k=KB)
        over_hT = hT_flat[:, 0:1024].rearrange("p (k n) -> p k n", k=KB)

        def parts(name, shape, at):
            return nc.alloc_sbuf_tensor_at(name, shape, F32R, offset=at)

        w_hi = parts("w_hi", [P, N_SPLIT, 4, CH], ring_at + 4 * M)
        w_lo = parts("w_lo", [P, N_SPLIT, 4, CH], ring_at + 4 * (M + N_SPLIT * HALF))
        hexpT_hi = parts("hexpT_hi", [P, 2, KB, P], hT_at)
        hexpT_lo = parts("hexpT_lo", [P, 2, KB, P], hT_at + 4 * 2048)
        xsT_hi = parts("xsT_hi", [P, 2, KB, P], mixed_at + 4 * 2048)
        xsT_lo = parts("xsT_lo", [P, 2, KB, P], work_at)
        final_w = mixed[:, 2048:3072]
        final_rows = mixed[:, 0:2048].rearrange("p (i n) -> p i n", i=2)

        c_raw = sb("c_raw", [P, KB, 2])
        c_act = sb("c_act", [P, KB, 2])
        wr = sb("wr", [P, KB, NE])
        br_bc = sb("br_bc", [P, NE])
        sink = sb("sink", [P, DEPTH, NH])
        fcol = sb("fcol", [64, DEPTH, 3])
        stat = sb("stat", [P, 5, 4])
        att = sb("att", [P, 2, 6, NH])
        rt = mixed[:, 6144:7168].rearrange("p (i n) -> p i n", i=16)
        rt4 = sb("rt4", [P, 8, 16])
        rt1 = sb("rt1", [P, 8, 4])
        w_tok = sb("w_tok", [P, 2, 4])
        idx_tok = sb("idx_tok", [P, 2, 4], I32)
        tok_id = sb("tok_id", [P, 4], I32)
        idx_exp = sb("idx_exp", [P, NE], I32)
        idx_over = sb("idx_over", [P, 1], I32)
        zero_i = work[:, 7680:7680 + ROWS_PER_PART].bitcast(I32)
        most = sb("most", [P, 1], I32)
        pace = c_raw[:, 0, :]
        idx_beyond = c_act[:, 0:4, :].rearrange("p k s -> p (k s)").rearrange("p (i t) -> p i t", i=2).bitcast(I32)
        spec_dram = nc.dram_tensor("spec_dram", (DEPTH, P, 2 * 5 * HY), F32, kind="Internal").ap()
        mod_dram = nc.dram_tensor("mod_dram", (DEPTH, 2, 6, D), F32, kind="Internal").ap()
        hp_dram = nc.dram_tensor("hp_dram", (DEPTH * 2, SEQ + 2, 3 * HY), F32, kind="Internal").ap()
        ys_dram = nc.dram_tensor("ys_dram", (P * NE, D), F32, kind="Internal").ap()
        ys_over = [nc.dram_tensor(f"ys_over{l}", (P * NE * OVER_BLOCKS[l], D), F32, kind="Internal").ap()
                   for l in range(DEPTH)]
        h2_of = [nc.dram_tensor(f"h2_dram{l}", (P * len(tokens_of(l)), D), F32, kind="Internal").ap() for l in range(DEPTH)]
        row_tok_of = [nc.dram_tensor(f"row_tok{l}", (P * ROWS_PER_PART, 1), I32, kind="Internal").ap()
                      for l in range(DEPTH)]

        slot_loaded = [sem(f"slot_loaded{i}") for i in range(6)]
        const_loaded = sem("const_loaded")
        small_loaded = sem("small_loaded")
        c_ready = sem("c_ready")
        mm_done = sem("mm_done")
        act_took = sem("act_took")
        dve_took = sem("dve_took")
        dve_step = sem("dve_step")
        act_step = sem("act_step")
        mod_stored = sem("mod_stored")
        zero_ready = sem("zero_ready")
        zero_stored = sem("zero_stored")
        ab_loaded = sem("ab_loaded")
        g_loaded = sem("g_loaded")
        var_ready = sem("var_ready")
        root_ready = sem("root_ready")
        rows_ready = sem("rows_ready")
        filt_loaded = sem("filt_loaded")
        four_loaded = sem("four_loaded")
        bias_loaded = sem("bias_loaded")
        sin_in = sem("sin_in")
        spec_stored = sem("spec_stored")
        spec_loaded = sem("spec_loaded")
        x_loaded = sem("x_loaded")
        sin_out = sem("sin_out")
        abs_ready = sem("abs_ready")
        pm_ready = sem("pm_ready")
        hp_stored = [sem(f"hp_stored{i}") for i in range(2)]
        max_ready = sem("max_ready")
        exp_done = sem("exp_done")
        sink_in = sem("sink_in")
        sink_exp = sem("sink_exp")
        ya_ready = sem("ya_ready")
        convw_loaded = sem("convw_loaded")
        stage_loaded = [sem(f"stage_loaded{i}") for i in range(2)]
        conv_done = sem("conv_done")
        spec_ready = sem("spec_ready")
        y_ready = sem("y_ready")
        merged_ready = sem("merged_ready")
        h2_stored = [sem(f"h2_stored{i}") for i in range(2)]
        sel_ready = sem("sel_ready")
        idx_ready = sem("idx_ready")
        scattered = sem("scattered")
        idx_loaded = sem("idx_loaded")
        xs_loaded = [sem(f"xs_loaded{i}") for i in range(2)]
        xt_mm = sem("xt_mm")
        xt_hi = sem("xt_hi")
        xt_lo = sem("xt_lo")
        hi_done = sem("hi_done")
        lo_done = sem("lo_done")
        w_used = sem("w_used")
        silu_done = sem("silu_done")
        h_done = sem("h_done")
        ht_mm = sem("ht_mm")
        ht_hi = sem("ht_hi")
        ht_lo = sem("ht_lo")
        ys_took = sem("ys_took")
        ys_stored = [sem(f"ys_stored{i}") for i in range(2)]
        got_loaded = [sem(f"got_loaded{i}") for i in range(4)]
        got_ready = sem("got_ready")
        combined = sem("combined")
        final_loaded = sem("final_loaded")
        final_ready = sem("final_ready")
        out_stored = sem("out_stored")
        over = [{n: sem(f"over{l}_{n}") for n in ("w", "idx", "xs", "xt", "xe", "gu", "s", "h", "ht", "he", "d", "ys",
                                                  "st", "got", "pace")} for l in range(DEPTH)]

        ctx.enter_context(nc.allow_non_contiguous_dma(reason="small vectors laid along the partitions"))
        block = ctx.enter_context(nc.Block())

        T_BEFORE = [0, 4]
        ROWS_AT = {(0, 0): 0, (0, 1): 4, (1, 0): 8, (1, 1): 12}
        N_SMALL = 16 * 11

        def expert_w(l, name, e, n, rows=slice(0, D)):
            w = A[name]
            if isinstance(e, int):
                return w[l, e, rows, n * CH:(n + 1) * CH].rearrange("(k p) n -> p k n", p=P)
            return w[l, bass.ds(e, 1), rows, n * CH:(n + 1) * CH].rearrange("o (k p) n -> p (o k) n", p=P)

        def slot(s, cols=CH):
            return ring[:, s * SLOT:s * SLOT + KB * cols].rearrange("p (k n) -> p k n", k=KB)

        def raw(i):
            return ring[:, i * HALF:(i + 1) * HALF].rearrange("p (k n) -> p k n", k=4)

        EXPERT_CHUNKS = (("w_exp_gate", 0), ("w_exp_up", 0), ("w_exp_gate", 1), ("w_exp_up", 1),
                         ("w_exp_down", 0), ("w_exp_down", 1))

        def ready_at(e, p):
            if isinstance(e, int):
                p = p - 8 if e == NE else p
                return (PER_EXPERT * e - 4 if e else 0) + p + 1
            return e * PER_EXPERT + (p - 3)

        def position(e, p):
            if isinstance(e, int) and e == 0:
                return p
            return (p + 2 - (8 if isinstance(e, int) and e == NE else 0)) % N_RAW

        def turns(e):
            return 8 if isinstance(e, int) and e == 0 else PER_EXPERT

        @block.sync
        def _(sp):
            sp.dma_start(const[:, :], A["k_const"]).then_inc(const_loaded, 16)
            owner = [None] * 3

            def wait_slot(s):
                if owner[s] is not None:
                    sp.wait_ge(owner[s][0], owner[s][1])

            def conv_loads(l, c):
                T = tokens_of(l)
                i = 3 * T_BEFORE[l] + c * len(T)
                for b in range(2):
                    sp.wait_ge(hp_stored[b], 16 * (i + len(T)) // 2)
                if c > 0:
                    sp.wait_ge(conv_done, i)
                sp.dma_start(conv_w[:, 0:3, :], A["conv_w"][l, :, c * HY:(c + 1) * HY].partition_broadcast(P))\
                    .then_inc(convw_loaded, 16)
                sp.dma_start(conv_w[:, 3, :], A["conv_b"][l, c * HY:(c + 1) * HY].partition_broadcast(P))\
                    .then_inc(convw_loaded, 16)
                for tb in T:
                    if i >= 2:
                        sp.wait_ge(conv_done, i - 1)
                    for j in range(3):
                        r = (tb % 2) * P + j
                        sp.dma_start(stage[:, i % 2, j, :], hp_dram[2 * l + tb // 2, r:r + P, c * HY:(c + 1) * HY])\
                            .then_inc(stage_loaded[i % 2], 16)
                    i += 1

            n = 0
            for l in range(DEPTH):
                until = layer_start[l + 1] if l + 1 < DEPTH else len(mix)
                while n < until:
                    key, src, last = mix[n]
                    s = n % 3
                    wait_slot(s)
                    if key[0] == "b":
                        dst = ring[:, s * SLOT:(s + 1) * SLOT].rearrange("p (k n) -> p k n", k=4)
                    else:
                        dst = slot(s, src.shape[-1])
                    sp.dma_start(dst, src).then_inc(slot_loaded[2 * s], 16)
                    owner[s] = (mm_done, DONE[last])
                    n += 1
                    if key[0] == "in" and key[2] in ("kv", "q", "f"):
                        conv_loads(key[1], ("kv", "q", "f").index(key[2]))
                def load(e, p):
                    name, half = EXPERT_CHUNKS[p // 2]
                    i = position(e, p) % N_RAW
                    if isinstance(e, int) and e == 0 and p < N_RAW:
                        wait_slot(i // 2)
                    else:
                        sp.wait_ge(lo_done, ready_at(e, p) + (l * PER_LAYER - N_RAW))
                    rows = slice(p % 2 * 512, p % 2 * 512 + 512)
                    sp.dma_start(raw(i), expert_w(l, name, e if p < 8 else e - 1, half, rows)).then_inc(slot_loaded[i], 16)

                def turn(e):
                    for p in range(turns(e)):
                        load(e, p)

                turn(0)
                turn(1)
                with sp.Fori(2, NE) as e:
                    turn(e)
                for p in range(8, PER_EXPERT):
                    load(NE, p)
                for s in range(3):
                    owner[s] = (lo_done, (l + 1) * PER_LAYER - N_RAW + 2 * s + 2)
                o = over[l]
                sp.wait_ge(idx_ready, 2 * l + 2)
                busiest = sp.value_load(most[0:1, 0:1], min_val=0, max_val=512)
                with sp.If(busiest > P):
                    sp.wait_ge(w_used, (l + 1) * PER_LAYER)

                    def load_all(e, done):
                        if done is not None:
                            sp.wait_ge(o["d"], done)
                        for c, (name, half) in enumerate(EXPERT_CHUNKS):
                            sp.dma_start(slot(c), expert_w(l, name, e, half)).then_inc(o["w"], 16)

                    load_all(0, None)
                    with sp.Fori(1, NE) as e:
                        load_all(e, e)
                    if OVER_BLOCKS[l] > 1:
                        with sp.Fori(1, OVER_BLOCKS[l]) as b:
                            with sp.Fori(0, NE) as e:
                                load_all(e, b * NE + e)
                    sp.wait_ge(o["d"], NE * OVER_BLOCKS[l])
            sp.wait_ge(final_ready, 1)
            sp.dma_start(out[0, 0:P, :], final_rows[:, 0, :]).then_inc(out_stored, 16)
            sp.wait_ge(final_ready, 2)
            sp.dma_start(out[0, P:2 * P, :], final_rows[:, 1, :]).then_inc(out_stored, 16)
            sp.wait_ge(out_stored, 32)

        @block.gpsimd
        def _(pool):
            small = [
                (c_raw[:, :, 0], A["c"].rearrange("o (k p) -> p (o k)", p=P)),
                (c_raw[:, :, 1], A["c_ctx"].rearrange("(k p) -> p k", p=P)),
                (mod_rows[0], A["b_mod"][0].partition_broadcast(2)),
                (mod_rows[1], A["b_mod"][1].partition_broadcast(2)),
                (norm_rows[:, :, 0, :], A["norm_mix"].partition_broadcast(2)),
                (norm_rows[:, :, 1, :], A["norm_ffn"].partition_broadcast(2)),
                (wr[:, :, :], A["w_router"].rearrange("(k p) e -> p k e", p=P)),
                (br_bc[:, :], A["b_router"].partition_broadcast(P)),
                (sink[:, :, :], A["attn_sink"].partition_broadcast(P)),
                (tok_id[:, :], A["k_tok"]),
                (fcol[:, :, 0], A["filt_b1"].rearrange("l h -> h l")),
            ]
            for dst, src in small:
                pool.dma_start(dst, src).then_inc(small_loaded, 16)
            pool.dma_start(fcol[:, :, 1], A["filt_freq"].rearrange("l h -> h l")).then_inc(filt_loaded, 16)
            pool.dma_start(fcol[:, :, 2], A["filt_b2"].rearrange("l h -> h l")).then_inc(filt_loaded, 16)
            pool.memset(zeros, 0.0).then_inc(zero_ready, 1)
            pool.memset(zero_i, 0).then_inc(zero_ready, 1)
            pool.wait_ge(zero_ready, 2)
            for r in (0, SEQ + 1):
                pool.dma_start(hp_dram[:, r, :], zeros).then_inc(zero_stored, 16)
            for l in range(DEPTH):
                pool.dma_start(row_tok_of[l].rearrange("(p m) o -> p (m o)", p=P), zero_i).then_inc(zero_stored, 16)
            pool.wait_ge(zero_stored, 16 * 4)
            for l in range(DEPTH):
                if l > 0:
                    pool.wait_ge(dve_took, TAKEN[("f3", l - 1, 1, 1, 1)])
                for dst, src in ((w1, A["filt_w1"][l]), (w2, A["filt_w2"][l]), (w3, A["filt_w3"][l]),
                                 (feats, A["k_feats"]), (decay, A["k_decay"].rearrange("p (i n) -> p i n", i=3))):
                    pool.dma_start(dst, src).then_inc(filt_loaded, 16)
                for o in range(2):
                    pool.wait_ge(dve_took, TAKEN[("fk", l, o, 4)])
                    pool.dma_start(spec_dram[l, :, o * 5 * HY:(o + 1) * 5 * HY],
                                   spectra[:, o, :, :].rearrange("p b n -> p (b n)")).then_inc(spec_stored, 16)
                pool.wait_ge(dve_took, TAKEN[("mod", l, 11)])
                pool.dma_start(mod_dram[l].rearrange("s j n -> s (j n)"), mod_rows[l]).then_inc(mod_stored, 16)
                pool.wait_ge(mod_stored, 16 * (l + 1))
            pool.dma_start(x[:, 0:2, :], A["x"][0].rearrange("(t p) n -> p t n", p=P)).then_inc(x_loaded, 16)
            pool.dma_start(x[:, 2:4, :], A["ctx"][0].rearrange("(t p) n -> p t n", p=P)).then_inc(x_loaded, 16)

            def rows_of(l, j):
                return mod_dram[l, :, j, :].partition_broadcast(P)

            for l in range(DEPTH):
                T = tokens_of(l)
                Lb = NE * l
                pool.dma_start(B_bc, rows_of(l, 0)).then_inc(ab_loaded, 16)
                pool.dma_start(A_bc, rows_of(l, 1)).then_inc(ab_loaded, 16)
                pool.wait_ge(conv_done, 3 * (T_BEFORE[l] + len(T)))
                pool.dma_start(four, A["k_four"]).then_inc(four_loaded, 16)
                pool.dma_start(spectra.rearrange("p o b n -> p (o b n)"), spec_dram[l]).then_inc(spec_loaded, 16)
                pool.wait_ge(mm_done, DONE[("fy", l, len(T) // 2 - 1, 3)])
                pool.dma_start(hy_bias, A["hyena_bias"][l].partition_broadcast(P)).then_inc(bias_loaded, 16)
                pool.wait_ge(y_ready, 2 * (T_BEFORE[l] + len(T)))
                pool.dma_start(G_bc, rows_of(l, 2)).then_inc(g_loaded, 16)
                pool.wait_ge(mm_done, DONE[("c", l, 1, len(T) // 2 - 1, 1)])
                pool.dma_start(B_bc, rows_of(l, 3)).then_inc(ab_loaded, 16)
                pool.dma_start(A_bc, rows_of(l, 4)).then_inc(ab_loaded, 16)
                pool.wait_ge(dve_took, TAKEN[("o", l, 1, T[-1])])
                pool.dma_start(G_bc, rows_of(l, 5)).then_inc(g_loaded, 16)
                for k, tb in enumerate(T):
                    pool.wait_ge(rows_ready, ROWS_AT[l, 1] + k + 1)
                    pool.dma_start(h2_of[l][tb * P:(tb + 1) * P, :], hrow[:, k % 2, :]).then_inc(h2_stored[k % 2], 16)
                pool.wait_ge(idx_ready, 2 * l + 2)
                for tb in T:
                    for i2 in range(2):
                        pool.indirect_dma_start(row_tok_of[l][:, :], bass.IndirectOffsetOnAxis(ap=idx_tok[:, i2, tb:tb + 1], axis=0),
                                                tok_id[:, tb:tb + 1], None).then_inc(scattered, 16)
                pool.wait_ge(scattered, 16 * 2 * (T_BEFORE[l] + len(T)))
                m_over = NE * OVER_BLOCKS[l]
                first_rows = row_tok_of[l][0:P * NE, :].rearrange("(p m) o -> p (m o)", p=P)
                over_rows = row_tok_of[l][P * NE:P * (NE + m_over), :].rearrange("(p m) o -> p (m o)", p=P)
                pool.dma_start(idx_exp[:, :], first_rows).then_inc(idx_loaded, 16)
                pool.wait_ge(idx_loaded, 16 * (l + 1))
                for b in range(2):
                    pool.wait_ge(h2_stored[b], 16 * (T_BEFORE[l] + len(T)) // 2)
                ys_rows = ys_dram.rearrange("(p m) n -> p m n", p=P)
                ys_beyond = ys_over[l].rearrange("(p m) n -> p m n", p=P)
                for e in range(NE + 2):
                    if e < NE:
                        if e >= 2:
                            pool.wait_ge(xt_mm, 2 * (Lb + e - 1))
                        pool.indirect_dma_start(xs[:, e % 2, :], None, h2_of[l][:, :],
                                                bass.IndirectOffsetOnAxis(ap=idx_exp[:, e:e + 1], axis=0))\
                            .then_inc(xs_loaded[e % 2], 16)
                    if e >= 2:
                        pool.wait_ge(ys_took, 2 * (Lb + e - 1))
                        pool.dma_start(ys_rows[:, e - 2, :], ys[:, e % 2, :]).then_inc(ys_stored[e % 2], 16)
                for b in range(2):
                    pool.wait_ge(ys_stored[b], 8 * (Lb + NE))
                o = over[l]
                busiest = pool.value_load(most[0:1, 0:1], min_val=0, max_val=512)
                with pool.If(busiest > P):
                    nc.gpsimd.tensor_tensor(pace, pace, pace, ALU.subtract).then_inc(o["pace"], 1)
                    with pool.Fori(0, OVER_BLOCKS[l]) as b:
                        with pool.Fori(0, NE) as e:
                            k = pool.snap(b * NE + e)
                            pool.dma_start(idx_over[:, :], over_rows[:, bass.ds(k, 1)]).then_inc(o["idx"], 16)
                            pool.wait_ge(o["idx"], k * 16 + 16)
                            pool.wait_ge(o["pace"], k * 2 + 1)
                            nc.gpsimd.tensor_tensor(pace, pace, pace, ALU.subtract).then_inc(o["pace"], 1)
                            pool.indirect_dma_start(xs[:, 0, :], None, h2_of[l][:, :],
                                                    bass.IndirectOffsetOnAxis(ap=idx_over[:, 0:1], axis=0))\
                                .then_inc(o["xs"], 16)
                            pool.wait_ge(o["ys"], k + 1)
                            pool.wait_ge(o["pace"], k * 2 + 2)
                            nc.gpsimd.tensor_tensor(pace, pace, pace, ALU.subtract).then_inc(o["pace"], 1)
                            pool.dma_start(ys_beyond[:, bass.ds(k, 1), :].rearrange("p o n -> p (o n)"), ys[:, 0, :])\
                                .then_inc(o["st"], 16)
                            pool.wait_ge(o["st"], k * 16 + 16)
                    pool.wait_ge(o["pace"], 2 * m_over + 1)
                for k, tb in enumerate(T):
                    for i2, got in ((0, got_a), (1, got_b)):
                        pool.indirect_dma_start(got[:, k, :], None, ys_dram[:, :],
                                                bass.IndirectOffsetOnAxis(ap=idx_tok[:, i2, tb:tb + 1], axis=0),
                                                bounds_check=P * NE - 1, oob_is_err=False).then_inc(got_loaded[k], 16)
                with pool.If(busiest > P):
                    for k, tb in enumerate(T):
                        pool.wait_ge(got_loaded[k], 32 * (l + 1))
                        for i2, got in ((0, got_a), (1, got_b)):
                            pool.indirect_dma_start(got[:, k, :], None, ys_over[l][:, :],
                                                    bass.IndirectOffsetOnAxis(ap=idx_beyond[:, i2, tb:tb + 1], axis=0),
                                                    bounds_check=P * m_over - 1, oob_is_err=False).then_inc(o["got"], 16)
                    pool.wait_ge(o["got"], 32 * len(T))
                nc.gpsimd.tensor_tensor(pace, pace, pace, ALU.subtract).then_inc(got_ready, 1)
                pool.wait_ge(got_ready, l + 1)
            pool.dma_start(final_w, A["norm_final"].partition_broadcast(P)).then_inc(final_loaded, 16)
            pool.wait_ge(final_loaded, 16)

        @block.scalar
        def _(act):
            took = [0]

            def take(name):
                assert taker[name] == "act" and TAKEN[name] == took[0] + 1, name
                took[0] += 1
                act.wait_ge(mm_done, DONE[name])
                return bank[(DONE[name] - 1) % 8]

            act.wait_ge(small_loaded, N_SMALL)
            nc.scalar.activation(c_act[:, :, :], c_raw[:, :, :], ACT.Silu).then_inc(c_ready, 1)

            for l in range(DEPTH):
                for n in range(2):
                    act.wait_ge(sin_in, 2 * l + n + 1)
                    nc.scalar.activation(hid[0:64, 2 + n, :], hid[0:64, 0, :], ACT.Sin).then_inc(sin_out, 1)
                for o in range(2):
                    if o:
                        act.wait_ge(mm_done, DONE[("fn", l, 0)])
                    for d in range(2):
                        for tt in range(2):
                            act.wait_ge(dve_took, TAKEN[("f3", l, o, d, tt)])
                            nc.scalar.activation(filt_abs[:, d, tt, :], filt[:, d, tt, :], ACT.Abs).then_inc(abs_ready, 1)

            def root(ph, nt):
                act.wait_ge(var_ready, ph + 1)
                nc.scalar.activation(stat[:, 2, 0:nt], stat[:, 1, 0:nt], ACT.Sqrt).then_inc(root_ready, 1)

            def transposed(l, ph, tbs):
                for tb in tbs:
                    for half in range(2):
                        b = take(("hT", l, ph, tb, half))
                        nc.scalar.activation(hT[:, 4 * half:4 * half + 4, tb * P:(tb + 1) * P],
                                             b[:, :].rearrange("p (k n) -> p k n", k=4), ACT.Copy)\
                            .then_inc(act_took, 1)

            for l in range(DEPTH):
                T = tokens_of(l)
                Lb = NE * l
                root(2 * l, 4)
                transposed(l, 0, range(4))
                i = 3 * T_BEFORE[l]
                for c, name in enumerate(("v", "x1", "x2")):
                    for tb in T:
                        b = take(("in", l, name, tb))
                        if i >= 2:
                            act.wait_ge(hp_stored[i % 2], 16 * (i // 2))
                        nc.scalar.activation(hstage[:, i % 2, :], b[:, :], ACT.Copy).then_inc(act_took, 1)
                        act.wait_ge(act_took, took[0])
                        r = 1 + (tb % 2) * P
                        act.dma_start(hp_dram[2 * l + tb // 2, r:r + P, c * HY:(c + 1) * HY], hstage[:, i % 2, :])\
                            .then_inc(hp_stored[i % 2], 16)
                        i += 1
                for tb in range(4):
                    b = take(("kT", l, tb))
                    nc.scalar.activation(kT[:, tb * P:(tb + 1) * P], b[:, 0:P], ACT.Copy).then_inc(act_took, 1)
                for tb in T:
                    b = take(("in", l, "f", tb))
                    nc.scalar.activation(frow[:, tb, :], b[:, :], ACT.Copy).then_inc(act_took, 1)
                for tb in T:
                    b = take(("qT", l, tb))
                    nc.scalar.activation(qT[:, :, tb * P:(tb + 1) * P], b[:, :].rearrange("p (j n) -> p j n", j=4),
                                         ACT.Copy).then_inc(act_took, 1)
                for s in range(len(T) // 2):
                    for g in range(5):
                        if g < 4:
                            b = take(("fp", l, s, g))
                            nc.scalar.activation(pq[:, g % 2, :], b[:, :], ACT.Copy).then_inc(act_took, 1)
                        if g > 0:
                            b = take(("fy", l, s, g - 1))
                            nc.scalar.activation(yfT[:, g - 1, s * SEQ:(s + 1) * SEQ], b[:, 0:SEQ], ACT.Copy)\
                                .then_inc(act_took, 1)
                heads = [(tb, h) for tb in T for h in range(NH)]
                hb = 8 * T_BEFORE[l]
                for i in range(len(heads) + 3):
                    if i < len(heads):
                        tb, h = heads[i]
                        nk = 512 if tb < 2 else 256
                        act.wait_ge(max_ready, hb + i + 1)
                        if i >= 2:
                            act.wait_ge(mm_done, DONE[("pt", l, *heads[i - 2])])
                        k = i // NH
                        if h == 0 and k >= 2:
                            act.wait_ge(ya_ready, T_BEFORE[l] + k - 1)
                        nc.scalar.activation(P_buf[:, i % 2, 0:nk], S_buf[:, i % 2, 0:nk], ACT.Exp,
                                             bias=att[:, k % 2, 1, h:h + 1], accum_out=att[:, k % 2, 2, h:h + 1]).then_inc(exp_done, 1)
                        if h == NH - 1:
                            act.wait_ge(sink_in, T_BEFORE[l] + i // NH + 1)
                            nc.scalar.activation(att[:, k % 2, 4, :], att[:, k % 2, 3, :], ACT.Exp).then_inc(sink_exp, 1)
                    if 2 <= i < len(heads) + 2:
                        tb, h = heads[i - 2]
                        nk = 4 if tb < 2 else 2
                        b = take(("pt", l, tb, h))
                        nc.scalar.activation(PT[:, i % 2, 0:nk, :], b[:, 0:nk * P].rearrange("p (k n) -> p k n", k=nk),
                                             ACT.Copy).then_inc(act_took, 1)
                    if i >= 3 and heads[i - 3][1] == NH - 1 and heads[i - 3][0] > 0:
                        tb = heads[i - 3][0] - 1
                        b = take(("yaT", l, tb))
                        nc.scalar.activation(yaT[:, :, tb * P:(tb + 1) * P], b[:, :].rearrange("p (j n) -> p j n", j=4),
                                             ACT.Copy).then_inc(act_took, 1)
                b = take(("yaT", l, T[-1]))
                nc.scalar.activation(yaT[:, :, T[-1] * P:(T[-1] + 1) * P], b[:, :].rearrange("p (j n) -> p j n", j=4),
                                     ACT.Copy).then_inc(act_took, 1)
                for tb in T:
                    b = take(("yhT", l, tb))
                    nc.scalar.activation(yhT[:, :, tb * P:(tb + 1) * P], b[:, :].rearrange("p (j n) -> p j n", j=4),
                                         ACT.Copy).then_inc(act_took, 1)
                seq = [(br, n, tb) for br in range(3) for n in range(2) for tb in T]
                for i, key in enumerate(seq):
                    b = take(("g", l, *key))
                    if i >= 2:
                        act.wait_ge(dve_took, TAKEN[("b", l, *seq[i - 2])])
                    nc.scalar.activation(gate_buf[:, i % 2, :], b[:, :], ACT.Sigmoid).then_inc(act_took, 1)
                for tb in T:
                    for half in range(2):
                        b = take(("mT", l, tb, half))
                        nc.scalar.activation(hT[:, 4 * half:4 * half + 4, tb * P:(tb + 1) * P],
                                             b[:, :].rearrange("p (k n) -> p k n", k=4), ACT.Copy)\
                            .then_inc(act_took, 1)
                root(2 * l + 1, len(T))
                transposed(l, 1, T)
                for tb in T:
                    b = take(("r", l, tb))
                    nc.scalar.activation(rt[:, 0, tb * NE:(tb + 1) * NE], b[:, 0:NE], ACT.Sigmoid).then_inc(act_took, 1)

                loaded = base_loads[l]
                Wb = l * PER_LAYER

                def high(e, p):
                    pos = position(e, p)
                    i = pos % N_RAW
                    if isinstance(e, int):
                        n = ready_at(e, p) - 1
                        act.wait_ge(slot_loaded[i], 16 * (loaded[i] + n // N_RAW + 1))
                    else:
                        act.wait_ge(slot_loaded[i], e * 32 + 16 * (loaded[i] + (p - 4 - i) // N_RAW + 1))
                    if isinstance(e, int) and ready_at(e, p) <= N_SPLIT:
                        act.wait_ge(dve_took, TAKEN[("o", l, 1, T[-1])])
                    else:
                        act.wait_ge(w_used, ready_at(e, p) + (Wb - N_SPLIT))
                    nc.scalar.activation(w_hi[:, pos % N_SPLIT, :, :], raw(i), ACT.Copy).then_inc(hi_done, 1)

                def take_xs(e, par):
                    for half in range(2):
                        act.wait_ge(xt_mm, e * 2 + (2 * Lb + half + 1))
                        nc.scalar.activation(xsT_hi[:, par, 4 * half:4 * half + 4, :],
                                             bank[2 + half][:, :].rearrange("p (k n) -> p k n", k=4), ACT.Copy)\
                            .then_inc(xt_hi, 1)

                def gate(e, n):
                    act.wait_ge(w_used, ready_at(e, 4 * n + 1) + Wb)
                    if not (isinstance(e, int) and e + Lb == 0):
                        act.wait_ge(h_done, e * 2 + (2 * Lb - 2 + n + 1))
                    nc.scalar.activation(silu[:, n, :], bank[2 + 2 * n][:, :], ACT.Silu).then_inc(silu_done, 1)

                def expert(e, par):
                    for p in range(turns(e)):
                        if p + 2 < turns(e):
                            high(e, p + 2)
                        else:
                            high_next(e, p + 2 - turns(e))
                        if p in (2, 6):
                            gate(e, p // 4)
                        if p == min(9, turns(e) - 1):
                            for half in range(2):
                                act.wait_ge(ht_mm, e * 2 + (2 * Lb + half + 1))
                                nc.scalar.activation(hexpT_hi[:, par, 4 * half:4 * half + 4, :],
                                                     bank[6 + half][:, :].rearrange("p (k n) -> p k n", k=4), ACT.Copy)\
                                    .then_inc(ht_hi, 1)
                            if not (isinstance(e, int) and e == NE - 1):
                                take_xs(e + 1, 1 - par)

                def high_next(e, p):
                    if isinstance(e, int) and e == NE - 1:
                        high(NE, 8 + p)
                    else:
                        high(e + 1, p)

                take_xs(0, 0)
                high(0, 0)
                high(0, 1)
                expert(0, 0)
                expert(1, 1)
                with act.Fori(1, NE // 2 - 1) as i:
                    expert(i * 2, 0)
                    expert(i * 2 + 1, 1)
                expert(NE - 2, 0)
                expert(NE - 1, 1)
                high(NE, 10)
                high(NE, 11)
                o = over[l]
                act.wait_ge(idx_ready, 2 * l + 2)
                busiest = act.value_load(most[0:1, 0:1], min_val=0, max_val=512)
                with act.If(busiest > P):
                    with act.Fori(0, OVER_BLOCKS[l] * NE) as k:
                        act.wait_ge(o["xt"], k + 1)
                        for half in range(2):
                            t = nc.scalar.activation(over_xT[:, 4 * half:4 * half + 4, :],
                                                     bank[2 + half][:, :].rearrange("p (k n) -> p k n", k=4), ACT.Copy)
                        t.then_inc(o["xe"], 1)
                        act.wait_ge(o["gu"], k + 1)
                        for n in range(2):
                            t = nc.scalar.activation(silu[:, n, :], bank[2 + 2 * n][:, :], ACT.Silu)
                        t.then_inc(o["s"], 1)
                        act.wait_ge(o["ht"], k + 1)
                        for half in range(2):
                            t = nc.scalar.activation(over_hT[:, 4 * half:4 * half + 4, :],
                                                     bank[6 + half][:, :].rearrange("p (k n) -> p k n", k=4), ACT.Copy)
                        t.then_inc(o["he"], 1)
            root(4, 2)

        @block.vector
        def _(dve):
            steps = [0]
            took = [0]

            def link(ins):
                steps[0] += 1
                ins.then_inc(dve_step, 1)
                dve.wait_ge(dve_step, steps[0])

            def take(name):
                assert taker[name] == "dve" and TAKEN[name] == took[0] + 1, name
                took[0] += 1
                dve.wait_ge(mm_done, DONE[name])
                return bank[(DONE[name] - 1) % 8]

            def TT(o, a, b, op):
                return nc.vector.tensor_tensor(o, a, b, op)

            dve.wait_ge(small_loaded, N_SMALL)

            def modulation(l, c):
                take_row = take(("mod", l, c))
                row = mod_rows[l][:, c * CH:(c + 1) * CH]
                TT(row, take_row[0:2, :], row, ALU.add).then_inc(dve_took, 1)
                dve.wait_ge(dve_took, took[0])
                if c in (2, 3, 8, 9):
                    link(nc.vector.scalar_tensor_tensor(out=row, in0=row, scalar=1.0,
                                                        in1=norm_rows[:, l, c // 6, (c % 2) * CH:(c % 2 + 1) * CH],
                                                        op0=ALU.add, op1=ALU.mult))

            def hidden_layer(l, n):
                b = take(("fl", l, n + 1))
                h0, h1 = hid[0:64, 0, :], hid[0:64, 1, :]
                if n == 0:
                    dve.wait_ge(filt_loaded, 16 * (7 + 5 * l))
                nc.vector.tensor_scalar(h0, b[0:64, 0:SEQ], fcol[:, l, 2 * n:2 * n + 1], fcol[:, l, 1:2],
                                        ALU.add, ALU.mult).then_inc(dve_took, 1)
                dve.wait_ge(dve_took, took[0])
                link(nc.vector.tensor_scalar(h1, h0, INV_2PI, MAGIC, ALU.mult, ALU.add))
                link(nc.vector.tensor_scalar(h1, h1, -MAGIC, None, ALU.add))
                for part in TWO_PI:
                    link(nc.vector.scalar_tensor_tensor(out=h0, in0=h1, scalar=-part, in1=h0, op0=ALU.mult,
                                                        op1=ALU.add))
                nc.vector.tensor_scalar(h0, h0, PI, -PI, ALU.min, ALU.max).then_inc(sin_in, 1)
                dve.wait_ge(sin_out, 2 * l + n + 1)

            def taps(l, o):
                if o or l:
                    dve.wait_ge(abs_ready, 8 * l + 4 * o)
                    dve.wait_ge(mm_done, DONE[("fk", l - 1 + o, 1 - o, 4)])
                for d in range(2):
                    for tt in range(2):
                        b = take(("f3", l, o, d, tt))
                        TT(filt[:, d, tt, :], b[:, :], decay[:, 2 if (d == 1 and tt == 0) else tt, :], ALU.mult)\
                            .then_inc(dve_took, 1)
                        dve.wait_ge(dve_took, took[0])
                for tt in range(2):
                    link(TT(filt_pm[:, 0, tt, :], filt[:, 0, tt, :], filt[:, 1, tt, :], ALU.add))
                    ins = TT(filt_pm[:, 1, tt, :], filt[:, 0, tt, :], filt[:, 1, tt, :], ALU.subtract)
                    link(ins) if tt == 0 else ins.then_inc(pm_ready, 1)
                dve.wait_ge(pm_ready, 2 * l + o + 1)

            def tap_norm(l, o):
                b = take(("fn", l, o))
                nc.vector.reciprocal(rnorm, b[:, :]).then_inc(dve_took, 1)
                dve.wait_ge(dve_took, took[0])

            def tap_spectra(l, o):
                if l:
                    dve.wait_ge(spec_stored, 16 * (o + 1))
                for k in range(5):
                    b = take(("fk", l, o, k))
                    TT(spectra[:, o, k, :], b[:, :], rnorm, ALU.mult).then_inc(dve_took, 1)
                    dve.wait_ge(dve_took, took[0])

            def filter_step(l, g):
                if g < 2:
                    hidden_layer(l, g)
                elif g == 2:
                    taps(l, 0)
                elif g in (3, 5):
                    tap_norm(l, g // 4)
                elif g == 4:
                    tap_spectra(l, 0)
                    taps(l, 1)
                else:
                    tap_spectra(l, 1)

            for kind, l, i in OPENING:
                modulation(l, i) if kind == "mod" else filter_step(l, i)

            def inverse_rms(ph, tbs):
                nt = len(tbs)
                for k, tb in enumerate(tbs):
                    link(nc.vector.tensor_tensor_reduce(hrow[:, k % 2, :], x[:, tb, :], x[:, tb, :], 1.0, 0.0,
                                                        ALU.mult, ALU.add, stat[:, 0, k:k + 1]))
                nc.vector.tensor_scalar(stat[:, 1, 0:nt], stat[:, 0, 0:nt], 1.0 / D, EPS, ALU.mult, ALU.add)\
                    .then_inc(var_ready, 1)
                dve.wait_ge(root_ready, ph + 1)
                link(nc.vector.reciprocal(stat[:, 3, 0:nt], stat[:, 2, 0:nt]))
                link(TT(stat[:, 4, 0:nt], stat[:, 3, 0:nt], stat[:, 3, 0:nt], ALU.mult))
                link(TT(stat[:, 4, 0:nt], stat[:, 4, 0:nt], stat[:, 1, 0:nt], ALU.mult))
                link(nc.vector.tensor_scalar(stat[:, 4, 0:nt], stat[:, 4, 0:nt], -0.5, 1.5, ALU.mult, ALU.add))
                link(TT(stat[:, 3, 0:nt], stat[:, 3, 0:nt], stat[:, 4, 0:nt], ALU.mult))

            def norm(l, p, tbs):
                ph = 2 * l + p
                inverse_rms(ph, tbs)
                dve.wait_ge(ab_loaded, 32 * (ph + 1))
                for k, tb in enumerate(tbs):
                    if k >= 2:
                        dve.wait_ge(mm_done, DONE[("hT", l, p, tbs[k - 2], 1)])
                        if p == 1:
                            dve.wait_ge(h2_stored[k % 2], 16 * (T_BEFORE[l] // 2 + k // 2))
                    link(nc.vector.scalar_tensor_tensor(out=hrow[:, k % 2, :], in0=x[:, tb, :], scalar=stat[:, 3, k:k + 1],
                                                        in1=A_bc[:, tb // 2, :], op0=ALU.mult, op1=ALU.mult))
                    TT(hrow[:, k % 2, :], hrow[:, k % 2, :], B_bc[:, tb // 2, :], ALU.add).then_inc(rows_ready, 1)

            def rotate(src, tb, nh, j, dst):
                w = nh * HD
                cos = rope[:, tb, 2 * j, :].unsqueeze(1).broadcast_to([P, nh, HD])
                sin = rope[:, tb, 2 * j + 1, :].rearrange("p (a b i) -> p a b i", a=2, b=2)
                t0 = rope_tmp[:, 0, 0:w].rearrange("p (h d) -> p h d", h=nh)
                t1 = rope_tmp[:, 1, 0:w].rearrange("p (h a b i) -> p h a b i", h=nh, a=2, b=2)
                s5 = src.rearrange("p (h a b i) -> p h a b i", h=nh, a=2, b=2)
                TT(t0, src.rearrange("p (h d) -> p h d", h=nh), cos, ALU.mult).then_inc(dve_step, 1)
                for b in range(2):
                    TT(t1[:, :, :, b, :], s5[:, :, :, 1 - b, :],
                       sin[:, :, b, :].unsqueeze(1).broadcast_to([P, nh, 2, 16]), ALU.mult).then_inc(dve_step, 1)
                steps[0] += 3
                dve.wait_ge(dve_step, steps[0])
                if nh == NH:
                    a = rope_tmp[:, 0, :].rearrange("p (g j d) -> p g j d", g=2, j=4)
                    b2 = rope_tmp[:, 1, :].rearrange("p (g j d) -> p g j d", g=2, j=4)
                    return TT(dst.rearrange("p (j g d) -> p g j d", g=2, j=4), a, b2, ALU.add)
                return TT(dst, rope_tmp[:, 0, 0:w], rope_tmp[:, 1, 0:w], ALU.add)

            dve.wait_ge(const_loaded, 16)
            dve.wait_ge(x_loaded, 32)
            for l in range(DEPTH):
                T = tokens_of(l)
                nt = len(T)

                def convolve(c):
                    i = 3 * T_BEFORE[l] + c * nt
                    dve.wait_ge(convw_loaded, 32 * (3 * l + c + 1))
                    for tb in T:
                        dve.wait_ge(stage_loaded[i % 2], 48 * (i // 2 + 1))
                        st = stage[:, i % 2, :, :]
                        link(TT(st, st, conv_w[:, 0:3, :], ALU.mult))
                        zt = z[:, tb, c, :]
                        link(TT(zt, st[:, 0, :], st[:, 1, :], ALU.add))
                        link(TT(zt, zt, st[:, 2, :], ALU.add))
                        TT(zt, zt, conv_w[:, 3, :], ALU.add).then_inc(conv_done, 1)
                        i += 1
                    dve.wait_ge(conv_done, i)

                Lb = NE * l
                norm(l, 0, range(4))
                convolve(0)
                convolve(1)
                for tb in range(4):
                    b = take(("in", l, "kv", tb))
                    link(nc.vector.tensor_copy(vrow[:, tb, :], b[:, P:2 * P]))
                    kdst = krow[:, tb, :]
                    if tb < 2:
                        rotate(b[:, 0:P], tb, NKV, 1, kdst).then_inc(dve_took, 1)
                        dve.wait_ge(dve_took, took[0])
                    else:
                        nc.vector.tensor_copy(kdst, b[:, 0:P]).then_inc(dve_took, 1)
                        dve.wait_ge(dve_took, took[0])
                convolve(2)
                for k, tb in enumerate(T):
                    b = take(("in", l, "q", tb))
                    if k == 0:
                        dve.wait_ge(mm_done, DONE[("hT", l, 0, 3, 1)])
                    if tb < 2:
                        rotate(b[:, :], tb, NH, 0, qrow[:, tb, :]).then_inc(dve_took, 1)
                        dve.wait_ge(dve_took, took[0])
                    else:
                        nc.vector.tensor_scalar(qrow[:, tb, :].rearrange("p (j g d) -> p g j d", g=2, j=4),
                                                b[:, :].rearrange("p (g j d) -> p g j d", g=2, j=4),
                                                HD ** -0.5, None, ALU.mult).then_inc(dve_took, 1)
                        dve.wait_ge(dve_took, took[0])
                heads = [(tb, h) for tb in T for h in range(NH)]
                hb = NH * T_BEFORE[l]
                dve.wait_ge(mm_done, DONE[("fy", l, nt // 2 - 1, 3)])

                def finish_block(tb, i):
                    n = T_BEFORE[l] + i
                    dve.wait_ge(sink_exp, n + 1)
                    dve.wait_ge(exp_done, NH * (n + 1))
                    link(TT(att[:, i % 2, 5, :], att[:, i % 2, 2, :], att[:, i % 2, 4, :], ALU.add))
                    link(nc.vector.reciprocal(att[:, i % 2, 5, :], att[:, i % 2, 5, :]))
                    dve.wait_ge(dve_took, took[0])
                    y3 = ya[:, i % 2, :].rearrange("p (h d) -> p h d", h=NH)
                    TT(y3, y3, att[:, i % 2, 5, :].unsqueeze(2).broadcast_to([P, NH, HD]), ALU.mult).then_inc(ya_ready, 1)

                for i in range(len(heads) + 3):
                    if i < len(heads):
                        tb, h = heads[i]
                        nk = 512 if tb < 2 else 256
                        b = take(("sc", l, tb, h))
                        if i >= 2:
                            dve.wait_ge(exp_done, hb + i - 1)
                        m = mask[:, tb, :] if tb < 2 else mask[:, 0, 256:512]
                        nc.vector.tensor_tensor_reduce(S_buf[:, i % 2, 0:nk], b[:, 0:nk], m, 1.0, -3.0e38, ALU.add,
                                                       ALU.max, att[:, i // NH % 2, 0, h:h + 1]).then_inc(dve_took, 1)
                        dve.wait_ge(dve_took, took[0])
                        nc.vector.tensor_scalar(att[:, i // NH % 2, 1, h:h + 1], att[:, i // NH % 2, 0, h:h + 1], sink[:, l, h:h + 1], -1.0,
                                                ALU.max, ALU.mult).then_inc(max_ready, 1)
                        if h == NH - 1:
                            dve.wait_ge(max_ready, hb + i + 1)
                            TT(att[:, i // NH % 2, 3, :], att[:, i // NH % 2, 1, :], sink[:, l, :], ALU.add).then_inc(sink_in, 1)
                    if i >= 3:
                        tb, h = heads[i - 3]
                        k = (i - 3) // NH
                        if h == 0 and k >= 2:
                            dve.wait_ge(mm_done, DONE[("yaT", l, T[k - 2])])
                        b = take(("pv", l, tb, h))
                        nc.vector.tensor_copy(ya[:, k % 2, h * HD:(h + 1) * HD], b[:, 0:HD]).then_inc(dve_took, 1)
                        dve.wait_ge(dve_took, took[0])
                        if h == NH - 1:
                            finish_block(tb, k)
                dve.wait_ge(bias_loaded, 16 * (l + 1))
                dve.wait_ge(spec_loaded, 16 * (l + 1))
                dve.wait_ge(mm_done, DONE[("yaT", l, T[-1])])
                for o in range(2):
                    for s in range(nt // 2):
                        for half in range(2):
                            re, im = spectra[:, o, half, :], spectra[:, o, 2 + half, :]
                            re2 = spectra[:, o, 4 if half == 0 else 1, :]
                            ur = take(("u", l, o, s, (FR0, FR1)[half]))
                            if half == 0 and o:
                                dve.wait_ge(mm_done, DONE[("c", l, 0, s, 1)])
                            yr, yi = Yspec[:, s, half, :], Yspec[:, s, 2 + half, :]
                            link(TT(yr, ur[:, :], re, ALU.mult))
                            TT(yi, ur[:, :], im, ALU.mult).then_inc(dve_took, 1)
                            dve.wait_ge(dve_took, took[0])
                            ui = take(("u", l, o, s, (FI0, FI1)[half]))
                            link(TT(hy_tmp[:, 0, :], ui[:, :], im, ALU.mult))
                            TT(hy_tmp[:, 1, :], ui[:, :], re2, ALU.mult).then_inc(dve_took, 1)
                            dve.wait_ge(dve_took, took[0])
                            link(TT(yr, yr, hy_tmp[:, 0, :], ALU.subtract))
                            TT(yi, yi, hy_tmp[:, 1, :], ALU.add).then_inc(spec_ready, 1)
                            dve.wait_ge(spec_ready, 2 * (o * (nt // 2) + s) + half + 1 + 2 * T_BEFORE[l])
                    for s in range(nt // 2):
                        for tt in range(2):
                            tb = 2 * s + tt
                            y = z[:, tb, 0, :]
                            link(TT(hy_tmp[:, tt, :], y, hy_bias[:, o, :], ALU.mult))
                            b = take(("c", l, o, s, tt))
                            TT(hy_tmp[:, tt, :], b[:, :], hy_tmp[:, tt, :], ALU.add).then_inc(dve_took, 1)
                            dve.wait_ge(dve_took, took[0])
                            TT(y, hy_tmp[:, tt, :], z[:, tb, 1 + o, :], ALU.mult).then_inc(y_ready, 1)
                        dve.wait_ge(y_ready, 2 * T_BEFORE[l] + o * nt + 2 * (s + 1))
                for br in range(3):
                    for n in range(2):
                        for tb in T:
                            b = take(("b", l, br, n, tb))
                            g = ("g", l, br, n, tb)
                            dve.wait_ge(act_took, TAKEN[g])
                            gb = gate_buf[:, (br * 2 * nt + n * nt + T.index(tb)) % 2, :]
                            m = merged[:, tb, n * CH:(n + 1) * CH]
                            if br == 0:
                                TT(m, b[:, :], gb, ALU.mult).then_inc(dve_took, 1)
                                dve.wait_ge(dve_took, took[0])
                                continue
                            TT(merge_tmp, b[:, :], gb, ALU.mult).then_inc(dve_took, 1)
                            dve.wait_ge(dve_took, took[0])
                            ins = TT(m, m, merge_tmp, ALU.add)
                            if br == 1:
                                link(ins)
                            else:
                                ins.then_inc(merged_ready, 1)
                                dve.wait_ge(merged_ready, 2 * T_BEFORE[l] + n * nt + T.index(tb) + 1)
                dve.wait_ge(g_loaded, 16 * (2 * l + 1))
                for n in range(2):
                    for tb in T:
                        b = take(("o", l, n, tb))
                        link(TT(out_tmp, b[:, :], G_bc[:, tb // 2, n * CH:(n + 1) * CH], ALU.mult))
                        xt = x[:, tb, n * CH:(n + 1) * CH]
                        TT(xt, xt, out_tmp, ALU.add).then_inc(dve_took, 1)
                        dve.wait_ge(dve_took, took[0])
                norm(l, 1, T)
                w16 = nt * NE
                dve.wait_ge(act_took, TAKEN[("r", l, T[-1])])

                def r(i):
                    return rt[:, i, 0:w16]

                def r4(i):
                    return r(i).rearrange("p (q i) -> p q i", i=4)

                def r16(i):
                    return r(i).rearrange("p (t e) -> p t e", e=NE)

                def beats(val, res, k):
                    for j in range(4):
                        if j < 3:
                            link(TT(res[j][:, :, j + 1:4], val[:, :, j:j + 1].broadcast_to([P, k, 3 - j]),
                                    val[:, :, j + 1:4], ALU.is_ge))
                        if j > 0:
                            link(TT(res[j][:, :, 0:j], val[:, :, j:j + 1].broadcast_to([P, k, j]), val[:, :, 0:j],
                                    ALU.is_gt))

                link(nc.vector.memset(rt[:, 2:6, :], 0.0))
                link(nc.vector.memset(rt4[:, 1:5, :], 0.0))
                link(TT(r16(1), r16(0), br_bc[:, :].unsqueeze(1).broadcast_to([P, nt, NE]), ALU.add))
                beats(r4(1), [r4(2 + j) for j in range(4)], nt * 4)
                link(TT(r(6), r(2), r(3), ALU.add))
                link(TT(r(6), r(6), r(4), ALU.add))
                link(TT(r(6), r(6), r(5), ALU.add))
                link(nc.vector.tensor_scalar(r(7), r(6), 2.0, None, ALU.is_lt))
                link(TT(r(8), r(1), r(7), ALU.mult))
                gs = rt4[:, 0, 0:nt * 4]
                link(nc.vector.tensor_reduce(gs, r4(8), AX.X, ALU.add))

                def q4(i):
                    return rt4[:, i, 0:nt * 4].rearrange("p (t g) -> p t g", g=4)

                beats(q4(0), [q4(1 + j) for j in range(4)], nt)
                link(TT(rt4[:, 5, 0:nt * 4], rt4[:, 1, 0:nt * 4], rt4[:, 2, 0:nt * 4], ALU.add))
                link(TT(rt4[:, 5, 0:nt * 4], rt4[:, 5, 0:nt * 4], rt4[:, 3, 0:nt * 4], ALU.add))
                link(TT(rt4[:, 5, 0:nt * 4], rt4[:, 5, 0:nt * 4], rt4[:, 4, 0:nt * 4], ALU.add))
                link(nc.vector.tensor_scalar(rt4[:, 6, 0:nt * 4], rt4[:, 5, 0:nt * 4], 1.0, None, ALU.is_lt))
                TT(r4(9), r4(7), rt4[:, 6, 0:nt * 4].unsqueeze(2).broadcast_to([P, nt * 4, 4]), ALU.mult)\
                    .then_inc(sel_ready, 1)
                dve.wait_ge(sel_ready, l + 1)
                link(TT(r(10), r(0), r(9), ALU.mult))
                link(nc.vector.tensor_reduce(rt1[:, 0, 0:nt], r16(10), AX.X, ALU.add))
                link(nc.vector.reciprocal(rt1[:, 1, 0:nt], rt1[:, 0, 0:nt]))
                link(TT(r16(10), r16(10), rt1[:, 1, 0:nt].unsqueeze(2).broadcast_to([P, nt, NE]), ALU.mult))
                b = take(("cnt", l))
                link(nc.vector.tensor_copy(r(11), b[:, 0:w16]))
                nc.vector.tensor_reduce(most[:, :], b[:, 64:80], AX.X, ALU.max).then_inc(dve_took, 1)
                dve.wait_ge(dve_took, took[0])
                m_over = NE * OVER_BLOCKS[l]
                link(nc.vector.scalar_tensor_tensor(out=r(12), in0=r(11), scalar=float(NE),
                                                    in1=const[:, C_EXP:C_EXP + w16], op0=ALU.mult, op1=ALU.add))
                if OVER_BLOCKS[l] > 1:
                    link(nc.vector.tensor_scalar(r(13), r(11), float(-P), 0.0, ALU.add, ALU.max))
                    link(nc.vector.scalar_tensor_tensor(out=r(12), in0=r(13), scalar=float(m_over - NE), in1=r(12),
                                                        op0=ALU.mult, op1=ALU.add))
                for blk in range(2, OVER_BLOCKS[l] + 1):
                    link(nc.vector.tensor_scalar(r(13), r(11), float(blk * P), float(NE - P * m_over), ALU.is_ge,
                                                 ALU.mult))
                    link(TT(r(12), r(12), r(13), ALU.add))
                link(nc.vector.scalar_tensor_tensor(out=r(12), in0=r(12), scalar=1.0, in1=r(9), op0=ALU.add,
                                                    op1=ALU.mult))
                link(nc.vector.tensor_reduce(rt1[:, 2, 0:nt], r16(12), AX.X, ALU.max))
                link(nc.vector.tensor_reduce(rt1[:, 3, 0:nt], r16(12), AX.X, ALU.add))
                link(TT(rt1[:, 3, 0:nt], rt1[:, 3, 0:nt], rt1[:, 2, 0:nt], ALU.subtract))
                link(TT(r16(13), r16(12), rt1[:, 2, 0:nt].unsqueeze(2).broadcast_to([P, nt, NE]), ALU.is_equal))
                link(TT(r(14), r(9), r(13), ALU.subtract))
                link(TT(r(13), r(13), r(10), ALU.mult))
                link(TT(r(14), r(14), r(10), ALU.mult))
                link(nc.vector.tensor_reduce(w_tok[:, 0, 0:nt], r16(13), AX.X, ALU.add))
                link(nc.vector.tensor_reduce(w_tok[:, 1, 0:nt], r16(14), AX.X, ALU.add))
                far = float(1 << 20)
                for i2 in range(2):
                    link(nc.vector.tensor_scalar(rt1[:, 4, 0:nt], rt1[:, 2 + i2, 0:nt], P * NE + 0.5, far, ALU.is_lt,
                                                 ALU.mult))
                    link(nc.vector.scalar_tensor_tensor(out=idx_beyond[:, i2, 0:nt], in0=rt1[:, 2 + i2, 0:nt],
                                                        scalar=float(-P * NE - 1), in1=rt1[:, 4, 0:nt], op0=ALU.add,
                                                        op1=ALU.add))
                for i2 in range(2):
                    nc.vector.tensor_scalar(idx_tok[:, i2, 0:nt], rt1[:, 2 + i2, 0:nt], -1.0, None, ALU.add)\
                        .then_inc(idx_ready, 1)

                Wb = l * PER_LAYER

                def low(e, p):
                    pos = position(e, p)
                    dve.wait_ge(hi_done, ready_at(e, p) + Wb)
                    TT(w_lo[:, pos % N_SPLIT, :, :], raw(pos % N_RAW), w_hi[:, pos % N_SPLIT, :, :].bitcast(F32),
                       ALU.subtract).then_inc(lo_done, 1)

                def low_next(e, p):
                    if isinstance(e, int) and e == NE - 1:
                        low(NE, 8 + p)
                    else:
                        low(e + 1, p)

                def take_ys(e, par, n):
                    dve.wait_ge(w_used, ready_at(e + 1, 9 + 2 * n) + Wb)
                    if n == 0 and not (isinstance(e, int) and e < 2):
                        dve.wait_ge(ys_stored[par], (e - par) * 8 + 8 * Lb)
                    nc.vector.tensor_copy(ys[:, par, n * CH:(n + 1) * CH], bank[n][:, :]).then_inc(ys_took, 1)

                def hidden(e, n):
                    dve.wait_ge(silu_done, e * 2 + (2 * Lb + n + 1))
                    dve.wait_ge(w_used, ready_at(e, 4 * n + 3) + Wb)
                    if not (isinstance(e, int) and e + Lb == 0):
                        dve.wait_ge(ht_mm, e * 2 + (2 * Lb - 2 + n + 1))
                    TT(hexp[:, n, :], bank[3 + 2 * n][:, :], silu[:, n, :], ALU.mult).then_inc(h_done, 1)

                def low_of(bk, hi, lo, half, par, made, out_sem, v):
                    dve.wait_ge(made, v)
                    part = slice(4 * half, 4 * half + 4)
                    TT(lo[:, par, part, :], bk[:, :].rearrange("p (k n) -> p k n", k=4),
                       hi[:, par, part, :].bitcast(F32), ALU.subtract).then_inc(out_sem, 1)

                def low_xs(e, par):
                    for half in range(2):
                        low_of(bank[2 + half], xsT_hi, xsT_lo, half, par, xt_hi, xt_lo, e * 2 + (2 * Lb + half + 1))

                def expert(e, par):
                    for p in range(turns(e)):
                        if p + 2 < turns(e):
                            low(e, p + 2)
                        else:
                            low_next(e, p + 2 - turns(e))
                        if p == 1 and not (isinstance(e, int) and e < 2):
                            take_ys(e - 2, par, 1)
                        if p == 4:
                            hidden(e, 0)
                        if p == min(8, turns(e) - 1):
                            hidden(e, 1)
                        if p == min(9, turns(e) - 1):
                            for half in range(2):
                                low_of(bank[6 + half], hexpT_hi, hexpT_lo, half, par, ht_hi, ht_lo,
                                       e * 2 + (2 * Lb + half + 1))
                            if not (isinstance(e, int) and e == NE - 1):
                                low_xs(e + 1, 1 - par)
                        if p == 10:
                            take_ys(e - 1, 1 - par, 0)

                low_xs(0, 0)
                low(0, 0)
                low(0, 1)
                for e in range(4):
                    expert(e, e % 2)
                with dve.Fori(2, NE // 2 - 1) as i:
                    expert(i * 2, 0)
                    expert(i * 2 + 1, 1)
                expert(NE - 2, 0)
                expert(NE - 1, 1)
                low(NE, 10)
                low(NE, 11)
                take_ys(NE - 2, 0, 1)
                take_ys(NE - 1, 1, 0)
                take_ys(NE - 1, 1, 1)
                o = over[l]
                dve.wait_ge(idx_ready, 2 * l + 2)
                busiest = dve.value_load(most[0:1, 0:1], min_val=0, max_val=512)
                with dve.If(busiest > P):
                    dve.wait_ge(ys_stored[0], 8 * (Lb + NE))
                    with dve.Fori(0, OVER_BLOCKS[l] * NE) as k:
                        dve.wait_ge(o["s"], k + 1)
                        for n in range(2):
                            t = TT(hexp[:, n, :], bank[3 + 2 * n][:, :], silu[:, n, :], ALU.mult)
                        t.then_inc(o["h"], 1)
                        dve.wait_ge(o["d"], k + 1)
                        for n in range(2):
                            t = nc.vector.tensor_copy(ys[:, 0, n * CH:(n + 1) * CH], bank[n][:, :])
                        t.then_inc(o["ys"], 1)
                dve.wait_ge(g_loaded, 16 * (2 * l + 2))
                dve.wait_ge(got_ready, l + 1)
                for k, tb in enumerate(T):
                    dve.wait_ge(got_loaded[k], 32 * (l + 1))
                    ga, gb = got_a[:, k, :], got_b[:, k, :]
                    link(nc.vector.tensor_scalar(ga, ga, w_tok[:, 0, k:k + 1], None, ALU.mult))
                    link(nc.vector.scalar_tensor_tensor(out=gb, in0=gb, scalar=w_tok[:, 1, k:k + 1], in1=ga,
                                                        op0=ALU.mult, op1=ALU.add))
                    link(TT(gb, gb, G_bc[:, tb // 2, :], ALU.mult))
                    TT(x[:, tb, :], x[:, tb, :], gb, ALU.add).then_inc(combined, 1)
                    dve.wait_ge(combined, T_BEFORE[l] + k + 1)
            inverse_rms(4, [0, 1])
            dve.wait_ge(final_loaded, 16)
            for tb in range(2):
                nc.vector.scalar_tensor_tensor(out=final_rows[:, tb, :], in0=x[:, tb, :], scalar=stat[:, 3, tb:tb + 1],
                                               in1=final_w, op0=ALU.mult, op1=ALU.mult).then_inc(final_ready, 1)

        @block.tensor
        def _(pe):
            at = [0]

            def begin(*name):
                i = at[0]
                assert order[i] == name, (order[i], name)
                if i >= 8:
                    old = order[i - 8]
                    pe.wait_ge(act_took if taker[old] == "act" else dve_took, TAKEN[old])
                at[0] += 1
                return bank[i % 8]

            def mm(o, a, b, first, last):
                return nc.tensor.matmul(o, a, b, start=first, stop=last)

            def wait_chunk(key):
                s, v = slot_at[key]
                pe.wait_ge(slot_loaded[2 * s], v)
                return s

            def turn(dst, src, n):
                for j in range(n):
                    ins = nc.tensor.transpose(dst[:, j * P:(j + 1) * P], src[:, j * P:(j + 1) * P], ident)
                return ins

            pe.wait_ge(const_loaded, 16)
            pe.wait_ge(c_ready, 1)

            def modulation(l, c):
                w = slot(wait_chunk(("mod", l, c)))
                b = begin("mod", l, c)
                for k in range(KB):
                    ins = mm(b[0:2, :], c_act[:, k, :], w[:, k, :], k == 0, k == KB - 1)
                ins.then_inc(mm_done, 1)

            def taps(l, o):
                pe.wait_ge(sin_out, 2 * l + 2)
                for d in range(2):
                    for tt in range(2):
                        b = begin("f3", l, o, d, tt)
                        mm(b[:, :], hid[0:64, 3, tt * P:(tt + 1) * P],
                           w3[:, (2 * o + d) * HY:(2 * o + d + 1) * HY], True, True).then_inc(mm_done, 1)

            def tap_norm(l, o):
                pe.wait_ge(abs_ready, 8 * l + 4 * o + 4)
                b = begin("fn", l, o)
                for i in range(4):
                    ins = mm(b[:, :], ones, filt_abs[:, i // 2, i % 2, :], i == 0, i == 3)
                ins.then_inc(mm_done, 1)

            def tap_spectra(l, o):
                pe.wait_ge(pm_ready, 2 * l + o + 1)
                for k, (blk, sign) in enumerate(((FR0, 0), (FR1, 0), (FIZ, 1), (FI1, 1), (FRN, 0))):
                    b = begin("fk", l, o, k)
                    for tt in range(2):
                        ins = mm(b[:, :], dft[:, tt, blk, :], filt_pm[:, sign, tt, :], tt == 0, tt == 1)
                    ins.then_inc(mm_done, 1)

            def filter_step(l, g):
                if g == 0:
                    pe.wait_ge(filt_loaded, 16 * (7 + 5 * l))
                    b = begin("fl", l, 1)
                    mm(b[0:64, 0:SEQ], w1, feats, True, True).then_inc(mm_done, 1)
                elif g == 1:
                    pe.wait_ge(sin_out, 2 * l + 1)
                    b = begin("fl", l, 2)
                    mm(b[0:64, 0:SEQ], w2, hid[0:64, 2, :], True, True).then_inc(mm_done, 1)
                elif g == 2:
                    taps(l, 0)
                elif g in (3, 5):
                    tap_norm(l, g // 4)
                elif g == 4:
                    tap_spectra(l, 0)
                    taps(l, 1)
                else:
                    tap_spectra(l, 1)

            for kind, l, i in OPENING:
                modulation(l, i) if kind == "mod" else filter_step(l, i)

            for l in range(DEPTH):
                T = tokens_of(l)
                nt = len(T)
                Lb = NE * l

                def turn_rows(p, tbs):
                    for k, tb in enumerate(tbs):
                        pe.wait_ge(rows_ready, ROWS_AT[l, p] + k + 1)
                        for half in range(2):
                            b = begin("hT", l, p, tb, half)
                            turn(b, hrow[:, k % 2, half * 512:(half + 1) * 512], 4).then_inc(mm_done, 1)

                def project(key, tb, name, cols=CH):
                    s, _ = slot_at[key]
                    w = slot(s, cols)
                    b = begin(*name)
                    for k in range(KB):
                        ins = mm(b[:, 0:cols], hT[:, k, tb * P:(tb + 1) * P], w[:, k, :], k == 0, k == KB - 1)
                    ins.then_inc(mm_done, 1)

                turn_rows(0, range(4))
                for c in ("v", "x1", "x2"):
                    wait_chunk(("in", l, c))
                    for tb in T:
                        pe.wait_ge(act_took, TAKEN[("hT", l, 0, tb, 1)])
                        project(("in", l, c), tb, ("in", l, c, tb))
                wait_chunk(("in", l, "kv"))
                for tb in range(4):
                    pe.wait_ge(act_took, TAKEN[("hT", l, 0, tb, 1)])
                    project(("in", l, "kv"), tb, ("in", l, "kv", tb), 256)
                wait_chunk(("in", l, "q"))
                for tb in T:
                    project(("in", l, "q"), tb, ("in", l, "q", tb))
                for tb in range(4):
                    pe.wait_ge(dve_took, TAKEN[("in", l, "kv", tb)])
                    b = begin("kT", l, tb)
                    turn(b, krow[:, tb, :], 1).then_inc(mm_done, 1)
                wait_chunk(("in", l, "f"))
                for tb in T:
                    project(("in", l, "f"), tb, ("in", l, "f", tb))
                for tb in T:
                    pe.wait_ge(dve_took, TAKEN[("in", l, "q", tb)])
                    b = begin("qT", l, tb)
                    turn(b, qrow[:, tb, :], 4).then_inc(mm_done, 1)
                pe.wait_ge(four_loaded, 16 * (l + 1))
                pe.wait_ge(act_took, TAKEN[("in", l, "f", T[-1])])
                for s in range(nt // 2):
                    for g in range(5):
                        if g < 4:
                            b = begin("fp", l, s, g)
                            for tt in range(2):
                                ins = mm(b[:, :], frow[:, 2 * s + tt, g * P:(g + 1) * P],
                                         four[:, tt * 512:(tt + 1) * 512], tt == 0, tt == 1)
                            ins.then_inc(mm_done, 1)
                        if g > 0:
                            pe.wait_ge(act_took, TAKEN[("fp", l, s, g - 1)])
                            b = begin("fy", l, s, g - 1)
                            for j in range(2):
                                ins = mm(b[:, 0:SEQ], four[:, 1024 + j * P:1024 + (j + 1) * P],
                                         pq[:, (g - 1) % 2, j * SEQ:(j + 1) * SEQ], j == 0, j == 1)
                            ins.then_inc(mm_done, 1)
                heads = [(tb, h) for tb in T for h in range(NH)]
                hb = NH * T_BEFORE[l]
                pe.wait_ge(act_took, TAKEN[("qT", l, T[-1])])

                def turn_ya(k):
                    pe.wait_ge(ya_ready, T_BEFORE[l] + k + 1)
                    b = begin("yaT", l, T[k])
                    turn(b, ya[:, k % 2, :], 4).then_inc(mm_done, 1)

                for i in range(len(heads) + 3):
                    if i < len(heads):
                        tb, h = heads[i]
                        g, j = h // 4, h % 4
                        keys = slice(0, 512) if tb < 2 else slice(256, 512)
                        b = begin("sc", l, tb, h)
                        mm(b[:, 0:keys.stop - keys.start], qT[g * HD:(g + 1) * HD, j, tb * P:(tb + 1) * P],
                           kT[g * HD:(g + 1) * HD, keys], True, True).then_inc(mm_done, 1)
                    if 2 <= i < len(heads) + 2:
                        tb, h = heads[i - 2]
                        pe.wait_ge(exp_done, hb + i - 1)
                        b = begin("pt", l, tb, h)
                        turn(b, P_buf[:, i % 2, :], 4 if tb < 2 else 2).then_inc(mm_done, 1)
                    if i >= 3:
                        tb, h = heads[i - 3]
                        g = h // 4
                        kb = range(4) if tb < 2 else range(2, 4)
                        pe.wait_ge(act_took, TAKEN[("pt", l, tb, h)])
                        b = begin("pv", l, tb, h)
                        for n, k in enumerate(kb):
                            ins = mm(b[:, 0:HD], PT[:, (i - 3) % 2, n, :], vrow[:, k, g * HD:(g + 1) * HD], n == 0,
                                     n == len(kb) - 1)
                        ins.then_inc(mm_done, 1)
                        if h == NH - 1 and tb > 0:
                            turn_ya((i - 3) // NH - 1)
                turn_ya(nt - 1)
                pe.wait_ge(conv_done, 3 * (T_BEFORE[l] + nt))
                for o in range(2):
                    for s in range(nt // 2):
                        if o:
                            pe.wait_ge(y_ready, 2 * T_BEFORE[l] + 2 * (s + 1))
                        for blk in (FR0, FI0, FR1, FI1):
                            b = begin("u", l, o, s, blk)
                            for tt in range(2):
                                ins = mm(b[:, :], dft[:, tt, blk, :], z[:, 2 * s + tt, 0, :], tt == 0, tt == 1)
                            ins.then_inc(mm_done, 1)
                    for s in range(nt // 2):
                        pe.wait_ge(spec_ready, 2 * T_BEFORE[l] + 2 * (o * (nt // 2) + s + 1))
                        for tt in range(2):
                            b = begin("c", l, o, s, tt)
                            for k in range(4):
                                ins = mm(b[:, :], inv[:, k, tt * P:(tt + 1) * P], Yspec[:, s, k, :], k == 0, k == 3)
                            ins.then_inc(mm_done, 1)
                for k, tb in enumerate(T):
                    pe.wait_ge(y_ready, 2 * T_BEFORE[l] + nt + k + 1)
                    b = begin("yhT", l, tb)
                    turn(b, z[:, tb, 0, :], 4).then_inc(mm_done, 1)
                pe.wait_ge(act_took, TAKEN[("yhT", l, T[-1])])
                for br in range(3):
                    wait_chunk(("g", l, br, 0))
                    sb_ = wait_chunk(("b", l, br))
                    wb = ring[:, sb_ * SLOT:(sb_ + 1) * SLOT].rearrange("p (k n) -> p k n", k=4)
                    for n in range(2):
                        wait_chunk(("g", l, br, n))
                        for tb in T:
                            project(("g", l, br, n), tb, ("g", l, br, n, tb))
                            b = begin("b", l, br, n, tb)
                            for k in range(4):
                                ins = mm(b[:, :], branch_T[br][:, k, tb * P:(tb + 1) * P], wb[:, k, n * CH:(n + 1) * CH],
                                         k == 0, k == 3)
                            ins.then_inc(mm_done, 1)
                for k, tb in enumerate(T):
                    pe.wait_ge(merged_ready, 2 * T_BEFORE[l] + nt + k + 1)
                    for half in range(2):
                        b = begin("mT", l, tb, half)
                        turn(b, merged[:, tb, half * 512:(half + 1) * 512], 4).then_inc(mm_done, 1)
                for n in range(2):
                    wait_chunk(("o", l, n))
                    for tb in T:
                        pe.wait_ge(act_took, TAKEN[("mT", l, tb, 1)])
                        project(("o", l, n), tb, ("o", l, n, tb))
                turn_rows(1, T)
                for tb in T:
                    pe.wait_ge(act_took, TAKEN[("hT", l, 1, tb, 1)])
                    b = begin("r", l, tb)
                    for k in range(KB):
                        ins = mm(b[:, 0:NE], hT[:, k, tb * P:(tb + 1) * P], wr[:, k, :], k == 0, k == KB - 1)
                    ins.then_inc(mm_done, 1)
                pe.wait_ge(sel_ready, l + 1)
                b = begin("cnt", l)
                sel = rt[:, 9, :].rearrange("p (t e) -> p t e", e=NE)
                for k in range(nt):
                    for k2 in range(k + 1):
                        mm(b[:, k * NE:(k + 1) * NE], tri if k2 == k else ones, sel[:, k2, :], k2 == 0, k2 == k)
                for k in range(nt):
                    ins = mm(b[:, 64:64 + NE], ones, sel[:, k, :], k == 0, k == nt - 1)
                ins.then_inc(mm_done, 1)

                pe.wait_ge(act_took, TAKEN[("r", l, T[-1])])
                pe.wait_ge(dve_took, TAKEN[("cnt", l)])
                Wb = l * PER_LAYER

                def turn_xs(e, par):
                    if isinstance(e, int):
                        pe.wait_ge(xs_loaded[par], 8 * Lb + 16 * (e // 2 + 1))
                    else:
                        pe.wait_ge(xs_loaded[par], (e - par) * 8 + (8 * Lb + 16))
                    if not (isinstance(e, int) and e == 0):
                        pe.wait_ge(h_done, e * 2 + (2 * Lb - 1))
                    for half in range(2):
                        turn(bank[2 + half], xs[:, par, half * 512:(half + 1) * 512], 4).then_inc(xt_mm, 1)

                def product(bk, hi, lo, e, p, par):
                    pe.wait_ge(lo_done, ready_at(e, p) + Wb)
                    i = position(e, p) % N_SPLIT
                    for k in range(4):
                        kk = 4 * (p % 2) + k
                        first = p % 2 == 0 and k == 0
                        mm(bk[:, :], hi[:, par, kk, :], w_hi[:, i, k, :], first, False)
                        mm(bk[:, :], hi[:, par, kk, :], w_lo[:, i, k, :], False, False)
                        ins = mm(bk[:, :], lo[:, par, kk, :], w_hi[:, i, k, :], False, p % 2 == 1 and k == 3)
                    ins.then_inc(w_used, 1)

                def gate_up(e, par):
                    pe.wait_ge(xt_lo, e * 2 + (2 * Lb + 2))
                    for p in range(8):
                        if p == 4 and not (isinstance(e, int) and e == 0):
                            pe.wait_ge(h_done, e * 2 + 2 * Lb)
                        product(bank[2 + p // 2], xsT_hi, xsT_lo, e, p, par)

                def down(e, par, n):
                    pe.wait_ge(ht_lo, e * 2 + (2 * Lb + 2))
                    if not (isinstance(e, int) and e + Lb == 0):
                        pe.wait_ge(ys_took, e * 2 + (2 * Lb - 2 + n + 1))
                    for p in (8 + 2 * n, 9 + 2 * n):
                        product(bank[n], hexpT_hi, hexpT_lo, e + 1, p, par)

                def turn_h(e):
                    for half in range(2):
                        pe.wait_ge(h_done, e * 2 + (2 * Lb + half + 1))
                        if not (isinstance(e, int) and e == 0):
                            pe.wait_ge(ht_lo, e * 2 + (2 * Lb - 2 + half + 1))
                        turn(bank[6 + half], hexp[:, half, :], 4).then_inc(ht_mm, 1)

                turn_xs(0, 0)
                gate_up(0, 0)
                turn_h(0)
                turn_xs(1, 1)

                def expert(e, par, last=False):
                    gate_up(e, par)
                    down(e - 1, 1 - par, 0)
                    turn_h(e)
                    if not last:
                        turn_xs(e + 1, 1 - par)
                    down(e - 1, 1 - par, 1)

                expert(1, 1)
                with pe.Fori(0, NE // 2 - 2) as i:
                    expert(i * 2 + 2, 0)
                    expert(i * 2 + 3, 1)
                expert(NE - 2, 0)
                expert(NE - 1, 1, last=True)
                down(NE - 1, 1, 0)
                down(NE - 1, 1, 1)
                pe.wait_ge(ys_took, 2 * (Lb + NE))
                o = over[l]
                pe.wait_ge(idx_ready, 2 * l + 2)
                busiest = pe.value_load(most[0:1, 0:1], min_val=0, max_val=512)
                with pe.If(busiest > P):
                    with pe.Fori(0, OVER_BLOCKS[l] * NE) as k:
                        pe.wait_ge(o["xs"], k * 16 + 16)
                        for half in range(2):
                            t = turn(bank[2 + half], xs[:, 0, half * 512:(half + 1) * 512], 4)
                        t.then_inc(o["xt"], 1)
                        pe.wait_ge(o["xe"], k + 1)
                        pe.wait_ge(o["w"], k * 96 + 96)
                        for c in range(4):
                            for kk in range(KB):
                                t = mm(bank[2 + c][:, :], over_xT[:, kk, :], slot(c)[:, kk, :], kk == 0, kk == KB - 1)
                        t.then_inc(o["gu"], 1)
                        pe.wait_ge(o["h"], k + 1)
                        for half in range(2):
                            t = turn(bank[6 + half], hexp[:, half, :], 4)
                        t.then_inc(o["ht"], 1)
                        pe.wait_ge(o["he"], k + 1)
                        for n in range(2):
                            for kk in range(KB):
                                t = mm(bank[n][:, :], over_hT[:, kk, :], slot(4 + n)[:, kk, :], kk == 0, kk == KB - 1)
                        t.then_inc(o["d"], 1)
                    pe.wait_ge(o["ys"], OVER_BLOCKS[l] * NE)


_INS = ['x', 'c', 'ctx', 'c_ctx', 'w_mod', 'b_mod', 'norm_mix', 'norm_ffn', 'w_in', 'attn_sink', 'conv_w', 'conv_b',
        'filt_w1', 'filt_b1', 'filt_freq', 'filt_w2', 'filt_b2', 'filt_w3', 'hyena_bias', 'w_branch_attn',
        'w_branch_fnet', 'w_branch_hyena', 'w_out', 'w_router', 'b_router', 'w_exp_gate', 'w_exp_up', 'w_exp_down',
        'norm_final']


def _constants():
    import math
    import numpy as np

    f32 = np.float32
    p = np.arange(128)
    const = np.zeros((128, C_END), f32)
    const[:, C_ID:C_ID + 128] = np.eye(128)
    const[:, C_TRI:C_TRI + 128] = p[:, None] < p[None, :]
    const[:, C_ONE:C_ONE + 128] = 1.0
    t = np.arange(256)
    f = np.arange(256)
    ang = 2 * np.pi * (np.outer(t, f) % 512) / 512
    cos, msin, alt = np.cos(ang), -np.sin(ang), (-1.0) ** t
    dft = np.zeros((256, 6, 128))
    dft[:, 0], dft[:, 1] = cos[:, :128], cos[:, 128:]
    dft[:, 2], dft[:, 3] = msin[:, :128], msin[:, 128:]
    dft[:, 4] = dft[:, 2]
    dft[:, 4, 0] = 0.0
    dft[:, 2, 0] = alt
    dft[:, 5] = dft[:, 0]
    dft[:, 5, 0] = alt
    const[:, C_DFT:C_INV] = dft.reshape(2, 128, 6 * 128).transpose(1, 0, 2).reshape(128, -1)
    inv = np.zeros((4, 128, 256))
    ci, si = 2 * cos.T / 512, 2 * msin.T / 512
    ci[0] /= 2
    si[0] = alt / 512
    inv[0], inv[1], inv[2], inv[3] = ci[:128], ci[128:], si[:128], si[128:]
    const[:, C_INV:C_ROPE] = inv.transpose(1, 0, 2).reshape(128, -1)
    freqs = (f32(10000.0) ** (-np.arange(16, dtype=f32) / f32(16))).astype(f32)
    rope = np.zeros((256, 4, 64))
    for half, pos in ((0, t // 64), (1, t % 64)):
        a = (pos.astype(f32)[:, None] * freqs).astype(f32).astype(np.float64)
        c = slice(32 * half, 32 * half + 32)
        rope[:, 2, c] = np.concatenate([np.cos(a), np.cos(a)], 1)
        rope[:, 3, c] = np.concatenate([-np.sin(a), np.sin(a)], 1)
    rope[:, 0:2] = rope[:, 2:4].astype(f32) * 0.125
    const[:, C_ROPE:C_MASK] = rope.reshape(2, 128, 256).transpose(1, 0, 2).reshape(128, -1)
    mask = np.zeros((256, 512))
    mask[:, :256] = np.where(np.abs(t[:, None] - t[None, :]) <= 128, 0.0, -1.0e30)
    const[:, C_MASK:C_EXP] = mask.reshape(2, 128, 512).transpose(1, 0, 2).reshape(128, -1)
    const[:, C_EXP:C_END] = np.tile(np.arange(16), 4)[None]
    an = 2 * np.pi * (np.outer(t, t) % 256) / 256
    ad = 2 * np.pi * (np.outer(p, p) % 128) / 128
    scale = 1.0 / math.sqrt(256 * 128)
    four = np.zeros((128, 1280))
    cs = np.concatenate([np.cos(an), np.sin(an)], 1)
    four[:, 0:512], four[:, 512:1024] = cs[:128], cs[128:]
    four[:, 1024:1152], four[:, 1152:1280] = np.cos(ad) * scale, -np.sin(ad) * scale
    pos = np.arange(256, dtype=f32)
    tt = pos / f32(255)
    omega = (f32(2.0 * math.pi) * pos / f32(256)).astype(f32)
    bands = np.linspace(1e-4, 15, 16, dtype=f32)
    arg = (omega[:, None] * bands).astype(f32)
    feats = np.concatenate([tt[:, None], np.cos(arg), -np.sin(arg)], -1).T
    deltas = np.abs(np.linspace(math.log(1e-2) / 1.5, math.log(1e-2) / 0.3, 512, dtype=f32))
    dec = np.exp(-tt[:, None] * deltas)
    decay = np.zeros((128, 3, 512), f32)
    decay[:, 0], decay[:, 1], decay[:, 2] = dec[:128], dec[128:], dec[:128]
    decay[0, 2] = 0.0
    tok = (np.arange(4)[None, :] * 128 + p[:, None]).astype(np.int32)
    return {"k_const": const, "k_four": four.astype(f32), "k_feats": np.ascontiguousarray(feats, f32),
            "k_decay": decay.reshape(128, -1), "k_tok": tok}


def kernel(**inputs):
    import numpy as _np
    import concourse.bacc as _bacc
    from concourse import mybir as _mybir
    from concourse.bass_utils import run_bass_kernel_spmd as _run

    nc = _bacc.Bacc("TRN2", target_bir_lowering=False, num_devices=1)
    arrays, aps = {}, {}
    for name in _INS:
        a = _np.ascontiguousarray(inputs[name])
        arrays[f"in_{name}_dram"] = a
        aps[name] = nc.dram_tensor(f"in_{name}_dram", a.shape, _mybir.dt.from_np(a.dtype), kind="ExternalInput").ap()
    for name, a in _constants().items():
        arrays[f"in_{name}_dram"] = a
        aps[name] = nc.dram_tensor(f"in_{name}_dram", a.shape, _mybir.dt.from_np(a.dtype), kind="ExternalInput").ap()
    out = nc.dram_tensor("out_0_dram", (1, SEQ, D), _mybir.dt.float32, kind="ExternalOutput").ap()
    hybrid_kernel(nc, aps, out)
    r = _run(nc, [arrays], core_ids=[0])
    return r.results[0]["out_0_dram"]
```

```python
from contextlib import ExitStack

import concourse.bass as bass
from concourse import mybir

F32 = mybir.dt.float32
F32R = mybir.dt.float32r
I32 = mybir.dt.int32
ALU = mybir.AluOpType
ACT = mybir.ActivationFunctionType
AX = mybir.AxisListType

P = 128
D = 1024
KB = D // P
SEQ = 256
DEPTH = 2
HD = 64
NH = 8
NKV = 2
NE = 16
EPS = 1e-6
HY = 512
CH = 512
SLOT = KB * CH
HALF = SLOT // 2
N_RAW, N_SPLIT = 6, 3
PER_EXPERT = 12
PER_LAYER = PER_EXPERT * NE
W_OFF = {"q": 0, "kv": 512, "f": 768, "v": 1280, "x1": 1792, "x2": 2304, "ga": 2816, "gf": 3840, "gh": 4864}
ROWS_PER_PART = 64
OVER_BLOCKS = [3, 1]
MAGIC = 12582912.0
TWO_PI = (6.28125, 0.0019350051879882812, 3.019915981956753e-07)
INV_2PI = 0.15915494309189535
PI = 3.1415925

C_ID, C_TRI, C_ONE = 0, 128, 256
C_DFT = 384
C_INV = C_DFT + 2 * 6 * P
C_ROPE = C_INV + 4 * SEQ
C_MASK = C_ROPE + 2 * 4 * HD
C_EXP = C_MASK + 2 * 512
C_END = C_EXP + 64
FR0, FR1, FI0, FI1, FIZ, FRN = range(6)


def tokens_of(l):
    return [0, 1, 2, 3] if l < DEPTH - 1 else [0, 1]


def plan_jobs(l):
    T = tokens_of(l)
    S = list(range(len(T) // 2))
    out = []

    def job(who, *name):
        out.append((name, who))

    for tb in range(4):
        for half in range(2):
            job("dve", "hT", l, 0, tb, half)
    for c in ("v", "x1", "x2"):
        for tb in T:
            job("act", "in", l, c, tb)
    for tb in T:
        job("dve", "in", l, "q", tb)
    for tb in range(4):
        job("dve", "in", l, "kv", tb)
    for tb in T:
        job("act", "in", l, "f", tb)
    for tb in range(4):
        job("act", "kT", l, tb)
    for tb in T:
        job("act", "qT", l, tb)
    for s in S:
        for g in range(5):
            if g < 4:
                job("act", "fp", l, s, g)
            if g > 0:
                job("act", "fy", l, s, g - 1)
    heads = [(tb, h) for tb in T for h in range(NH)]
    for i in range(len(heads) + 3):
        if i < len(heads):
            job("dve", "sc", l, *heads[i])
        if 2 <= i < len(heads) + 2:
            job("act", "pt", l, *heads[i - 2])
        if i >= 3:
            job("dve", "pv", l, *heads[i - 3])
            if heads[i - 3][1] == NH - 1 and heads[i - 3][0] > 0:
                job("act", "yaT", l, heads[i - 3][0] - 1)
    job("act", "yaT", l, T[-1])
    for o in range(2):
        for s in S:
            for b in (FR0, FI0, FR1, FI1):
                job("dve", "u", l, o, s, b)
        for s in S:
            for tt in range(2):
                job("dve", "c", l, o, s, tt)
    for tb in T:
        job("act", "yhT", l, tb)
    for br in range(3):
        for n in range(2):
            for tb in T:
                job("act", "g", l, br, n, tb)
        for n in range(2):
            for tb in T:
                job("dve", "b", l, br, n, tb)
    for tb in T:
        for half in range(2):
            job("dve", "mT", l, tb, half)
    for n in range(2):
        for tb in T:
            job("dve", "o", l, n, tb)
    for tb in T:
        for half in range(2):
            job("act", "hT", l, 1, tb, half)
    for tb in T:
        job("act", "r", l, tb)
    job("dve", "cnt", l)
    return out


def filter_jobs(l, g):
    taps = [[("f3", l, o, d, tt) for d in range(2) for tt in range(2)] for o in range(2)]
    spec = [[("fk", l, o, b) for b in range(5)] for o in range(2)]
    return [[("fl", l, 1)], [("fl", l, 2)], taps[0], [("fn", l, 0)], spec[0] + taps[1], [("fn", l, 1)], spec[1]][g]


FILTER_AFTER = [[1, 2, 3, 5, 6, 8, 9], [2, 3, 4, 5, 6, 7, 8]]
OPENING = []
for _l in range(DEPTH):
    for _c in range(12):
        OPENING.append(("mod", _l, _c))
        if _c in FILTER_AFTER[_l]:
            OPENING.append(("filter", _l, FILTER_AFTER[_l].index(_c)))


def hybrid_kernel(nc, A, out):
    jobs = []
    for kind, l, i in OPENING:
        jobs += [(n, "dve") for n in ([(kind, l, i)] if kind == "mod" else filter_jobs(l, i))]
    for l in range(DEPTH):
        jobs += plan_jobs(l)
    order = [n for n, _ in jobs]
    taker = dict(jobs)
    DONE = {n: i + 1 for i, n in enumerate(order)}
    TAKEN, seen = {}, {"act": 0, "dve": 0}
    for n in order:
        seen[taker[n]] += 1
        TAKEN[n] = seen[taker[n]]

    def w_in(l, name, n, cols):
        o = W_OFF[name] + n * CH
        return A["w_in"][l, :, o:o + cols].rearrange("(k p) n -> p k n", p=P)

    mix = []
    for l in range(DEPTH):
        for c in range(12):
            mix.append((("mod", l, c), A["w_mod"][l, :, c * CH:(c + 1) * CH].rearrange("(k p) n -> p k n", p=P),
                        ("mod", l, c)))
    layer_start = []
    for l in range(DEPTH):
        layer_start.append(len(mix))
        last = tokens_of(l)[-1]
        for c in ("v", "x1", "x2", "q", "kv", "f"):
            mix.append((("in", l, c), w_in(l, c, 0, 256 if c == "kv" else CH), ("in", l, c, 3 if c == "kv" else last)))
        for br, (g, wb) in enumerate((("ga", "w_branch_attn"), ("gf", "w_branch_fnet"), ("gh", "w_branch_hyena"))):
            mix.append((("g", l, br, 0), w_in(l, g, 0, CH), ("g", l, br, 0, last)))
            mix.append((("g", l, br, 1), w_in(l, g, 1, CH), ("g", l, br, 1, last)))
            mix.append((("b", l, br), A[wb][l].rearrange("(k p) n -> p k n", p=P), ("b", l, br, 1, last)))
        for n in range(2):
            mix.append((("o", l, n), A["w_out"][l, :, n * CH:(n + 1) * CH].rearrange("(k p) n -> p k n", p=P),
                        ("o", l, n, last)))
    slot_at, loads, base_loads, n_mix = {}, [0] * N_RAW, [], 0
    for l in range(DEPTH):
        until = layer_start[l + 1] if l + 1 < DEPTH else len(mix)
        for key, _, _ in mix[n_mix:until]:
            s = n_mix % 2 if key[0] == "mod" else (n_mix - layer_start[l]) % 2
            loads[2 * s] += 1
            loads[2 * s + 1] += 1
            slot_at[key] = (s, 16 * loads[2 * s])
            n_mix += 1
        base_loads.append(list(loads))
        loads = [x + PER_LAYER // N_RAW for x in loads]

    SPLIT = [(key, last) for key, _, last in mix if key[0] in ("mod", "in", "g", "b", "o")]
    SPLIT_NO = {key: i for i, (key, _) in enumerate(SPLIT)}

    ctx = ExitStack()
    with ctx:
        def sb(name, shape, dt=F32):
            return ctx.enter_context(nc.sbuf_tensor(name, shape, dt))

        def sem(name):
            return ctx.enter_context(nc.semaphore(name))

        bank = [ctx.enter_context(nc.psum_tensor(f"bank{i}", [P, 512], F32)) for i in range(8)]

        ring_at = -(-nc.sbuf_base // 32) * 32
        ring = sb("ring", [P, 6 * SLOT])
        x_at = -(-nc.sbuf_base // 32) * 32
        x = sb("x", [P, 4, D])
        hT_at = -(-nc.sbuf_base // 32) * 32
        hT = sb("hT", [P, KB, 512])
        work_at = -(-nc.sbuf_base // 32) * 32
        work = sb("work", [P, 8192])
        mixed_at = -(-nc.sbuf_base // 32) * 32
        mixed = sb("mixed", [P, 7168])
        const = sb("const", [P, C_END])
        ident = const[:, C_ID:C_ID + P]
        tri = const[:, C_TRI:C_TRI + P]
        ones = const[:, C_ONE:C_ONE + P]
        dft = const[:, C_DFT:C_INV].rearrange("p (t b m) -> p t b m", t=2, b=6)
        inv = const[:, C_INV:C_ROPE].rearrange("p (b m) -> p b m", b=4)
        rope = const[:, C_ROPE:C_MASK].rearrange("p (t j d) -> p t j d", t=2, j=4)
        mask = const[:, C_MASK:C_EXP].rearrange("p (t k) -> p t k", t=2)
        expert_id = const[:, C_EXP:C_END].rearrange("p (t e) -> p t e", t=4)

        M = 3 * SLOT

        def lent(a, n):
            return ring[:, M + a:M + a + n]

        z = lent(0, 6144).rearrange("p (t c n) -> p t c n", t=4, c=3)
        filt = lent(0, 2048).rearrange("p (d t n) -> p d t n", d=2, t=2)
        filt_pm = lent(2048, 2048).rearrange("p (d t n) -> p d t n", d=2, t=2)
        filt_abs = lent(4096, 2048).rearrange("p (d t n) -> p d t n", d=2, t=2)
        merged = lent(0, 4096).rearrange("p (t n) -> p t n", t=4)
        spectra = lent(6144, 5120).rearrange("p (o b n) -> p o b n", o=2, b=5)
        hstage = lent(6144, 1024).rearrange("p (i n) -> p i n", i=2)
        gate_buf = lent(8192, 4096).rearrange("p (t n) -> p t n", t=4)
        merge_tmp = lent(7168, 512)
        out_tmp = lent(7680, 512)
        hid = lent(11264, 1024).rearrange("p (i n) -> p i n", i=4)
        pq = lent(11264, 1024).rearrange("p (i n) -> p i n", i=2)
        hy_bias = lent(11264, 1024).rearrange("p (o n) -> p o n", o=2)
        x_flat = x[:, :, :].rearrange("p t n -> p (t n)")
        w3 = x_flat[0:64, 0:2048]
        w1 = x_flat[0:33, 2048:2112]
        w2 = x_flat[0:64, 2112:2176]
        feats = x_flat[0:33, 2304:2560]
        decay = x_flat[:, 2560:4096].rearrange("p (i n) -> p i n", i=3)
        mod_rows = [work[0:2, 0:6 * D], mixed[0:2, 0:6 * D]]
        zeros = work[0:4, 6144:6144 + 3 * HY]
        rnorm = mixed[:, 6144:6656]
        norm_rows = hT[0:2, :, :].rearrange("p k n -> p (k n)").rearrange("p (l i n) -> p l i n", l=2, i=2)

        A_bc = work[:, 0:2048].rearrange("p (s n) -> p s n", s=2)
        B_bc = work[:, 2048:4096].rearrange("p (s n) -> p s n", s=2)
        G_bc = work[:, 4096:6144].rearrange("p (s n) -> p s n", s=2)
        hrow = work[:, 6144:8192].rearrange("p (i n) -> p i n", i=2)
        four = work[:, 0:1280]
        S_buf = work[:, 0:1024].rearrange("p (i n) -> p i n", i=2)
        P_buf = work[:, 1024:2048].rearrange("p (i n) -> p i n", i=2)
        PT = work[:, 2048:3072].rearrange("p (i k n) -> p i k n", i=2, k=4)
        ya = work[:, 3072:4096].rearrange("p (i n) -> p i n", i=2)
        stage = work[:, 0:3072].rearrange("p (i j n) -> p i j n", i=2, j=3)
        Yspec = work[:, 0:4096].rearrange("p (s b n) -> p s b n", s=2, b=4)
        hy_tmp = work[:, 4096:5120].rearrange("p (i n) -> p i n", i=2)
        rope_tmp = work[:, 4096:5120].rearrange("p (i n) -> p i n", i=2)
        krow = work[:, 5120:5632].rearrange("p (t n) -> p t n", t=4)
        conv_w = mixed[:, 5120:7168].rearrange("p (j n) -> p j n", j=4)
        qrow = work[:, 6144:8192].rearrange("p (t n) -> p t n", t=4)
        got_a = lent(0, 4096).rearrange("p (i n) -> p i n", i=4)
        got_b = lent(4096, 4096).rearrange("p (i n) -> p i n", i=4)

        qT = mixed[:, 0:2048].rearrange("p (j n) -> p j n", j=4)
        yhT = mixed[:, 0:2048].rearrange("p (j n) -> p j n", j=4)
        kT = mixed[:, 2048:2560]
        vrow = mixed[:, 2560:3072].rearrange("p (t n) -> p t n", t=4)
        yaT = mixed[:, 3072:5120].rearrange("p (j n) -> p j n", j=4)
        frow = mixed[:, 3072:5120].rearrange("p (t n) -> p t n", t=4)
        yfT = mixed[:, 5120:7168].rearrange("p (j n) -> p j n", j=4)
        branch_T = [yaT, yfT, yhT]
        xs = mixed[:, 0:2048].rearrange("p (i n) -> p i n", i=2)
        silu = mixed[:, 4096:5120].rearrange("p (i n) -> p i n", i=2)
        hexp = mixed[:, 5120:6144].rearrange("p (i n) -> p i n", i=2)
        hT_flat = hT[:, :, :].rearrange("p k n -> p (k n)")
        ys = work[:, 2048:4096].rearrange("p (i n) -> p i n", i=2)
        over_xT = work[:, 0:1024].rearrange("p (k n) -> p k n", k=KB)
        over_hT = hT_flat[:, 0:1024].rearrange("p (k n) -> p k n", k=KB)

        def parts(name, shape, at):
            return nc.alloc_sbuf_tensor_at(name, shape, F32R, offset=at)

        w_hi = parts("w_hi", [P, N_SPLIT, HALF], ring_at + 4 * M)
        w_lo = parts("w_lo", [P, N_SPLIT, HALF], ring_at + 4 * (M + N_SPLIT * HALF))
        hexpT_hi = parts("hexpT_hi", [P, 2, KB, P], hT_at)
        hexpT_lo = parts("hexpT_lo", [P, 2, KB, P], hT_at + 4 * 2048)
        xsT_hi = parts("xsT_hi", [P, 2, KB, P], mixed_at + 4 * 2048)
        xsT_lo = parts("xsT_lo", [P, 2, KB, P], work_at)
        final_w = mixed[:, 2048:3072]
        final_rows = mixed[:, 0:2048].rearrange("p (i n) -> p i n", i=2)

        m_hi = parts("m_hi", [P, 4, 2 * CH], ring_at + 4 * 2 * SLOT)
        m_lo = parts("m_lo", [P, 2 * SLOT], ring_at)
        hT_hi = parts("hT_hi", [P, KB, 512], hT_at)
        hT_lo = parts("hT_lo", [P, 4, KB, P], x_at)
        branch_hi = parts("branch_hi", [P, 4, 512], ring_at + 4 * (M + 4096))
        branch_lo = [parts(f"branch_lo{br}", [P, 4, 512], mixed_at + 4 * at) for br, at in enumerate((3072, 5120, 0))]
        mT_lo = parts("mT_lo", [P, 4, KB, P], ring_at + 4 * M)

        c_raw_at = -(-nc.sbuf_base // 32) * 32
        c_raw = sb("c_raw", [P, KB, 2])
        c_act_at = -(-nc.sbuf_base // 32) * 32
        c_act = sb("c_act", [P, KB, 2])
        c_hi = parts("c_hi", [P, KB, 2], c_raw_at)
        c_lo = parts("c_lo", [P, KB, 2], c_act_at)
        wr = sb("wr", [P, KB, NE])
        br_bc = sb("br_bc", [P, NE])
        sink = sb("sink", [P, DEPTH, NH])
        fcol = sb("fcol", [64, DEPTH, 3])
        stat = sb("stat", [P, 5, 4])
        att = sb("att", [P, 2, 6, NH])
        rt = mixed[:, 6144:7168].rearrange("p (i n) -> p i n", i=16)
        rt4 = sb("rt4", [P, 8, 16])
        rt1 = sb("rt1", [P, 8, 4])
        w_tok = sb("w_tok", [P, 2, 4])
        idx_tok = sb("idx_tok", [P, 2, 4], I32)
        tok_id = sb("tok_id", [P, 4], I32)
        idx_exp = sb("idx_exp", [P, NE], I32)
        idx_over = sb("idx_over", [P, 1], I32)
        zero_i = work[:, 7680:7680 + ROWS_PER_PART].bitcast(I32)
        most = sb("most", [P, 1], I32)
        pace = fcol[:, 0, 0:2]
        idx_beyond = c_act[:, 0:4, :].rearrange("p k s -> p (k s)").rearrange("p (i t) -> p i t", i=2).bitcast(I32)
        spec_dram = nc.dram_tensor("spec_dram", (DEPTH, P, 2 * 5 * HY), F32, kind="Internal").ap()
        x_dram = nc.dram_tensor("x_dram", (P * 2, D), F32, kind="Internal").ap()
        mod_dram = nc.dram_tensor("mod_dram", (DEPTH, 2, 6, D), F32, kind="Internal").ap()
        hp_dram = nc.dram_tensor("hp_dram", (DEPTH * 2, SEQ + 2, 3 * HY), F32, kind="Internal").ap()
        ys_dram = nc.dram_tensor("ys_dram", (P * NE, D), F32, kind="Internal").ap()
        ys_over = [nc.dram_tensor(f"ys_over{l}", (P * NE * OVER_BLOCKS[l], D), F32, kind="Internal").ap()
                   for l in range(DEPTH)]
        h2_of = [nc.dram_tensor(f"h2_dram{l}", (P * len(tokens_of(l)), D), F32, kind="Internal").ap() for l in range(DEPTH)]
        row_tok_of = [nc.dram_tensor(f"row_tok{l}", (P * ROWS_PER_PART, 1), I32, kind="Internal").ap()
                      for l in range(DEPTH)]

        slot_loaded = [sem(f"slot_loaded{i}") for i in range(6)]
        const_loaded = sem("const_loaded")
        small_loaded = sem("small_loaded")
        c_loaded = sem("c_loaded")
        c_ready = sem("c_ready")
        c_low = sem("c_low")
        mm_done = sem("mm_done")
        act_took = sem("act_took")
        dve_took = sem("dve_took")
        dve_step = sem("dve_step")
        act_step = sem("act_step")
        mod_stored = sem("mod_stored")
        zero_ready = sem("zero_ready")
        zero_stored = sem("zero_stored")
        ab_loaded = sem("ab_loaded")
        g_loaded = sem("g_loaded")
        squared = sem("squared")
        scaled = sem("scaled")
        var_ready = sem("var_ready")
        root_ready = sem("root_ready")
        rows_ready = sem("rows_ready")
        filt_loaded = sem("filt_loaded")
        four_loaded = sem("four_loaded")
        bias_loaded = sem("bias_loaded")
        sin_in = sem("sin_in")
        spec_stored = sem("spec_stored")
        spec_loaded = sem("spec_loaded")
        x_loaded = sem("x_loaded")
        x_stored = sem("x_stored")
        split_hi = sem("split_hi")
        split_lo = sem("split_lo")
        split_used = sem("split_used")
        hT_high = sem("hT_high")
        mT_high = sem("mT_high")
        branch_high = sem("branch_high")
        branch_low = sem("branch_low")
        sin_out = sem("sin_out")
        abs_ready = sem("abs_ready")
        pm_ready = sem("pm_ready")
        hp_stored = [sem(f"hp_stored{i}") for i in range(2)]
        max_ready = sem("max_ready")
        exp_done = sem("exp_done")
        sink_in = sem("sink_in")
        sink_exp = sem("sink_exp")
        ya_ready = sem("ya_ready")
        convw_loaded = sem("convw_loaded")
        stage_loaded = [sem(f"stage_loaded{i}") for i in range(2)]
        conv_done = sem("conv_done")
        spec_ready = sem("spec_ready")
        y_ready = sem("y_ready")
        merged_ready = sem("merged_ready")
        h2_stored = [sem(f"h2_stored{i}") for i in range(2)]
        sel_ready = sem("sel_ready")
        idx_ready = sem("idx_ready")
        scattered = sem("scattered")
        idx_loaded = sem("idx_loaded")
        xs_loaded = [sem(f"xs_loaded{i}") for i in range(2)]
        xt_mm = sem("xt_mm")
        xt_hi = sem("xt_hi")
        xt_lo = sem("xt_lo")
        hi_done = sem("hi_done")
        lo_done = sem("lo_done")
        w_used = sem("w_used")
        silu_done = sem("silu_done")
        h_done = sem("h_done")
        ht_mm = sem("ht_mm")
        ht_hi = sem("ht_hi")
        ht_lo = sem("ht_lo")
        ys_took = sem("ys_took")
        ys_stored = [sem(f"ys_stored{i}") for i in range(2)]
        got_loaded = [sem(f"got_loaded{i}") for i in range(4)]
        got_ready = sem("got_ready")
        combined = sem("combined")
        final_loaded = sem("final_loaded")
        final_ready = sem("final_ready")
        out_stored = sem("out_stored")
        over = [{n: sem(f"over{l}_{n}") for n in ("w", "idx", "xs", "xt", "xe", "gu", "s", "h", "ht", "he", "d", "ys",
                                                  "st", "got", "pace")} for l in range(DEPTH)]

        ctx.enter_context(nc.allow_non_contiguous_dma(reason="small vectors laid along the partitions"))
        block = ctx.enter_context(nc.Block())

        T_BEFORE = [0, 4]
        ROWS_AT = {(0, 0): 0, (0, 1): 4, (1, 0): 8, (1, 1): 12}
        N_SMALL = 16 * 9

        def expert_w(l, name, e, n):
            w = A[name]
            if isinstance(e, int):
                return w[l, e, :, n * CH:(n + 1) * CH].rearrange("(k p) n -> p k n", p=P)
            return w[l, bass.ds(e, 1), :, n * CH:(n + 1) * CH].rearrange("o (k p) n -> p (o k) n", p=P)

        def slot(s, cols=CH):
            return ring[:, s * SLOT:s * SLOT + KB * cols].rearrange("p (k n) -> p k n", k=KB)

        def quarter_w(l, name, e, q):
            rows = slice(2 * P * q, 2 * P * (q + 1))
            if isinstance(e, int):
                return A[name][l, e, rows, :].rearrange("(p k) n -> p (k n)", k=2)
            return A[name][l, bass.ds(e, 1), rows, :].rearrange("o (p k) n -> p (o k n)", k=2)

        def quarter(key, q):
            cols = 256 if key[0] == "in" and key[2] == "kv" else CH
            at = slot_at[key][0] * SLOT + q * 2 * cols
            return slice(at, at + 2 * cols), 2 * cols

        def raw(i):
            return ring[:, i * HALF:(i + 1) * HALF]

        EXPERT_CHUNKS = (("w_exp_gate", 0), ("w_exp_up", 0), ("w_exp_gate", 1), ("w_exp_up", 1),
                         ("w_exp_down", 0), ("w_exp_down", 1))
        EXPERT_W = ("w_exp_gate", "w_exp_up", "w_exp_down")

        def ready_at(e, p):
            if isinstance(e, int):
                p = p - 8 if e == NE else p
                return (PER_EXPERT * e - 4 if e else 0) + p + 1
            return e * PER_EXPERT + (p - 3)

        def position(e, p):
            if isinstance(e, int) and e == 0:
                return p
            return (p + 2 - (8 if isinstance(e, int) and e == NE else 0)) % N_RAW

        def turns(e):
            return 8 if isinstance(e, int) and e == 0 else PER_EXPERT

        @block.sync
        def _(sp):
            owner = [None] * N_RAW

            def wait_place(i):
                if owner[i] is not None:
                    sp.wait_ge(owner[i][0], owner[i][1])

            def conv_loads(l, c):
                T = tokens_of(l)
                i = 3 * T_BEFORE[l] + c * len(T)
                for b in range(2):
                    sp.wait_ge(hp_stored[b], 16 * (i + len(T)) // 2)
                if c > 0:
                    sp.wait_ge(conv_done, i)
                elif l == 0:
                    sp.wait_ge(mod_stored, 16 * DEPTH)
                sp.dma_start(conv_w[:, 0:3, :], A["conv_w"][l, :, c * HY:(c + 1) * HY].partition_broadcast(P))\
                    .then_inc(convw_loaded, 16)
                sp.dma_start(conv_w[:, 3, :], A["conv_b"][l, c * HY:(c + 1) * HY].partition_broadcast(P))\
                    .then_inc(convw_loaded, 16)
                for tb in T:
                    if i >= 2:
                        sp.wait_ge(conv_done, i - 1)
                    for j in range(3):
                        r = (tb % 2) * P + j
                        sp.dma_start(stage[:, i % 2, j, :], hp_dram[2 * l + tb // 2, r:r + P, c * HY:(c + 1) * HY])\
                            .then_inc(stage_loaded[i % 2], 16)
                    i += 1

            n = 0
            for l in range(DEPTH):
                until = layer_start[l + 1] if l + 1 < DEPTH else len(mix)
                while n < until:
                    key, src, last = mix[n]
                    s = slot_at[key][0]
                    if key[0] == "b":
                        dst = ring[:, s * SLOT:(s + 1) * SLOT].rearrange("p (k n) -> p k n", k=4)
                    else:
                        dst = slot(s, src.shape[-1])
                    k2 = src.shape[1] // 2
                    for half in range(2):
                        wait_place(2 * s + half)
                        part = slice(half * k2, (half + 1) * k2)
                        sp.dma_start(dst[:, part, :], src[:, part, :]).then_inc(slot_loaded[2 * s + half], 16)
                        owner[2 * s + half] = (mm_done, DONE[last])
                    if key in SPLIT_NO and src.shape[-1] >= CH:
                        owner[2 * s] = (split_used, 3 * SPLIT_NO[key] + 2)
                    if n == 1:
                        sp.dma_start(const[:, :], A["k_const"]).then_inc(const_loaded, 16)
                    n += 1
                    if key[0] == "in" and key[2] in ("x2", "q", "kv"):
                        conv_loads(key[1], ("x2", "q", "kv").index(key[2]))
                def load(e, p):
                    i = position(e, p) % N_RAW
                    if isinstance(e, int) and e == 0 and p < N_RAW:
                        wait_place(i)
                        if i // 2 == 2:
                            sp.wait_ge(mm_done, DONE[("o", l, 1, tokens_of(l)[-1])])
                    else:
                        sp.wait_ge(lo_done, ready_at(e, p) + (l * PER_LAYER - N_RAW))
                    sp.dma_start(raw(i), quarter_w(l, EXPERT_W[p // 4], e if p < 8 else e - 1, p % 4))\
                        .then_inc(slot_loaded[i], 16)

                def turn(e):
                    for p in range(turns(e)):
                        load(e, p)

                turn(0)
                turn(1)
                with sp.Fori(2, NE) as e:
                    turn(e)
                for p in range(8, PER_EXPERT):
                    load(NE, p)
                for i in range(N_RAW):
                    owner[i] = (lo_done, (l + 1) * PER_LAYER - N_RAW + i + 1)
                o = over[l]
                sp.wait_ge(idx_ready, 2 * l + 2)
                busiest = sp.value_load(most[0:1, 0:1], min_val=0, max_val=512)
                with sp.If(busiest > P):
                    sp.wait_ge(w_used, (l + 1) * PER_LAYER)

                    def load_all(e, done):
                        if done is not None:
                            sp.wait_ge(o["d"], done)
                        for c, (name, half) in enumerate(EXPERT_CHUNKS):
                            sp.dma_start(slot(c), expert_w(l, name, e, half)).then_inc(o["w"], 16)

                    load_all(0, None)
                    with sp.Fori(1, NE) as e:
                        load_all(e, e)
                    if OVER_BLOCKS[l] > 1:
                        with sp.Fori(1, OVER_BLOCKS[l]) as b:
                            with sp.Fori(0, NE) as e:
                                load_all(e, b * NE + e)
                    sp.wait_ge(o["d"], NE * OVER_BLOCKS[l])
            sp.wait_ge(final_ready, 1)
            sp.dma_start(out[0, 0:P, :], final_rows[:, 0, :]).then_inc(out_stored, 16)
            sp.wait_ge(final_ready, 2)
            sp.dma_start(out[0, P:2 * P, :], final_rows[:, 1, :]).then_inc(out_stored, 16)
            sp.wait_ge(out_stored, 32)

        @block.gpsimd
        def _(pool):
            def rows_of(l, j):
                return mod_dram[l, :, j, :].partition_broadcast(P)

            small = [
                (mod_rows[0], A["b_mod"][0].partition_broadcast(2)),
                (mod_rows[1], A["b_mod"][1].partition_broadcast(2)),
                (norm_rows[:, :, 0, :], A["norm_mix"].partition_broadcast(2)),
                (norm_rows[:, :, 1, :], A["norm_ffn"].partition_broadcast(2)),
                (wr[:, :, :], A["w_router"].rearrange("(k p) e -> p k e", p=P)),
                (br_bc[:, :], A["b_router"].partition_broadcast(P)),
                (sink[:, :, :], A["attn_sink"].partition_broadcast(P)),
                (tok_id[:, :], A["k_tok"]),
                (fcol[:, :, 0], A["filt_b1"].rearrange("l h -> h l")),
            ]
            for dst, src in small:
                pool.dma_start(dst, src).then_inc(small_loaded, 16)
            pool.dma_start(fcol[:, :, 1], A["filt_freq"].rearrange("l h -> h l")).then_inc(filt_loaded, 16)
            pool.dma_start(fcol[:, :, 2], A["filt_b2"].rearrange("l h -> h l")).then_inc(filt_loaded, 16)
            pool.memset(zeros, 0.0).then_inc(zero_ready, 1)
            pool.memset(zero_i, 0).then_inc(zero_ready, 1)
            pool.wait_ge(zero_ready, 2)
            for r in (0, SEQ + 1):
                pool.dma_start(hp_dram[:, r, :], zeros).then_inc(zero_stored, 16)
            for l in range(DEPTH):
                pool.dma_start(row_tok_of[l].rearrange("(p m) o -> p (m o)", p=P), zero_i).then_inc(zero_stored, 16)
            pool.wait_ge(zero_stored, 16 * 4)
            for l in range(DEPTH):
                if l > 0:
                    pool.wait_ge(dve_took, TAKEN[("f3", l - 1, 1, 1, 1)])
                for dst, src in ((w1, A["filt_w1"][l]), (w2, A["filt_w2"][l]), (w3, A["filt_w3"][l]),
                                 (feats, A["k_feats"]), (decay, A["k_decay"].rearrange("p (i n) -> p i n", i=3))):
                    pool.dma_start(dst, src).then_inc(filt_loaded, 16)
                if l == 1:
                    pool.dma_start(B_bc, rows_of(0, 0)).then_inc(ab_loaded, 16)
                    pool.dma_start(A_bc, rows_of(0, 1)).then_inc(ab_loaded, 16)
                for o in range(2):
                    pool.wait_ge(dve_took, TAKEN[("fk", l, o, 4)])
                    pool.dma_start(spec_dram[l, :, o * 5 * HY:(o + 1) * 5 * HY],
                                   spectra[:, o, :, :].rearrange("p b n -> p (b n)")).then_inc(spec_stored, 16)
                if l == DEPTH - 1:
                    pool.dma_start(x[:, 0:2, :], A["x"][0].rearrange("(t p) n -> p t n", p=P)).then_inc(x_loaded, 16)
                    pool.dma_start(x[:, 2:4, :], A["ctx"][0].rearrange("(t p) n -> p t n", p=P)).then_inc(x_loaded, 16)
                pool.wait_ge(dve_took, TAKEN[("mod", l, 11)])
                pool.dma_start(mod_dram[l].rearrange("s j n -> s (j n)"), mod_rows[l]).then_inc(mod_stored, 16)
                pool.wait_ge(mod_stored, 16 * (l + 1))

            for l in range(DEPTH):
                T = tokens_of(l)
                Lb = NE * l
                if l > 0:
                    pool.dma_start(B_bc, rows_of(l, 0)).then_inc(ab_loaded, 16)
                    pool.dma_start(A_bc, rows_of(l, 1)).then_inc(ab_loaded, 16)
                pool.wait_ge(conv_done, 3 * (T_BEFORE[l] + len(T)))
                pool.dma_start(four, A["k_four"]).then_inc(four_loaded, 16)
                pool.dma_start(spectra.rearrange("p o b n -> p (o b n)"), spec_dram[l]).then_inc(spec_loaded, 16)
                pool.wait_ge(mm_done, DONE[("fy", l, len(T) // 2 - 1, 3)])
                pool.dma_start(hy_bias, A["hyena_bias"][l].partition_broadcast(P)).then_inc(bias_loaded, 16)
                pool.wait_ge(y_ready, 2 * (T_BEFORE[l] + len(T)))
                pool.dma_start(G_bc, rows_of(l, 2)).then_inc(g_loaded, 16)
                pool.wait_ge(mm_done, DONE[("c", l, 1, len(T) // 2 - 1, 1)])
                pool.dma_start(B_bc, rows_of(l, 3)).then_inc(ab_loaded, 16)
                pool.dma_start(A_bc, rows_of(l, 4)).then_inc(ab_loaded, 16)
                pool.wait_ge(mm_done, DONE[("g", l, 2, 1, T[-1])])
                x_src = A["x"][0] if l == 0 else x_dram
                pool.dma_start(x[:, 0:2, :], x_src.rearrange("(t p) n -> p t n", p=P)).then_inc(x_loaded, 16)
                if len(T) > 2:
                    pool.dma_start(x[:, 2:4, :], A["ctx"][0].rearrange("(t p) n -> p t n", p=P)).then_inc(x_loaded, 16)
                pool.wait_ge(dve_took, TAKEN[("o", l, 1, T[-1])])
                pool.dma_start(G_bc, rows_of(l, 5)).then_inc(g_loaded, 16)
                for k, tb in enumerate(T):
                    pool.wait_ge(rows_ready, ROWS_AT[l, 1] + k + 1)
                    pool.dma_start(h2_of[l][tb * P:(tb + 1) * P, :], hrow[:, k % 2, :]).then_inc(h2_stored[k % 2], 16)
                pool.wait_ge(idx_ready, 2 * l + 2)
                for tb in T:
                    for i2 in range(2):
                        pool.indirect_dma_start(row_tok_of[l][:, :], bass.IndirectOffsetOnAxis(ap=idx_tok[:, i2, tb:tb + 1], axis=0),
                                                tok_id[:, tb:tb + 1], None).then_inc(scattered, 16)
                pool.wait_ge(scattered, 16 * 2 * (T_BEFORE[l] + len(T)))
                m_over = NE * OVER_BLOCKS[l]
                first_rows = row_tok_of[l][0:P * NE, :].rearrange("(p m) o -> p (m o)", p=P)
                over_rows = row_tok_of[l][P * NE:P * (NE + m_over), :].rearrange("(p m) o -> p (m o)", p=P)
                pool.dma_start(idx_exp[:, :], first_rows).then_inc(idx_loaded, 16)
                pool.wait_ge(idx_loaded, 16 * (l + 1))
                for b in range(2):
                    pool.wait_ge(h2_stored[b], 16 * (T_BEFORE[l] + len(T)) // 2)
                ys_rows = ys_dram.rearrange("(p m) n -> p m n", p=P)
                ys_beyond = ys_over[l].rearrange("(p m) n -> p m n", p=P)
                for e in range(NE + 2):
                    if e < NE:
                        if e >= 2:
                            pool.wait_ge(xt_mm, 2 * (Lb + e - 1))
                        pool.indirect_dma_start(xs[:, e % 2, :], None, h2_of[l][:, :],
                                                bass.IndirectOffsetOnAxis(ap=idx_exp[:, e:e + 1], axis=0))\
                            .then_inc(xs_loaded[e % 2], 16)
                    if e >= 2:
                        pool.wait_ge(ys_took, 2 * (Lb + e - 1))
                        pool.dma_start(ys_rows[:, e - 2, :], ys[:, e % 2, :]).then_inc(ys_stored[e % 2], 16)
                for b in range(2):
                    pool.wait_ge(ys_stored[b], 8 * (Lb + NE))
                o = over[l]
                busiest = pool.value_load(most[0:1, 0:1], min_val=0, max_val=512)
                with pool.If(busiest > P):
                    nc.gpsimd.tensor_tensor(pace, pace, pace, ALU.subtract).then_inc(o["pace"], 1)
                    with pool.Fori(0, OVER_BLOCKS[l]) as b:
                        with pool.Fori(0, NE) as e:
                            k = pool.snap(b * NE + e)
                            pool.dma_start(idx_over[:, :], over_rows[:, bass.ds(k, 1)]).then_inc(o["idx"], 16)
                            pool.wait_ge(o["idx"], k * 16 + 16)
                            pool.wait_ge(o["pace"], k * 2 + 1)
                            nc.gpsimd.tensor_tensor(pace, pace, pace, ALU.subtract).then_inc(o["pace"], 1)
                            pool.indirect_dma_start(xs[:, 0, :], None, h2_of[l][:, :],
                                                    bass.IndirectOffsetOnAxis(ap=idx_over[:, 0:1], axis=0))\
                                .then_inc(o["xs"], 16)
                            pool.wait_ge(o["ys"], k + 1)
                            pool.wait_ge(o["pace"], k * 2 + 2)
                            nc.gpsimd.tensor_tensor(pace, pace, pace, ALU.subtract).then_inc(o["pace"], 1)
                            pool.dma_start(ys_beyond[:, bass.ds(k, 1), :].rearrange("p o n -> p (o n)"), ys[:, 0, :])\
                                .then_inc(o["st"], 16)
                            pool.wait_ge(o["st"], k * 16 + 16)
                    pool.wait_ge(o["pace"], 2 * m_over + 1)
                for k, tb in enumerate(T):
                    for i2, got in ((0, got_a), (1, got_b)):
                        pool.indirect_dma_start(got[:, k, :], None, ys_dram[:, :],
                                                bass.IndirectOffsetOnAxis(ap=idx_tok[:, i2, tb:tb + 1], axis=0),
                                                bounds_check=P * NE - 1, oob_is_err=False).then_inc(got_loaded[k], 16)
                with pool.If(busiest > P):
                    for k, tb in enumerate(T):
                        pool.wait_ge(got_loaded[k], 32 * (l + 1))
                        for i2, got in ((0, got_a), (1, got_b)):
                            pool.indirect_dma_start(got[:, k, :], None, ys_over[l][:, :],
                                                    bass.IndirectOffsetOnAxis(ap=idx_beyond[:, i2, tb:tb + 1], axis=0),
                                                    bounds_check=P * m_over - 1, oob_is_err=False).then_inc(o["got"], 16)
                    pool.wait_ge(o["got"], 32 * len(T))
                nc.gpsimd.tensor_tensor(pace, pace, pace, ALU.subtract).then_inc(got_ready, 1)
                pool.wait_ge(got_ready, l + 1)
                if l + 1 < DEPTH:
                    for tb in range(2):
                        pool.wait_ge(combined, tb + 1)
                        pool.dma_start(x_dram[tb * P:(tb + 1) * P, :], x[:, tb, :]).then_inc(x_stored, 16)
                    pool.wait_ge(x_stored, 32)
            pool.dma_start(final_w, A["norm_final"].partition_broadcast(P)).then_inc(final_loaded, 16)
            pool.wait_ge(final_loaded, 16)

        @block.scalar
        def _(act):
            took = [0]

            def take(name):
                assert taker[name] == "act" and TAKEN[name] == took[0] + 1, name
                took[0] += 1
                act.wait_ge(mm_done, DONE[name])
                return bank[(DONE[name] - 1) % 8]

            act.dma_start(c_raw[:, :, 0], A["c"].rearrange("o (k p) -> p (o k)", p=P)).then_inc(c_loaded, 16)
            act.dma_start(c_raw[:, :, 1], A["c_ctx"].rearrange("(k p) -> p k", p=P)).then_inc(c_loaded, 16)
            act.wait_ge(c_loaded, 32)
            nc.scalar.activation(c_act[:, :, :], c_raw[:, :, :], ACT.Silu).then_inc(c_ready, 1)
            act.wait_ge(c_ready, 1)
            nc.scalar.activation(c_hi[:, :, :], c_act[:, :, :], ACT.Copy).then_inc(c_ready, 1)

            SQUARES = [0, 4, 8, 12, 14]

            def squares(ph, tbs, ready):
                for k, tb in enumerate(tbs):
                    ready(k)
                    if k >= 2:
                        act.wait_ge(squared, SQUARES[ph] + k - 1)
                    nc.scalar.activation(hrow[:, k % 2, :], x[:, tb, :], ACT.Square,
                                         accum_out=stat[:, 0, k:k + 1]).then_inc(squared, 1)

            def root(ph, nt):
                act.wait_ge(var_ready, ph + 1)
                nc.scalar.activation(stat[:, 2, 0:nt], stat[:, 1, 0:nt], ACT.Sqrt).then_inc(root_ready, 1)

            def split_high(key):
                c = SPLIT_NO[key]
                s, v = slot_at[key]
                for q in range(4):
                    act.wait_ge(slot_loaded[2 * s + q // 2], v)
                    if c:
                        if q < 3:
                            act.wait_ge(split_used, 3 * (c - 1) + q + 1)
                        else:
                            act.wait_ge(mm_done, DONE[SPLIT[c - 1][1]])
                    cols, n = quarter(key, q)
                    nc.scalar.activation(m_hi[:, q, 0:n], ring[:, cols], ACT.Copy).then_inc(split_hi, 1)
                    yield

            def high_parts(l, tb, half, name, out_sem):
                act.wait_ge(mm_done, DONE[name])
                b = bank[(DONE[name] - 1) % 8]
                nc.scalar.activation(hT_hi[:, 4 * half:4 * half + 4, tb * P:(tb + 1) * P],
                                     b[:, :].rearrange("p (k n) -> p k n", k=4), ACT.Copy).then_inc(out_sem, 1)

            def transposed(l, ph, tbs):
                for tb in tbs:
                    for half in range(2):
                        b = take(("hT", l, ph, tb, half))
                        nc.scalar.activation(hT[:, 4 * half:4 * half + 4, tb * P:(tb + 1) * P],
                                             b[:, :].rearrange("p (k n) -> p k n", k=4), ACT.Copy)\
                            .then_inc(act_took, 1)

            def filter_step(l, g):
                if g < 2:
                    act.wait_ge(sin_in, 2 * l + g + 1)
                    nc.scalar.activation(hid[0:64, 2 + g, :], hid[0:64, 0, :], ACT.Sin).then_inc(sin_out, 1)
                if g in (2, 4):
                    o = g // 4
                    if o:
                        act.wait_ge(mm_done, DONE[("fn", l, 0)])
                    for d in range(2):
                        for tt in range(2):
                            act.wait_ge(dve_took, TAKEN[("f3", l, o, d, tt)])
                            nc.scalar.activation(filt_abs[:, d, tt, :], filt[:, d, tt, :], ACT.Abs).then_inc(abs_ready, 1)

            for _ in split_high(("mod", 0, 0)):
                pass
            for kind, l, i in OPENING:
                if kind == "filter":
                    filter_step(l, i)
                elif (l, i) == (DEPTH - 1, 11):
                    root(0, 4)
                    for _ in split_high(("in", 0, "v")):
                        pass
                else:
                    if (l, i) == (DEPTH - 1, 10):
                        squares(0, range(4), lambda k: act.wait_ge(x_loaded, 32))
                    for _ in split_high(("mod", l, i + 1) if i < 11 else ("mod", l + 1, 0)):
                        pass

            for l in range(DEPTH):
                T = tokens_of(l)
                Lb = NE * l
                if l:
                    squares(2 * l, range(4), lambda k: act.wait_ge(combined, T_BEFORE[l - 1] + k + 1))
                    root(2 * l, 4)
                for tb in range(4):
                    for half in range(2):
                        high_parts(l, tb, half, ("hT", l, 0, tb, half), hT_high)
                i = 3 * T_BEFORE[l]
                for c, name in enumerate(("v", "x1", "x2")):
                    ahead = split_high(("in", l, ("x1", "x2", "q")[c]))
                    for _ in range(3):
                        next(ahead)
                    for k, tb in enumerate(T):
                        if k == len(T) // 2:
                            next(ahead)
                        b = take(("in", l, name, tb))
                        if i >= 2:
                            act.wait_ge(hp_stored[i % 2], 16 * (i // 2))
                        nc.scalar.activation(hstage[:, i % 2, :], b[:, :], ACT.Copy).then_inc(act_took, 1)
                        act.wait_ge(act_took, took[0])
                        r = 1 + (tb % 2) * P
                        act.dma_start(hp_dram[2 * l + tb // 2, r:r + P, c * HY:(c + 1) * HY], hstage[:, i % 2, :])\
                            .then_inc(hp_stored[i % 2], 16)
                        i += 1
                for name in ("kv", "f"):
                    for _ in split_high(("in", l, name)):
                        pass
                ahead = split_high(("g", l, 0, 0))
                for _ in range(3):
                    next(ahead)
                for k, tb in enumerate(T):
                    if k == len(T) // 2:
                        next(ahead)
                    b = take(("in", l, "f", tb))
                    nc.scalar.activation(frow[:, tb, :], b[:, :], ACT.Copy).then_inc(act_took, 1)
                for tb in range(4):
                    b = take(("kT", l, tb))
                    nc.scalar.activation(kT[:, tb * P:(tb + 1) * P], b[:, 0:P], ACT.Copy).then_inc(act_took, 1)
                for tb in T:
                    b = take(("qT", l, tb))
                    nc.scalar.activation(qT[:, :, tb * P:(tb + 1) * P], b[:, :].rearrange("p (j n) -> p j n", j=4),
                                         ACT.Copy).then_inc(act_took, 1)
                for s in range(len(T) // 2):
                    for g in range(5):
                        if g < 4:
                            b = take(("fp", l, s, g))
                            nc.scalar.activation(pq[:, g % 2, :], b[:, :], ACT.Copy).then_inc(act_took, 1)
                        if g > 0:
                            b = take(("fy", l, s, g - 1))
                            nc.scalar.activation(yfT[:, g - 1, s * SEQ:(s + 1) * SEQ], b[:, 0:SEQ], ACT.Copy)\
                                .then_inc(act_took, 1)
                heads = [(tb, h) for tb in T for h in range(NH)]
                hb = 8 * T_BEFORE[l]
                for i in range(len(heads) + 3):
                    if i < len(heads):
                        tb, h = heads[i]
                        nk = 512 if tb < 2 else 256
                        act.wait_ge(max_ready, hb + i + 1)
                        if i >= 2:
                            act.wait_ge(mm_done, DONE[("pt", l, *heads[i - 2])])
                        k = i // NH
                        if h == 0 and k >= 2:
                            act.wait_ge(ya_ready, T_BEFORE[l] + k - 1)
                        nc.scalar.activation(P_buf[:, i % 2, 0:nk], S_buf[:, i % 2, 0:nk], ACT.Exp,
                                             bias=att[:, k % 2, 1, h:h + 1], accum_out=att[:, k % 2, 2, h:h + 1]).then_inc(exp_done, 1)
                        if h == NH - 1:
                            act.wait_ge(sink_in, T_BEFORE[l] + i // NH + 1)
                            nc.scalar.activation(att[:, k % 2, 4, :], att[:, k % 2, 3, :], ACT.Exp).then_inc(sink_exp, 1)
                    if 2 <= i < len(heads) + 2:
                        tb, h = heads[i - 2]
                        nk = 4 if tb < 2 else 2
                        b = take(("pt", l, tb, h))
                        nc.scalar.activation(PT[:, i % 2, 0:nk, :], b[:, 0:nk * P].rearrange("p (k n) -> p k n", k=nk),
                                             ACT.Copy).then_inc(act_took, 1)
                    if i >= 3 and heads[i - 3][1] == NH - 1 and heads[i - 3][0] > 0:
                        tb = heads[i - 3][0] - 1
                        b = take(("yaT", l, tb))
                        nc.scalar.activation(yaT[:, :, tb * P:(tb + 1) * P], b[:, :].rearrange("p (j n) -> p j n", j=4),
                                             ACT.Copy).then_inc(act_took, 1)
                b = take(("yaT", l, T[-1]))
                nc.scalar.activation(yaT[:, :, T[-1] * P:(T[-1] + 1) * P], b[:, :].rearrange("p (j n) -> p j n", j=4),
                                     ACT.Copy).then_inc(act_took, 1)
                for tb in T:
                    b = take(("yhT", l, tb))
                    nc.scalar.activation(yhT[:, :, tb * P:(tb + 1) * P], b[:, :].rearrange("p (j n) -> p j n", j=4),
                                         ACT.Copy).then_inc(act_took, 1)
                for br in range(3):
                    for n in range(2):
                        if n == 0:
                            for _ in split_high(("g", l, br, 1)):
                                pass
                        if br and n == 0:
                            act.wait_ge(dve_took, TAKEN[("b", l, br - 1, 1, T[-1])])
                        for tb in T:
                            b = take(("g", l, br, n, tb))
                            nc.scalar.activation(gate_buf[:, tb, n * CH:(n + 1) * CH], b[:, :], ACT.Sigmoid)\
                                .then_inc(act_took, 1)
                        if n == 0:
                            w = len(T) * P
                            if br:
                                act.wait_ge(mm_done, DONE[("b", l, br - 1, 1, T[-1])])
                            else:
                                act.wait_ge(act_took, TAKEN[("yhT", l, T[-1])])
                            nc.scalar.activation(branch_hi[:, :, 0:w], branch_T[br][:, :, 0:w], ACT.Copy)\
                                .then_inc(branch_high, 1)
                            for _ in split_high(("b", l, br)):
                                pass
                    for _ in split_high(("g", l, br + 1, 0) if br < 2 else ("o", l, 0)):
                        pass
                for tb in T:
                    for half in range(2):
                        high_parts(l, tb, half, ("mT", l, tb, half), mT_high)
                for _ in split_high(("o", l, 1)):
                    pass
                squares(2 * l + 1, T, lambda k: act.wait_ge(dve_took, TAKEN[("o", l, 1, T[k])]))
                root(2 * l + 1, len(T))
                transposed(l, 1, T)
                for tb in T:
                    b = take(("r", l, tb))
                    nc.scalar.activation(rt[:, 0, tb * NE:(tb + 1) * NE], b[:, 0:NE], ACT.Sigmoid).then_inc(act_took, 1)

                loaded = base_loads[l]
                Wb = l * PER_LAYER

                def high(e, p):
                    pos = position(e, p)
                    i = pos % N_RAW
                    if isinstance(e, int):
                        n = ready_at(e, p) - 1
                        act.wait_ge(slot_loaded[i], 16 * (loaded[i] + n // N_RAW + 1))
                    else:
                        act.wait_ge(slot_loaded[i], e * 32 + 16 * (loaded[i] + (p - 4 - i) // N_RAW + 1))
                    if isinstance(e, int) and ready_at(e, p) <= N_SPLIT:
                        act.wait_ge(dve_took, TAKEN[("o", l, 1, T[-1])])
                    else:
                        act.wait_ge(w_used, ready_at(e, p) + (Wb - N_SPLIT))
                    nc.scalar.activation(w_hi[:, pos % N_SPLIT, :], raw(i), ACT.Copy).then_inc(hi_done, 1)

                def take_xs(e, par):
                    for half in range(2):
                        act.wait_ge(xt_mm, e * 2 + (2 * Lb + half + 1))
                        nc.scalar.activation(xsT_hi[:, par, 4 * half:4 * half + 4, :],
                                             bank[2 + half][:, :].rearrange("p (k n) -> p k n", k=4), ACT.Copy)\
                            .then_inc(xt_hi, 1)

                def gate(e):
                    act.wait_ge(w_used, ready_at(e, 3) + Wb)
                    if not (isinstance(e, int) and e + Lb == 0):
                        act.wait_ge(h_done, e * 2 + 2 * Lb)
                    for n in range(2):
                        nc.scalar.activation(silu[:, n, :], bank[2 + 2 * n][:, :], ACT.Silu).then_inc(silu_done, 1)

                def expert(e, par):
                    for p in range(turns(e)):
                        if p + 2 < turns(e):
                            high(e, p + 2)
                        else:
                            high_next(e, p + 2 - turns(e))
                        if p == 4:
                            gate(e)
                        if p == min(9, turns(e) - 1):
                            for half in range(2):
                                act.wait_ge(ht_mm, e * 2 + (2 * Lb + half + 1))
                                nc.scalar.activation(hexpT_hi[:, par, 4 * half:4 * half + 4, :],
                                                     bank[6 + half][:, :].rearrange("p (k n) -> p k n", k=4), ACT.Copy)\
                                    .then_inc(ht_hi, 1)
                            if not (isinstance(e, int) and e == NE - 1):
                                take_xs(e + 1, 1 - par)

                def high_next(e, p):
                    if isinstance(e, int) and e == NE - 1:
                        high(NE, 8 + p)
                    else:
                        high(e + 1, p)

                take_xs(0, 0)
                high(0, 0)
                high(0, 1)
                expert(0, 0)
                expert(1, 1)
                with act.Fori(1, NE // 2 - 1) as i:
                    expert(i * 2, 0)
                    expert(i * 2 + 1, 1)
                expert(NE - 2, 0)
                expert(NE - 1, 1)
                high(NE, 10)
                high(NE, 11)
                o = over[l]
                act.wait_ge(idx_ready, 2 * l + 2)
                busiest = act.value_load(most[0:1, 0:1], min_val=0, max_val=512)
                with act.If(busiest > P):
                    with act.Fori(0, OVER_BLOCKS[l] * NE) as k:
                        act.wait_ge(o["xt"], k + 1)
                        for half in range(2):
                            t = nc.scalar.activation(over_xT[:, 4 * half:4 * half + 4, :],
                                                     bank[2 + half][:, :].rearrange("p (k n) -> p k n", k=4), ACT.Copy)
                        t.then_inc(o["xe"], 1)
                        act.wait_ge(o["gu"], k + 1)
                        for n in range(2):
                            t = nc.scalar.activation(silu[:, n, :], bank[2 + 2 * n][:, :], ACT.Silu)
                        t.then_inc(o["s"], 1)
                        act.wait_ge(o["ht"], k + 1)
                        for half in range(2):
                            t = nc.scalar.activation(over_hT[:, 4 * half:4 * half + 4, :],
                                                     bank[6 + half][:, :].rearrange("p (k n) -> p k n", k=4), ACT.Copy)
                        t.then_inc(o["he"], 1)
                    act.wait_ge(o["d"], OVER_BLOCKS[l] * NE)
                if l + 1 < DEPTH:
                    act.wait_ge(lo_done, (l + 1) * PER_LAYER)
                    for _ in split_high(("in", l + 1, "v")):
                        pass
                act.wait_ge(got_ready, l + 1)
                for k, tb in enumerate(T):
                    act.wait_ge(got_loaded[k], 32 * (l + 1))
                    nc.scalar.activation(got_a[:, k, :], got_a[:, k, :], ACT.Copy, scale=w_tok[:, 0, k:k + 1])\
                        .then_inc(scaled, 1)
            squares(4, range(2), lambda k: act.wait_ge(combined, T_BEFORE[1] + k + 1))
            root(4, 2)

        @block.vector
        def _(dve):
            steps = [0]
            took = [0]

            def link(ins):
                steps[0] += 1
                ins.then_inc(dve_step, 1)
                dve.wait_ge(dve_step, steps[0])

            def take(name):
                assert taker[name] == "dve" and TAKEN[name] == took[0] + 1, name
                took[0] += 1
                dve.wait_ge(mm_done, DONE[name])
                return bank[(DONE[name] - 1) % 8]

            def TT(o, a, b, op):
                return nc.vector.tensor_tensor(o, a, b, op)

            dve.wait_ge(c_ready, 2)
            TT(c_lo[:, :, :], c_act[:, :, :], c_hi[:, :, :].bitcast(F32), ALU.subtract).then_inc(c_low, 1)


            def modulation(l, c):
                take_row = take(("mod", l, c))
                row = mod_rows[l][:, c * CH:(c + 1) * CH]
                TT(row, take_row[0:2, :], row, ALU.add).then_inc(dve_took, 1)
                dve.wait_ge(dve_took, took[0])
                if c in (2, 3, 8, 9):
                    link(nc.vector.scalar_tensor_tensor(out=row, in0=row, scalar=1.0,
                                                        in1=norm_rows[:, l, c // 6, (c % 2) * CH:(c % 2 + 1) * CH],
                                                        op0=ALU.add, op1=ALU.mult))

            def hidden_layer(l, n):
                b = take(("fl", l, n + 1))
                h0, h1 = hid[0:64, 0, :], hid[0:64, 1, :]
                if n == 0:
                    dve.wait_ge(filt_loaded, 16 * (7 + 5 * l))
                nc.vector.tensor_scalar(h0, b[0:64, 0:SEQ], fcol[:, l, 2 * n:2 * n + 1], fcol[:, l, 1:2],
                                        ALU.add, ALU.mult).then_inc(dve_took, 1)
                dve.wait_ge(dve_took, took[0])
                link(nc.vector.tensor_scalar(h1, h0, INV_2PI, MAGIC, ALU.mult, ALU.add))
                link(nc.vector.tensor_scalar(h1, h1, -MAGIC, None, ALU.add))
                for part in TWO_PI:
                    link(nc.vector.scalar_tensor_tensor(out=h0, in0=h1, scalar=-part, in1=h0, op0=ALU.mult,
                                                        op1=ALU.add))
                nc.vector.tensor_scalar(h0, h0, PI, -PI, ALU.min, ALU.max).then_inc(sin_in, 1)
                dve.wait_ge(sin_out, 2 * l + n + 1)

            def taps(l, o):
                if o or l:
                    dve.wait_ge(abs_ready, 8 * l + 4 * o)
                    dve.wait_ge(mm_done, DONE[("fk", l - 1 + o, 1 - o, 4)])
                for d in range(2):
                    for tt in range(2):
                        b = take(("f3", l, o, d, tt))
                        TT(filt[:, d, tt, :], b[:, :], decay[:, 2 if (d == 1 and tt == 0) else tt, :], ALU.mult)\
                            .then_inc(dve_took, 1)
                        dve.wait_ge(dve_took, took[0])
                for tt in range(2):
                    link(TT(filt_pm[:, 0, tt, :], filt[:, 0, tt, :], filt[:, 1, tt, :], ALU.add))
                    ins = TT(filt_pm[:, 1, tt, :], filt[:, 0, tt, :], filt[:, 1, tt, :], ALU.subtract)
                    link(ins) if tt == 0 else ins.then_inc(pm_ready, 1)
                dve.wait_ge(pm_ready, 2 * l + o + 1)

            def tap_norm(l, o):
                b = take(("fn", l, o))
                nc.vector.reciprocal(rnorm, b[:, :]).then_inc(dve_took, 1)
                dve.wait_ge(dve_took, took[0])

            def tap_spectra(l, o):
                if l:
                    dve.wait_ge(spec_stored, 16 * (o + 1))
                for k in range(5):
                    b = take(("fk", l, o, k))
                    TT(spectra[:, o, k, :], b[:, :], rnorm, ALU.mult).then_inc(dve_took, 1)
                    dve.wait_ge(dve_took, took[0])

            def filter_step(l, g):
                if g < 2:
                    hidden_layer(l, g)
                elif g == 2:
                    taps(l, 0)
                elif g in (3, 5):
                    tap_norm(l, g // 4)
                elif g == 4:
                    tap_spectra(l, 0)
                    taps(l, 1)
                else:
                    tap_spectra(l, 1)

            def inverse_rms(ph, tbs):
                nt = len(tbs)
                dve.wait_ge(squared, [4, 8, 12, 14, 16][ph])
                nc.vector.tensor_scalar(stat[:, 1, 0:nt], stat[:, 0, 0:nt], 1.0 / D, EPS, ALU.mult, ALU.add)\
                    .then_inc(var_ready, 1)
                dve.wait_ge(root_ready, ph + 1)
                link(nc.vector.reciprocal(stat[:, 3, 0:nt], stat[:, 2, 0:nt]))
                link(TT(stat[:, 4, 0:nt], stat[:, 3, 0:nt], stat[:, 3, 0:nt], ALU.mult))
                link(TT(stat[:, 4, 0:nt], stat[:, 4, 0:nt], stat[:, 1, 0:nt], ALU.mult))
                link(nc.vector.tensor_scalar(stat[:, 4, 0:nt], stat[:, 4, 0:nt], -0.5, 1.5, ALU.mult, ALU.add))
                link(TT(stat[:, 3, 0:nt], stat[:, 3, 0:nt], stat[:, 4, 0:nt], ALU.mult))

            def split_low(key):
                for q in range(4):
                    dve.wait_ge(split_hi, 4 * SPLIT_NO[key] + q + 1)
                    cols, n = quarter(key, q)
                    TT(m_lo[:, cols], ring[:, cols], m_hi[:, q, 0:n].bitcast(F32), ALU.subtract).then_inc(split_lo, 1)
                    yield

            for _ in split_low(("mod", 0, 0)):
                pass
            dve.wait_ge(small_loaded, N_SMALL)
            for kind, l, i in OPENING:
                if kind == "filter":
                    filter_step(l, i)
                    continue
                if (l, i) != (DEPTH - 1, 11):
                    for _ in split_low(("mod", l, i + 1) if i < 11 else ("mod", l + 1, 0)):
                        pass
                else:
                    inverse_rms(0, range(4))
                modulation(l, i)

            def low_parts(l, tb, half, name, lo, in_sem, v):
                b = take(name)
                dve.wait_ge(in_sem, v)
                TT(lo[:, tb, 4 * half:4 * half + 4, :], b[:, :].rearrange("p (k n) -> p k n", k=4),
                   hT_hi[:, 4 * half:4 * half + 4, tb * P:(tb + 1) * P].bitcast(F32), ALU.subtract).then_inc(dve_took, 1)

            def low_rows(l, tb):
                if l and tb < 2:
                    dve.wait_ge(x_stored, 16 * (tb + 1))
                for half in range(2):
                    low_parts(l, tb, half, ("hT", l, 0, tb, half), hT_lo, hT_high, 8 * l + 2 * tb + half + 1)

            def norm(l, p, tbs):
                ph = 2 * l + p
                if ph:
                    inverse_rms(ph, tbs)
                dve.wait_ge(ab_loaded, 32 * (ph + 1))
                for k, tb in enumerate(tbs):
                    if k >= 2:
                        dve.wait_ge(mm_done, DONE[("hT", l, p, tbs[k - 2], 1)])
                        if p == 1:
                            dve.wait_ge(h2_stored[k % 2], 16 * (T_BEFORE[l] // 2 + k // 2))
                    link(nc.vector.scalar_tensor_tensor(out=hrow[:, k % 2, :], in0=x[:, tb, :], scalar=stat[:, 3, k:k + 1],
                                                        in1=A_bc[:, tb // 2, :], op0=ALU.mult, op1=ALU.mult))
                    TT(hrow[:, k % 2, :], hrow[:, k % 2, :], B_bc[:, tb // 2, :], ALU.add).then_inc(rows_ready, 1)
                    if ph == 0 and k == 1:
                        for _ in split_low(("in", 0, "v")):
                            pass
                    if p == 0 and k >= 2:
                        low_rows(l, tbs[k - 2])
                if p == 0:
                    low_rows(l, 2)
                    low_rows(l, 3)

            def rotate(src, tb, nh, j, dst):
                w = nh * HD
                cos = rope[:, tb, 2 * j, :].unsqueeze(1).broadcast_to([P, nh, HD])
                sin = rope[:, tb, 2 * j + 1, :].rearrange("p (a b i) -> p a b i", a=2, b=2)
                t0 = rope_tmp[:, 0, 0:w].rearrange("p (h d) -> p h d", h=nh)
                t1 = rope_tmp[:, 1, 0:w].rearrange("p (h a b i) -> p h a b i", h=nh, a=2, b=2)
                s5 = src.rearrange("p (h a b i) -> p h a b i", h=nh, a=2, b=2)
                TT(t0, src.rearrange("p (h d) -> p h d", h=nh), cos, ALU.mult).then_inc(dve_step, 1)
                for b in range(2):
                    TT(t1[:, :, :, b, :], s5[:, :, :, 1 - b, :],
                       sin[:, :, b, :].unsqueeze(1).broadcast_to([P, nh, 2, 16]), ALU.mult).then_inc(dve_step, 1)
                steps[0] += 3
                dve.wait_ge(dve_step, steps[0])
                if nh == NH:
                    a = rope_tmp[:, 0, :].rearrange("p (g j d) -> p g j d", g=2, j=4)
                    b2 = rope_tmp[:, 1, :].rearrange("p (g j d) -> p g j d", g=2, j=4)
                    return TT(dst.rearrange("p (j g d) -> p g j d", g=2, j=4), a, b2, ALU.add)
                return TT(dst, rope_tmp[:, 0, 0:w], rope_tmp[:, 1, 0:w], ALU.add)

            dve.wait_ge(const_loaded, 16)
            for l in range(DEPTH):
                T = tokens_of(l)
                nt = len(T)

                def convolve(c, key):
                    i = 3 * T_BEFORE[l] + c * nt
                    low = split_low(key)
                    dve.wait_ge(convw_loaded, 32 * (3 * l + c + 1))
                    for tb in T:
                        dve.wait_ge(stage_loaded[i % 2], 48 * (i // 2 + 1))
                        st = stage[:, i % 2, :, :]
                        link(TT(st, st, conv_w[:, 0:3, :], ALU.mult))
                        zt = z[:, tb, c, :]
                        link(TT(zt, st[:, 0, :], st[:, 1, :], ALU.add))
                        link(TT(zt, zt, st[:, 2, :], ALU.add))
                        TT(zt, zt, conv_w[:, 3, :], ALU.add).then_inc(conv_done, 1)
                        i += 1
                        for _ in range(4 // nt):
                            next(low)
                    dve.wait_ge(conv_done, i)

                Lb = NE * l
                norm(l, 0, range(4))
                for _ in split_low(("in", l, "x1")):
                    pass
                convolve(0, ("in", l, "x2"))
                convolve(1, ("in", l, "q"))
                convolve(2, ("in", l, "kv"))
                low = split_low(("in", l, "f"))
                for k, tb in enumerate(T):
                    b = take(("in", l, "q", tb))
                    if k == 0:
                        dve.wait_ge(mm_done, DONE[("hT", l, 0, 3, 1)])
                    if tb < 2:
                        rotate(b[:, :], tb, NH, 0, qrow[:, tb, :]).then_inc(dve_took, 1)
                        dve.wait_ge(dve_took, took[0])
                    else:
                        nc.vector.tensor_scalar(qrow[:, tb, :].rearrange("p (j g d) -> p g j d", g=2, j=4),
                                                b[:, :].rearrange("p (g j d) -> p g j d", g=2, j=4),
                                                HD ** -0.5, None, ALU.mult).then_inc(dve_took, 1)
                        dve.wait_ge(dve_took, took[0])
                    for _ in range(4 // nt):
                        next(low)
                for tb in range(4):
                    b = take(("in", l, "kv", tb))
                    link(nc.vector.tensor_copy(vrow[:, tb, :], b[:, P:2 * P]))
                    kdst = krow[:, tb, :]
                    if tb < 2:
                        rotate(b[:, 0:P], tb, NKV, 1, kdst).then_inc(dve_took, 1)
                        dve.wait_ge(dve_took, took[0])
                    else:
                        nc.vector.tensor_copy(kdst, b[:, 0:P]).then_inc(dve_took, 1)
                        dve.wait_ge(dve_took, took[0])
                for _ in split_low(("g", l, 0, 0)):
                    pass
                heads = [(tb, h) for tb in T for h in range(NH)]
                hb = NH * T_BEFORE[l]
                dve.wait_ge(mm_done, DONE[("fy", l, nt // 2 - 1, 3)])

                def finish_block(tb, i):
                    n = T_BEFORE[l] + i
                    dve.wait_ge(sink_exp, n + 1)
                    dve.wait_ge(exp_done, NH * (n + 1))
                    link(TT(att[:, i % 2, 5, :], att[:, i % 2, 2, :], att[:, i % 2, 4, :], ALU.add))
                    link(nc.vector.reciprocal(att[:, i % 2, 5, :], att[:, i % 2, 5, :]))
                    dve.wait_ge(dve_took, took[0])
                    y3 = ya[:, i % 2, :].rearrange("p (h d) -> p h d", h=NH)
                    TT(y3, y3, att[:, i % 2, 5, :].unsqueeze(2).broadcast_to([P, NH, HD]), ALU.mult).then_inc(ya_ready, 1)

                for i in range(len(heads) + 3):
                    if i < len(heads):
                        tb, h = heads[i]
                        nk = 512 if tb < 2 else 256
                        b = take(("sc", l, tb, h))
                        if i >= 2:
                            dve.wait_ge(exp_done, hb + i - 1)
                        m = mask[:, tb, :] if tb < 2 else mask[:, 0, 256:512]
                        nc.vector.tensor_tensor_reduce(S_buf[:, i % 2, 0:nk], b[:, 0:nk], m, 1.0, -3.0e38, ALU.add,
                                                       ALU.max, att[:, i // NH % 2, 0, h:h + 1]).then_inc(dve_took, 1)
                        dve.wait_ge(dve_took, took[0])
                        nc.vector.tensor_scalar(att[:, i // NH % 2, 1, h:h + 1], att[:, i // NH % 2, 0, h:h + 1], sink[:, l, h:h + 1], -1.0,
                                                ALU.max, ALU.mult).then_inc(max_ready, 1)
                        if h == NH - 1:
                            dve.wait_ge(max_ready, hb + i + 1)
                            TT(att[:, i // NH % 2, 3, :], att[:, i // NH % 2, 1, :], sink[:, l, :], ALU.add).then_inc(sink_in, 1)
                    if i >= 3:
                        tb, h = heads[i - 3]
                        k = (i - 3) // NH
                        if h == 0 and k >= 2:
                            dve.wait_ge(mm_done, DONE[("yaT", l, T[k - 2])])
                        b = take(("pv", l, tb, h))
                        nc.vector.tensor_copy(ya[:, k % 2, h * HD:(h + 1) * HD], b[:, 0:HD]).then_inc(dve_took, 1)
                        dve.wait_ge(dve_took, took[0])
                        if h == NH - 1:
                            finish_block(tb, k)
                dve.wait_ge(bias_loaded, 16 * (l + 1))
                dve.wait_ge(spec_loaded, 16 * (l + 1))
                dve.wait_ge(mm_done, DONE[("yaT", l, T[-1])])
                for o in range(2):
                    for s in range(nt // 2):
                        for half in range(2):
                            re, im = spectra[:, o, half, :], spectra[:, o, 2 + half, :]
                            re2 = spectra[:, o, 4 if half == 0 else 1, :]
                            ur = take(("u", l, o, s, (FR0, FR1)[half]))
                            if half == 0 and o:
                                dve.wait_ge(mm_done, DONE[("c", l, 0, s, 1)])
                            yr, yi = Yspec[:, s, half, :], Yspec[:, s, 2 + half, :]
                            link(TT(yr, ur[:, :], re, ALU.mult))
                            TT(yi, ur[:, :], im, ALU.mult).then_inc(dve_took, 1)
                            dve.wait_ge(dve_took, took[0])
                            ui = take(("u", l, o, s, (FI0, FI1)[half]))
                            link(TT(hy_tmp[:, 0, :], ui[:, :], im, ALU.mult))
                            TT(hy_tmp[:, 1, :], ui[:, :], re2, ALU.mult).then_inc(dve_took, 1)
                            dve.wait_ge(dve_took, took[0])
                            link(TT(yr, yr, hy_tmp[:, 0, :], ALU.subtract))
                            TT(yi, yi, hy_tmp[:, 1, :], ALU.add).then_inc(spec_ready, 1)
                            dve.wait_ge(spec_ready, 2 * (o * (nt // 2) + s) + half + 1 + 2 * T_BEFORE[l])
                    for s in range(nt // 2):
                        for tt in range(2):
                            tb = 2 * s + tt
                            y = z[:, tb, 0, :]
                            link(TT(hy_tmp[:, tt, :], y, hy_bias[:, o, :], ALU.mult))
                            b = take(("c", l, o, s, tt))
                            TT(hy_tmp[:, tt, :], b[:, :], hy_tmp[:, tt, :], ALU.add).then_inc(dve_took, 1)
                            dve.wait_ge(dve_took, took[0])
                            TT(y, hy_tmp[:, tt, :], z[:, tb, 1 + o, :], ALU.mult).then_inc(y_ready, 1)
                        dve.wait_ge(y_ready, 2 * T_BEFORE[l] + o * nt + 2 * (s + 1))
                for br in range(3):
                    for _ in split_low(("g", l, br, 1)):
                        pass
                    w = nt * P
                    dve.wait_ge(branch_high, 3 * l + br + 1)
                    TT(branch_lo[br][:, :, 0:w], branch_T[br][:, :, 0:w], branch_hi[:, :, 0:w].bitcast(F32),
                       ALU.subtract).then_inc(branch_low, 1)
                    for _ in split_low(("b", l, br)):
                        pass
                    low = split_low(("g", l, br + 1, 0) if br < 2 else ("o", l, 0))
                    for n in range(2):
                        if n:
                            for _ in range(3):
                                next(low)
                        for tb in T:
                            if n and tb == 1:
                                next(low)
                            b = take(("b", l, br, n, tb))
                            g = ("g", l, br, n, tb)
                            dve.wait_ge(act_took, TAKEN[g])
                            gb = gate_buf[:, tb, n * CH:(n + 1) * CH]
                            m = merged[:, tb, n * CH:(n + 1) * CH]
                            if br == 0:
                                TT(m, b[:, :], gb, ALU.mult).then_inc(dve_took, 1)
                                dve.wait_ge(dve_took, took[0])
                                continue
                            TT(merge_tmp, b[:, :], gb, ALU.mult).then_inc(dve_took, 1)
                            dve.wait_ge(dve_took, took[0])
                            ins = TT(m, m, merge_tmp, ALU.add)
                            if br == 1:
                                link(ins)
                            else:
                                ins.then_inc(merged_ready, 1)
                                dve.wait_ge(merged_ready, 2 * T_BEFORE[l] + n * nt + T.index(tb) + 1)
                for tb in T:
                    for half in range(2):
                        low_parts(l, tb, half, ("mT", l, tb, half), mT_lo, mT_high, 2 * T_BEFORE[l] + 2 * tb + half + 1)
                for _ in split_low(("o", l, 1)):
                    pass
                dve.wait_ge(g_loaded, 16 * (2 * l + 1))
                dve.wait_ge(x_loaded, (64, 80)[l])
                for n in range(2):
                    for tb in T:
                        b = take(("o", l, n, tb))
                        link(TT(out_tmp, b[:, :], G_bc[:, tb // 2, n * CH:(n + 1) * CH], ALU.mult))
                        xt = x[:, tb, n * CH:(n + 1) * CH]
                        TT(xt, xt, out_tmp, ALU.add).then_inc(dve_took, 1)
                        dve.wait_ge(dve_took, took[0])
                norm(l, 1, T)
                w16 = nt * NE
                dve.wait_ge(act_took, TAKEN[("r", l, T[-1])])

                def r(i):
                    return rt[:, i, 0:w16]

                def r4(i):
                    return r(i).rearrange("p (q i) -> p q i", i=4)

                def r16(i):
                    return r(i).rearrange("p (t e) -> p t e", e=NE)

                def beats(val, res, k):
                    for j in range(4):
                        if j < 3:
                            link(TT(res[j][:, :, j + 1:4], val[:, :, j:j + 1].broadcast_to([P, k, 3 - j]),
                                    val[:, :, j + 1:4], ALU.is_ge))
                        if j > 0:
                            link(TT(res[j][:, :, 0:j], val[:, :, j:j + 1].broadcast_to([P, k, j]), val[:, :, 0:j],
                                    ALU.is_gt))

                link(nc.vector.memset(rt[:, 2:6, :], 0.0))
                link(nc.vector.memset(rt4[:, 1:5, :], 0.0))
                link(TT(r16(1), r16(0), br_bc[:, :].unsqueeze(1).broadcast_to([P, nt, NE]), ALU.add))
                beats(r4(1), [r4(2 + j) for j in range(4)], nt * 4)
                link(TT(r(6), r(2), r(3), ALU.add))
                link(TT(r(6), r(6), r(4), ALU.add))
                link(TT(r(6), r(6), r(5), ALU.add))
                link(nc.vector.tensor_scalar(r(7), r(6), 2.0, None, ALU.is_lt))
                link(TT(r(8), r(1), r(7), ALU.mult))
                gs = rt4[:, 0, 0:nt * 4]
                link(nc.vector.tensor_reduce(gs, r4(8), AX.X, ALU.add))

                def q4(i):
                    return rt4[:, i, 0:nt * 4].rearrange("p (t g) -> p t g", g=4)

                beats(q4(0), [q4(1 + j) for j in range(4)], nt)
                link(TT(rt4[:, 5, 0:nt * 4], rt4[:, 1, 0:nt * 4], rt4[:, 2, 0:nt * 4], ALU.add))
                link(TT(rt4[:, 5, 0:nt * 4], rt4[:, 5, 0:nt * 4], rt4[:, 3, 0:nt * 4], ALU.add))
                link(TT(rt4[:, 5, 0:nt * 4], rt4[:, 5, 0:nt * 4], rt4[:, 4, 0:nt * 4], ALU.add))
                link(nc.vector.tensor_scalar(rt4[:, 6, 0:nt * 4], rt4[:, 5, 0:nt * 4], 1.0, None, ALU.is_lt))
                TT(r4(9), r4(7), rt4[:, 6, 0:nt * 4].unsqueeze(2).broadcast_to([P, nt * 4, 4]), ALU.mult)\
                    .then_inc(sel_ready, 1)
                dve.wait_ge(sel_ready, l + 1)
                link(TT(r(10), r(0), r(9), ALU.mult))
                link(nc.vector.tensor_reduce(rt1[:, 0, 0:nt], r16(10), AX.X, ALU.add))
                link(nc.vector.reciprocal(rt1[:, 1, 0:nt], rt1[:, 0, 0:nt]))
                link(TT(r16(10), r16(10), rt1[:, 1, 0:nt].unsqueeze(2).broadcast_to([P, nt, NE]), ALU.mult))
                b = take(("cnt", l))
                link(nc.vector.tensor_copy(r(11), b[:, 0:w16]))
                nc.vector.tensor_reduce(most[:, :], b[:, 64:80], AX.X, ALU.max).then_inc(dve_took, 1)
                dve.wait_ge(dve_took, took[0])
                m_over = NE * OVER_BLOCKS[l]
                link(nc.vector.scalar_tensor_tensor(out=r(12), in0=r(11), scalar=float(NE),
                                                    in1=const[:, C_EXP:C_EXP + w16], op0=ALU.mult, op1=ALU.add))
                if OVER_BLOCKS[l] > 1:
                    link(nc.vector.tensor_scalar(r(13), r(11), float(-P), 0.0, ALU.add, ALU.max))
                    link(nc.vector.scalar_tensor_tensor(out=r(12), in0=r(13), scalar=float(m_over - NE), in1=r(12),
                                                        op0=ALU.mult, op1=ALU.add))
                for blk in range(2, OVER_BLOCKS[l] + 1):
                    link(nc.vector.tensor_scalar(r(13), r(11), float(blk * P), float(NE - P * m_over), ALU.is_ge,
                                                 ALU.mult))
                    link(TT(r(12), r(12), r(13), ALU.add))
                link(nc.vector.scalar_tensor_tensor(out=r(12), in0=r(12), scalar=1.0, in1=r(9), op0=ALU.add,
                                                    op1=ALU.mult))
                link(nc.vector.tensor_reduce(rt1[:, 2, 0:nt], r16(12), AX.X, ALU.max))
                link(nc.vector.tensor_reduce(rt1[:, 3, 0:nt], r16(12), AX.X, ALU.add))
                link(TT(rt1[:, 3, 0:nt], rt1[:, 3, 0:nt], rt1[:, 2, 0:nt], ALU.subtract))
                link(TT(r16(13), r16(12), rt1[:, 2, 0:nt].unsqueeze(2).broadcast_to([P, nt, NE]), ALU.is_equal))
                link(TT(r(14), r(9), r(13), ALU.subtract))
                link(TT(r(13), r(13), r(10), ALU.mult))
                link(TT(r(14), r(14), r(10), ALU.mult))
                link(nc.vector.tensor_reduce(w_tok[:, 0, 0:nt], r16(13), AX.X, ALU.add))
                link(nc.vector.tensor_reduce(w_tok[:, 1, 0:nt], r16(14), AX.X, ALU.add))
                far = float(1 << 20)
                for i2 in range(2):
                    link(nc.vector.tensor_scalar(rt1[:, 4, 0:nt], rt1[:, 2 + i2, 0:nt], P * NE + 0.5, far, ALU.is_lt,
                                                 ALU.mult))
                    link(nc.vector.scalar_tensor_tensor(out=idx_beyond[:, i2, 0:nt], in0=rt1[:, 2 + i2, 0:nt],
                                                        scalar=float(-P * NE - 1), in1=rt1[:, 4, 0:nt], op0=ALU.add,
                                                        op1=ALU.add))
                for i2 in range(2):
                    nc.vector.tensor_scalar(idx_tok[:, i2, 0:nt], rt1[:, 2 + i2, 0:nt], -1.0, None, ALU.add)\
                        .then_inc(idx_ready, 1)

                Wb = l * PER_LAYER

                def low(e, p):
                    pos = position(e, p)
                    dve.wait_ge(hi_done, ready_at(e, p) + Wb)
                    TT(w_lo[:, pos % N_SPLIT, :], raw(pos % N_RAW), w_hi[:, pos % N_SPLIT, :].bitcast(F32),
                       ALU.subtract).then_inc(lo_done, 1)

                def low_next(e, p):
                    if isinstance(e, int) and e == NE - 1:
                        low(NE, 8 + p)
                    else:
                        low(e + 1, p)

                def take_ys(e, par):
                    dve.wait_ge(w_used, ready_at(e + 1, 11) + Wb)
                    if not (isinstance(e, int) and e < 2):
                        dve.wait_ge(ys_stored[par], (e - par) * 8 + 8 * Lb)
                    for n in range(2):
                        nc.vector.tensor_copy(ys[:, par, n * CH:(n + 1) * CH], bank[n][:, :]).then_inc(ys_took, 1)

                def hidden(e):
                    dve.wait_ge(silu_done, e * 2 + (2 * Lb + 2))
                    dve.wait_ge(w_used, ready_at(e, 7) + Wb)
                    if not (isinstance(e, int) and e + Lb == 0):
                        dve.wait_ge(ht_mm, e * 2 + 2 * Lb)
                    for n in range(2):
                        TT(hexp[:, n, :], bank[3 + 2 * n][:, :], silu[:, n, :], ALU.mult).then_inc(h_done, 1)

                def low_of(bk, hi, lo, half, par, made, out_sem, v):
                    dve.wait_ge(made, v)
                    part = slice(4 * half, 4 * half + 4)
                    TT(lo[:, par, part, :], bk[:, :].rearrange("p (k n) -> p k n", k=4),
                       hi[:, par, part, :].bitcast(F32), ALU.subtract).then_inc(out_sem, 1)

                def low_xs(e, par):
                    for half in range(2):
                        low_of(bank[2 + half], xsT_hi, xsT_lo, half, par, xt_hi, xt_lo, e * 2 + (2 * Lb + half + 1))

                def expert(e, par):
                    for p in range(turns(e)):
                        if p + 2 < turns(e):
                            low(e, p + 2)
                        else:
                            low_next(e, p + 2 - turns(e))
                        if p == 1 and not (isinstance(e, int) and e < 2):
                            take_ys(e - 2, par)
                        if p == min(8, turns(e) - 1):
                            hidden(e)
                        if p == min(9, turns(e) - 1):
                            for half in range(2):
                                low_of(bank[6 + half], hexpT_hi, hexpT_lo, half, par, ht_hi, ht_lo,
                                       e * 2 + (2 * Lb + half + 1))
                            if not (isinstance(e, int) and e == NE - 1):
                                low_xs(e + 1, 1 - par)

                low_xs(0, 0)
                low(0, 0)
                low(0, 1)
                for e in range(4):
                    expert(e, e % 2)
                with dve.Fori(2, NE // 2 - 1) as i:
                    expert(i * 2, 0)
                    expert(i * 2 + 1, 1)
                expert(NE - 2, 0)
                expert(NE - 1, 1)
                take_ys(NE - 2, 0)
                low(NE, 10)
                low(NE, 11)
                take_ys(NE - 1, 1)
                o = over[l]
                dve.wait_ge(idx_ready, 2 * l + 2)
                busiest = dve.value_load(most[0:1, 0:1], min_val=0, max_val=512)
                with dve.If(busiest > P):
                    dve.wait_ge(ys_stored[0], 8 * (Lb + NE))
                    with dve.Fori(0, OVER_BLOCKS[l] * NE) as k:
                        dve.wait_ge(o["s"], k + 1)
                        for n in range(2):
                            t = TT(hexp[:, n, :], bank[3 + 2 * n][:, :], silu[:, n, :], ALU.mult)
                        t.then_inc(o["h"], 1)
                        dve.wait_ge(o["d"], k + 1)
                        for n in range(2):
                            t = nc.vector.tensor_copy(ys[:, 0, n * CH:(n + 1) * CH], bank[n][:, :])
                        t.then_inc(o["ys"], 1)
                if l + 1 < DEPTH:
                    for _ in split_low(("in", l + 1, "v")):
                        pass
                dve.wait_ge(g_loaded, 16 * (2 * l + 2))
                dve.wait_ge(got_ready, l + 1)
                for k, tb in enumerate(T):
                    dve.wait_ge(got_loaded[k], 32 * (l + 1))
                    dve.wait_ge(scaled, T_BEFORE[l] + k + 1)
                    ga, gb = got_a[:, k, :], got_b[:, k, :]
                    link(nc.vector.scalar_tensor_tensor(out=gb, in0=gb, scalar=w_tok[:, 1, k:k + 1], in1=ga,
                                                        op0=ALU.mult, op1=ALU.add))
                    link(TT(gb, gb, G_bc[:, tb // 2, :], ALU.mult))
                    TT(x[:, tb, :], x[:, tb, :], gb, ALU.add).then_inc(combined, 1)
                    dve.wait_ge(combined, T_BEFORE[l] + k + 1)
            inverse_rms(4, [0, 1])
            dve.wait_ge(final_loaded, 16)
            for tb in range(2):
                nc.vector.scalar_tensor_tensor(out=final_rows[:, tb, :], in0=x[:, tb, :], scalar=stat[:, 3, tb:tb + 1],
                                               in1=final_w, op0=ALU.mult, op1=ALU.mult).then_inc(final_ready, 1)

        @block.tensor
        def _(pe):
            at = [0]

            def begin(*name):
                i = at[0]
                assert order[i] == name, (order[i], name)
                if i >= 8:
                    old = order[i - 8]
                    pe.wait_ge(act_took if taker[old] == "act" else dve_took, TAKEN[old])
                at[0] += 1
                return bank[i % 8]

            def mm(o, a, b, first, last):
                return nc.tensor.matmul(o, a, b, start=first, stop=last)

            def turn(dst, src, n):
                for j in range(n):
                    ins = nc.tensor.transpose(dst[:, j * P:(j + 1) * P], src[:, j * P:(j + 1) * P], ident)
                return ins

            pe.wait_ge(c_low, 1)

            def modulation(l, c):
                key = ("mod", l, c)
                b = begin(*key)
                for q in range(4):
                    pe.wait_ge(split_lo, 4 * SPLIT_NO[key] + q + 1)
                    at, _ = quarter(key, q)
                    for k in range(2):
                        kk = 2 * q + k
                        wh = m_hi[:, q, k * CH:(k + 1) * CH]
                        mm(b[0:2, :], c_hi[:, kk, :], wh, kk == 0, False)
                        mm(b[0:2, :], c_hi[:, kk, :], m_lo[:, at.start + k * CH:at.start + (k + 1) * CH], False, False)
                        ins = mm(b[0:2, :], c_lo[:, kk, :], wh, False, kk == KB - 1)
                    if q < 3:
                        ins.then_inc(split_used, 1)
                    else:
                        ins.then_inc(mm_done, 1)

            def taps(l, o):
                pe.wait_ge(sin_out, 2 * l + 2)
                for d in range(2):
                    for tt in range(2):
                        b = begin("f3", l, o, d, tt)
                        mm(b[:, :], hid[0:64, 3, tt * P:(tt + 1) * P],
                           w3[:, (2 * o + d) * HY:(2 * o + d + 1) * HY], True, True).then_inc(mm_done, 1)

            def tap_norm(l, o):
                pe.wait_ge(abs_ready, 8 * l + 4 * o + 4)
                b = begin("fn", l, o)
                for i in range(4):
                    ins = mm(b[:, :], ones, filt_abs[:, i // 2, i % 2, :], i == 0, i == 3)
                ins.then_inc(mm_done, 1)

            def tap_spectra(l, o):
                pe.wait_ge(pm_ready, 2 * l + o + 1)
                for k, (blk, sign) in enumerate(((FR0, 0), (FR1, 0), (FIZ, 1), (FI1, 1), (FRN, 0))):
                    b = begin("fk", l, o, k)
                    for tt in range(2):
                        ins = mm(b[:, :], dft[:, tt, blk, :], filt_pm[:, sign, tt, :], tt == 0, tt == 1)
                    ins.then_inc(mm_done, 1)

            def filter_step(l, g):
                if g == 0:
                    pe.wait_ge(filt_loaded, 16 * (7 + 5 * l))
                    b = begin("fl", l, 1)
                    mm(b[0:64, 0:SEQ], w1, feats, True, True).then_inc(mm_done, 1)
                elif g == 1:
                    pe.wait_ge(sin_out, 2 * l + 1)
                    b = begin("fl", l, 2)
                    mm(b[0:64, 0:SEQ], w2, hid[0:64, 2, :], True, True).then_inc(mm_done, 1)
                elif g == 2:
                    taps(l, 0)
                elif g in (3, 5):
                    if l == 0 and g == 3:
                        pe.wait_ge(const_loaded, 16)
                    tap_norm(l, g // 4)
                elif g == 4:
                    tap_spectra(l, 0)
                    taps(l, 1)
                else:
                    tap_spectra(l, 1)

            for kind, l, i in OPENING:
                modulation(l, i) if kind == "mod" else filter_step(l, i)
            pe.wait_ge(small_loaded, N_SMALL)

            for l in range(DEPTH):
                T = tokens_of(l)
                nt = len(T)
                Lb = NE * l

                def turn_rows(p, tbs):
                    for k, tb in enumerate(tbs):
                        pe.wait_ge(rows_ready, ROWS_AT[l, p] + k + 1)
                        for half in range(2):
                            b = begin("hT", l, p, tb, half)
                            turn(b, hrow[:, k % 2, half * 512:(half + 1) * 512], 4).then_inc(mm_done, 1)

                def part_products(b, lo, tb, key, q, last):
                    cols, n = quarter(key, q)
                    c = n // 2
                    for k in range(2):
                        kk = 2 * q + k
                        th, tl = hT_hi[:, kk, tb * P:(tb + 1) * P], lo[:, tb, kk, :]
                        wh = m_hi[:, q, k * c:(k + 1) * c]
                        wl = m_lo[:, cols.start + k * c:cols.start + (k + 1) * c]
                        mm(b[:, 0:c], th, wh, kk == 0, False)
                        mm(b[:, 0:c], th, wl, False, False)
                        ins = mm(b[:, 0:c], tl, wh, False, kk == KB - 1)
                    if q == 3:
                        ins.then_inc(mm_done, 1)
                    elif last:
                        ins.then_inc(split_used, 1)

                def project(key, names, tbs, lo=hT_lo, ready=None):
                    n0 = 4 * SPLIT_NO[key]
                    if ready is None:
                        banks = [begin(*n) for n in names]
                        for q in range(4):
                            pe.wait_ge(split_lo, n0 + q + 1)
                            for b, tb in zip(banks, tbs):
                                part_products(b, lo, tb, key, q, tb == tbs[-1])
                        return
                    for name, tb in zip(names, tbs):
                        pe.wait_ge(dve_took, TAKEN[ready(tb)])
                        b = begin(*name)
                        for q in range(4):
                            pe.wait_ge(split_lo, n0 + q + 1)
                            part_products(b, lo, tb, key, q, tb == tbs[-1])

                turn_rows(0, range(4))
                for c in ("v", "x1", "x2", "q", "kv", "f"):
                    tbs = range(4) if c == "kv" else T
                    if c == "x1":
                        pe.wait_ge(dve_took, TAKEN[("hT", l, 0, 3, 1)])
                    project(("in", l, c), [("in", l, c, tb) for tb in tbs], tbs,
                            ready=(lambda tb: ("hT", l, 0, tb, 1)) if c == "v" else None)
                for tb in range(4):
                    pe.wait_ge(dve_took, TAKEN[("in", l, "kv", tb)])
                    b = begin("kT", l, tb)
                    turn(b, krow[:, tb, :], 1).then_inc(mm_done, 1)
                for tb in T:
                    pe.wait_ge(dve_took, TAKEN[("in", l, "q", tb)])
                    b = begin("qT", l, tb)
                    turn(b, qrow[:, tb, :], 4).then_inc(mm_done, 1)
                pe.wait_ge(four_loaded, 16 * (l + 1))
                pe.wait_ge(act_took, TAKEN[("in", l, "f", T[-1])])
                for s in range(nt // 2):
                    for g in range(5):
                        if g < 4:
                            b = begin("fp", l, s, g)
                            for tt in range(2):
                                ins = mm(b[:, :], frow[:, 2 * s + tt, g * P:(g + 1) * P],
                                         four[:, tt * 512:(tt + 1) * 512], tt == 0, tt == 1)
                            ins.then_inc(mm_done, 1)
                        if g > 0:
                            pe.wait_ge(act_took, TAKEN[("fp", l, s, g - 1)])
                            b = begin("fy", l, s, g - 1)
                            for j in range(2):
                                ins = mm(b[:, 0:SEQ], four[:, 1024 + j * P:1024 + (j + 1) * P],
                                         pq[:, (g - 1) % 2, j * SEQ:(j + 1) * SEQ], j == 0, j == 1)
                            ins.then_inc(mm_done, 1)
                heads = [(tb, h) for tb in T for h in range(NH)]
                hb = NH * T_BEFORE[l]
                pe.wait_ge(act_took, TAKEN[("qT", l, T[-1])])

                def turn_ya(k):
                    pe.wait_ge(ya_ready, T_BEFORE[l] + k + 1)
                    b = begin("yaT", l, T[k])
                    turn(b, ya[:, k % 2, :], 4).then_inc(mm_done, 1)

                for i in range(len(heads) + 3):
                    if i < len(heads):
                        tb, h = heads[i]
                        g, j = h // 4, h % 4
                        keys = slice(0, 512) if tb < 2 else slice(256, 512)
                        b = begin("sc", l, tb, h)
                        mm(b[:, 0:keys.stop - keys.start], qT[g * HD:(g + 1) * HD, j, tb * P:(tb + 1) * P],
                           kT[g * HD:(g + 1) * HD, keys], True, True).then_inc(mm_done, 1)
                    if 2 <= i < len(heads) + 2:
                        tb, h = heads[i - 2]
                        pe.wait_ge(exp_done, hb + i - 1)
                        b = begin("pt", l, tb, h)
                        turn(b, P_buf[:, i % 2, :], 4 if tb < 2 else 2).then_inc(mm_done, 1)
                    if i >= 3:
                        tb, h = heads[i - 3]
                        g = h // 4
                        kb = range(4) if tb < 2 else range(2, 4)
                        pe.wait_ge(act_took, TAKEN[("pt", l, tb, h)])
                        b = begin("pv", l, tb, h)
                        for n, k in enumerate(kb):
                            ins = mm(b[:, 0:HD], PT[:, (i - 3) % 2, n, :], vrow[:, k, g * HD:(g + 1) * HD], n == 0,
                                     n == len(kb) - 1)
                        ins.then_inc(mm_done, 1)
                        if h == NH - 1 and tb > 0:
                            turn_ya((i - 3) // NH - 1)
                turn_ya(nt - 1)
                pe.wait_ge(conv_done, 3 * (T_BEFORE[l] + nt))
                for o in range(2):
                    for s in range(nt // 2):
                        if o:
                            pe.wait_ge(y_ready, 2 * T_BEFORE[l] + 2 * (s + 1))
                        for blk in (FR0, FI0, FR1, FI1):
                            b = begin("u", l, o, s, blk)
                            for tt in range(2):
                                ins = mm(b[:, :], dft[:, tt, blk, :], z[:, 2 * s + tt, 0, :], tt == 0, tt == 1)
                            ins.then_inc(mm_done, 1)
                    for s in range(nt // 2):
                        pe.wait_ge(spec_ready, 2 * T_BEFORE[l] + 2 * (o * (nt // 2) + s + 1))
                        for tt in range(2):
                            b = begin("c", l, o, s, tt)
                            for k in range(4):
                                ins = mm(b[:, :], inv[:, k, tt * P:(tt + 1) * P], Yspec[:, s, k, :], k == 0, k == 3)
                            ins.then_inc(mm_done, 1)
                for k, tb in enumerate(T):
                    pe.wait_ge(y_ready, 2 * T_BEFORE[l] + nt + k + 1)
                    b = begin("yhT", l, tb)
                    turn(b, z[:, tb, 0, :], 4).then_inc(mm_done, 1)
                pe.wait_ge(act_took, TAKEN[("yhT", l, T[-1])])
                for br in range(3):
                    for n in range(2):
                        project(("g", l, br, n), [("g", l, br, n, tb) for tb in T], T)
                    pe.wait_ge(branch_low, 3 * l + br + 1)
                    for n in range(2):
                        banks = [begin("b", l, br, n, tb) for tb in T]
                        for q in range(4):
                            pe.wait_ge(split_lo, 4 * SPLIT_NO[("b", l, br)] + q + 1)
                            cols, _ = quarter(("b", l, br), q)
                            wh = m_hi[:, q, n * CH:(n + 1) * CH]
                            wl = m_lo[:, cols.start + n * CH:cols.start + (n + 1) * CH]
                            for b, tb in zip(banks, T):
                                th, tl = (t[:, q, tb * P:(tb + 1) * P] for t in (branch_hi, branch_lo[br]))
                                mm(b[:, :], th, wh, q == 0, False)
                                mm(b[:, :], th, wl, False, False)
                                ins = mm(b[:, :], tl, wh, False, q == 3)
                                if q == 3:
                                    ins.then_inc(mm_done, 1)
                            if q < 3 and n == 1:
                                ins.then_inc(split_used, 1)
                for k, tb in enumerate(T):
                    pe.wait_ge(merged_ready, 2 * T_BEFORE[l] + nt + k + 1)
                    for half in range(2):
                        b = begin("mT", l, tb, half)
                        turn(b, merged[:, tb, half * 512:(half + 1) * 512], 4).then_inc(mm_done, 1)
                for n in range(2):
                    project(("o", l, n), [("o", l, n, tb) for tb in T], T, lo=mT_lo,
                            ready=(lambda tb: ("mT", l, tb, 1)) if n == 0 else None)
                turn_rows(1, T)
                for tb in T:
                    pe.wait_ge(act_took, TAKEN[("hT", l, 1, tb, 1)])
                    b = begin("r", l, tb)
                    for k in range(KB):
                        ins = mm(b[:, 0:NE], hT[:, k, tb * P:(tb + 1) * P], wr[:, k, :], k == 0, k == KB - 1)
                    ins.then_inc(mm_done, 1)
                pe.wait_ge(sel_ready, l + 1)
                b = begin("cnt", l)
                sel = rt[:, 9, :].rearrange("p (t e) -> p t e", e=NE)
                for k in range(nt):
                    for k2 in range(k + 1):
                        mm(b[:, k * NE:(k + 1) * NE], tri if k2 == k else ones, sel[:, k2, :], k2 == 0, k2 == k)
                for k in range(nt):
                    ins = mm(b[:, 64:64 + NE], ones, sel[:, k, :], k == 0, k == nt - 1)
                ins.then_inc(mm_done, 1)

                pe.wait_ge(act_took, TAKEN[("r", l, T[-1])])
                pe.wait_ge(dve_took, TAKEN[("cnt", l)])
                Wb = l * PER_LAYER

                def turn_xs(e, par):
                    if isinstance(e, int):
                        pe.wait_ge(xs_loaded[par], 8 * Lb + 16 * (e // 2 + 1))
                    else:
                        pe.wait_ge(xs_loaded[par], (e - par) * 8 + (8 * Lb + 16))
                    if not (isinstance(e, int) and e == 0):
                        pe.wait_ge(h_done, e * 2 + 2 * Lb)
                    for half in range(2):
                        turn_rows_of(bank[2 + half], xs[:, par, half * 512:(half + 1) * 512]).then_inc(xt_mm, 1)

                def turn_rows_of(dst, src):
                    s4 = src.rearrange("p (q i k) -> p q k i", q=2, k=2)
                    for j in range(4):
                        ins = nc.tensor.transpose(dst[:, j * P:(j + 1) * P], s4[:, j // 2, j % 2, :], ident)
                    return ins

                def product(bk, hi, lo, e, p, par):
                    pe.wait_ge(lo_done, ready_at(e, p) + Wb)
                    i = position(e, p) % N_SPLIT
                    for k in range(2):
                        kk = 2 * (p % 4) + k
                        first = p % 4 == 0 and k == 0
                        for n in range(2):
                            cols = slice(k * D + n * CH, k * D + (n + 1) * CH)
                            mm(bk[n][:, :], hi[:, par, kk, :], w_hi[:, i, cols], first, False)
                            mm(bk[n][:, :], hi[:, par, kk, :], w_lo[:, i, cols], False, False)
                        for n in range(2):
                            cols = slice(k * D + n * CH, k * D + (n + 1) * CH)
                            ins = mm(bk[n][:, :], lo[:, par, kk, :], w_hi[:, i, cols], False, p % 4 == 3 and k == 1)
                    ins.then_inc(w_used, 1)

                def gate_up(e, par):
                    pe.wait_ge(xt_lo, e * 2 + (2 * Lb + 2))
                    for p in range(8):
                        up = p // 4
                        product((bank[2 + up], bank[4 + up]), xsT_hi, xsT_lo, e, p, par)

                def down(e, par, part):
                    pe.wait_ge(ht_lo, e * 2 + (2 * Lb + 2))
                    if not (isinstance(e, int) and e + Lb == 0):
                        pe.wait_ge(ys_took, e * 2 + 2 * Lb)
                    for p in (8 + 2 * part, 9 + 2 * part):
                        product((bank[0], bank[1]), hexpT_hi, hexpT_lo, e + 1, p, par)

                def turn_h(e):
                    for half in range(2):
                        pe.wait_ge(h_done, e * 2 + (2 * Lb + half + 1))
                        if not (isinstance(e, int) and e == 0):
                            pe.wait_ge(ht_lo, e * 2 + (2 * Lb - 2 + half + 1))
                        turn_rows_of(bank[6 + half], hexp[:, half, :]).then_inc(ht_mm, 1)

                turn_xs(0, 0)
                gate_up(0, 0)
                turn_h(0)
                turn_xs(1, 1)

                def expert(e, par, last=False):
                    gate_up(e, par)
                    down(e - 1, 1 - par, 0)
                    turn_h(e)
                    if not last:
                        turn_xs(e + 1, 1 - par)
                    down(e - 1, 1 - par, 1)

                expert(1, 1)
                with pe.Fori(0, NE // 2 - 2) as i:
                    expert(i * 2 + 2, 0)
                    expert(i * 2 + 3, 1)
                expert(NE - 2, 0)
                expert(NE - 1, 1, last=True)
                down(NE - 1, 1, 0)
                down(NE - 1, 1, 1)
                pe.wait_ge(ys_took, 2 * (Lb + NE))
                o = over[l]
                pe.wait_ge(idx_ready, 2 * l + 2)
                busiest = pe.value_load(most[0:1, 0:1], min_val=0, max_val=512)
                with pe.If(busiest > P):
                    with pe.Fori(0, OVER_BLOCKS[l] * NE) as k:
                        pe.wait_ge(o["xs"], k * 16 + 16)
                        for half in range(2):
                            t = turn(bank[2 + half], xs[:, 0, half * 512:(half + 1) * 512], 4)
                        t.then_inc(o["xt"], 1)
                        pe.wait_ge(o["xe"], k + 1)
                        pe.wait_ge(o["w"], k * 96 + 96)
                        for c in range(4):
                            for kk in range(KB):
                                t = mm(bank[2 + c][:, :], over_xT[:, kk, :], slot(c)[:, kk, :], kk == 0, kk == KB - 1)
                        t.then_inc(o["gu"], 1)
                        pe.wait_ge(o["h"], k + 1)
                        for half in range(2):
                            t = turn(bank[6 + half], hexp[:, half, :], 4)
                        t.then_inc(o["ht"], 1)
                        pe.wait_ge(o["he"], k + 1)
                        for n in range(2):
                            for kk in range(KB):
                                t = mm(bank[n][:, :], over_hT[:, kk, :], slot(4 + n)[:, kk, :], kk == 0, kk == KB - 1)
                        t.then_inc(o["d"], 1)
                    pe.wait_ge(o["ys"], OVER_BLOCKS[l] * NE)


_INS = ['x', 'c', 'ctx', 'c_ctx', 'w_mod', 'b_mod', 'norm_mix', 'norm_ffn', 'w_in', 'attn_sink', 'conv_w', 'conv_b',
        'filt_w1', 'filt_b1', 'filt_freq', 'filt_w2', 'filt_b2', 'filt_w3', 'hyena_bias', 'w_branch_attn',
        'w_branch_fnet', 'w_branch_hyena', 'w_out', 'w_router', 'b_router', 'w_exp_gate', 'w_exp_up', 'w_exp_down',
        'norm_final']


def _constants():
    import math
    import numpy as np

    f32 = np.float32
    p = np.arange(128)
    const = np.zeros((128, C_END), f32)
    const[:, C_ID:C_ID + 128] = np.eye(128)
    const[:, C_TRI:C_TRI + 128] = p[:, None] < p[None, :]
    const[:, C_ONE:C_ONE + 128] = 1.0
    t = np.arange(256)
    f = np.arange(256)
    ang = 2 * np.pi * (np.outer(t, f) % 512) / 512
    cos, msin, alt = np.cos(ang), -np.sin(ang), (-1.0) ** t
    dft = np.zeros((256, 6, 128))
    dft[:, 0], dft[:, 1] = cos[:, :128], cos[:, 128:]
    dft[:, 2], dft[:, 3] = msin[:, :128], msin[:, 128:]
    dft[:, 4] = dft[:, 2]
    dft[:, 4, 0] = 0.0
    dft[:, 2, 0] = alt
    dft[:, 5] = dft[:, 0]
    dft[:, 5, 0] = alt
    const[:, C_DFT:C_INV] = dft.reshape(2, 128, 6 * 128).transpose(1, 0, 2).reshape(128, -1)
    inv = np.zeros((4, 128, 256))
    ci, si = 2 * cos.T / 512, 2 * msin.T / 512
    ci[0] /= 2
    si[0] = alt / 512
    inv[0], inv[1], inv[2], inv[3] = ci[:128], ci[128:], si[:128], si[128:]
    const[:, C_INV:C_ROPE] = inv.transpose(1, 0, 2).reshape(128, -1)
    freqs = (f32(10000.0) ** (-np.arange(16, dtype=f32) / f32(16))).astype(f32)
    rope = np.zeros((256, 4, 64))
    for half, pos in ((0, t // 64), (1, t % 64)):
        a = (pos.astype(f32)[:, None] * freqs).astype(f32).astype(np.float64)
        c = slice(32 * half, 32 * half + 32)
        rope[:, 2, c] = np.concatenate([np.cos(a), np.cos(a)], 1)
        rope[:, 3, c] = np.concatenate([-np.sin(a), np.sin(a)], 1)
    rope[:, 0:2] = rope[:, 2:4].astype(f32) * 0.125
    const[:, C_ROPE:C_MASK] = rope.reshape(2, 128, 256).transpose(1, 0, 2).reshape(128, -1)
    mask = np.zeros((256, 512))
    mask[:, :256] = np.where(np.abs(t[:, None] - t[None, :]) <= 128, 0.0, -1.0e30)
    const[:, C_MASK:C_EXP] = mask.reshape(2, 128, 512).transpose(1, 0, 2).reshape(128, -1)
    const[:, C_EXP:C_END] = np.tile(np.arange(16), 4)[None]
    an = 2 * np.pi * (np.outer(t, t) % 256) / 256
    ad = 2 * np.pi * (np.outer(p, p) % 128) / 128
    scale = 1.0 / math.sqrt(256 * 128)
    four = np.zeros((128, 1280))
    cs = np.concatenate([np.cos(an), np.sin(an)], 1)
    four[:, 0:512], four[:, 512:1024] = cs[:128], cs[128:]
    four[:, 1024:1152], four[:, 1152:1280] = np.cos(ad) * scale, -np.sin(ad) * scale
    pos = np.arange(256, dtype=f32)
    tt = pos / f32(255)
    omega = (f32(2.0 * math.pi) * pos / f32(256)).astype(f32)
    bands = np.linspace(1e-4, 15, 16, dtype=f32)
    arg = (omega[:, None] * bands).astype(f32)
    feats = np.concatenate([tt[:, None], np.cos(arg), -np.sin(arg)], -1).T
    deltas = np.abs(np.linspace(math.log(1e-2) / 1.5, math.log(1e-2) / 0.3, 512, dtype=f32))
    dec = np.exp(-tt[:, None] * deltas)
    decay = np.zeros((128, 3, 512), f32)
    decay[:, 0], decay[:, 1], decay[:, 2] = dec[:128], dec[128:], dec[:128]
    decay[0, 2] = 0.0
    tok = (np.arange(4)[None, :] * 128 + p[:, None]).astype(np.int32)
    return {"k_const": const, "k_four": four.astype(f32), "k_feats": np.ascontiguousarray(feats, f32),
            "k_decay": decay.reshape(128, -1), "k_tok": tok}


def kernel(**inputs):
    import numpy as _np
    import concourse.bacc as _bacc
    from concourse import mybir as _mybir
    from concourse.bass_utils import run_bass_kernel_spmd as _run

    nc = _bacc.Bacc("TRN2", target_bir_lowering=False, num_devices=1)
    arrays, aps = {}, {}
    for name in _INS:
        a = _np.ascontiguousarray(inputs[name])
        arrays[f"in_{name}_dram"] = a
        aps[name] = nc.dram_tensor(f"in_{name}_dram", a.shape, _mybir.dt.from_np(a.dtype), kind="ExternalInput").ap()
    for name, a in _constants().items():
        arrays[f"in_{name}_dram"] = a
        aps[name] = nc.dram_tensor(f"in_{name}_dram", a.shape, _mybir.dt.from_np(a.dtype), kind="ExternalInput").ap()
    out = nc.dram_tensor("out_0_dram", (1, SEQ, D), _mybir.dt.float32, kind="ExternalOutput").ap()
    hybrid_kernel(nc, aps, out)
    r = _run(nc, [arrays], core_ids=[0])
    return r.results[0]["out_0_dram"]
```
